# Optimizing a Trainium2 kernel written in Bass

```python
import jax, jax.numpy as jnp
from jax import lax
import numpy as np
import math
import jax
import jax.numpy as jnp

D_MODEL = 1024
BATCH = 1
SEQ = 256
DEPTH = 1

GRID_W = 64
CTX_LEN = 256
D_MIX = D_MODEL
RET_DIM = 64
RET_WIDTH = D_MIX // 2
RET_HEADS = RET_WIDTH // RET_DIM
RWKV_DIM = 64
RWKV_WIDTH = D_MIX - RET_WIDTH
RWKV_HEADS = RWKV_WIDTH // RWKV_DIM
DECAY_LORA = 64
ICLR_LORA = 64
GATE_LORA = 128
CHUNK = 128
CONV_W = 3
N_EXPERTS = 16
EC_CAPACITY = 2
D_EXPERT = D_MODEL
ROPE_BASE = 10000.0
NORM_EPS = 1e-6
RWKV_GN_EPS = 64e-5
RET_COLS = 5 * RET_WIDTH
RWKV_SPLITS = (RWKV_WIDTH, RWKV_WIDTH, RWKV_WIDTH, DECAY_LORA, DECAY_LORA, ICLR_LORA, GATE_LORA, GATE_LORA)
RWKV_COLS = sum(RWKV_SPLITS)
D_IN = RET_COLS + RWKV_COLS


def split_cols(u, sizes):
    outs, start = [], 0
    for s in sizes:
        outs.append(u[..., start:start + s])
        start += s
    return outs

def flip(t):
    return jnp.flip(t, axis=1)

def rms_norm(x, g):
    xf = x.astype(jnp.float32)
    y = xf * lax.rsqrt(jnp.mean(xf * xf, axis=-1, keepdims=True) + NORM_EPS)
    return (y * g.astype(jnp.float32)).astype(x.dtype)

def head_rms(y):
    y = y * lax.rsqrt(jnp.mean(y * y, axis=-1, keepdims=True) + NORM_EPS)
    return y.reshape(y.shape[0], y.shape[1], -1)

def depthwise_conv(x, w):
    return lax.conv_general_dilated(x, w[:, None, :].astype(x.dtype), window_strides=(1,), padding='SAME',
                                    dimension_numbers=('NWC', 'WIO', 'NWC'), feature_group_count=x.shape[-1])

def axial_rope(x):
    n_tok, d = x.shape[1], x.shape[-1]
    rows = n_tok // GRID_W
    row = jnp.repeat(jnp.arange(rows, dtype=jnp.float32), GRID_W)
    col = jnp.tile(jnp.arange(GRID_W, dtype=jnp.float32), rows)
    n_freq = d // 4
    freq = ROPE_BASE ** (-jnp.arange(n_freq, dtype=jnp.float32) / n_freq)
    ang = jnp.concatenate([row[:, None] * freq, col[:, None] * freq], axis=-1)[None, :, None, :]
    cos, sin = jnp.cos(ang), jnp.sin(ang)
    x1, x2 = x[..., : d // 2], x[..., d // 2:]
    return jnp.concatenate([x1 * cos - x2 * sin, x2 * cos + x1 * sin], axis=-1)

def retention_scan(q, k, v, log_gamma, s0):
    B, T, H, d = q.shape
    n = T // CHUNK
    to_chunks = lambda t: t.reshape(B, n, CHUNK, H, d).transpose(1, 0, 3, 2, 4)
    idx = jnp.arange(CHUNK, dtype=jnp.float32)
    rel = idx[:, None] - idx[None, :]
    decay_in = jnp.where(rel >= 0, jnp.exp(jnp.maximum(rel, 0.0) * log_gamma[:, None, None]), 0.0)
    q_dec = jnp.exp((idx + 1.0) * log_gamma[:, None])[..., None]
    k_dec = jnp.exp((CHUNK - 1.0 - idx) * log_gamma[:, None])[..., None]
    chunk_dec = jnp.exp(CHUNK * log_gamma)[:, None, None]

    def step(S, inp):
        qc, kc, vc = inp
        scores = jnp.einsum('bhid,bhjd->bhij', qc, kc) * decay_in
        out = jnp.einsum('bhij,bhjd->bhid', scores, vc) + jnp.einsum('bhid,bhde->bhie', qc * q_dec, S)
        S = S * chunk_dec + jnp.einsum('bhjd,bhje->bhde', kc * k_dec, vc)
        return S, out

    S_fin, ys = lax.scan(step, s0, (to_chunks(q), to_chunks(k), to_chunks(v)))
    return ys.transpose(1, 0, 3, 2, 4).reshape(B, T, H, d), S_fin

def retention_group(u, uc, need_ctx):
    def split_heads(t):
        q, k, v, gf, gb = split_cols(t.astype(jnp.float32), (RET_WIDTH,) * 5)
        hd = lambda a: a.reshape(a.shape[0], a.shape[1], RET_HEADS, RET_DIM)
        return hd(q), hd(k) * RET_DIM ** -0.5, hd(v), gf, gb

    q, k, v, gf, gb = split_heads(u)
    qc, kc, vc, gfc, gbc = split_heads(uc)
    q, k = axial_rope(q), axial_rope(k)
    log_gamma = jnp.log1p(-jnp.exp2(-5.0 - jnp.arange(RET_HEADS, dtype=jnp.float32)))
    s0 = jnp.zeros((u.shape[0], RET_HEADS, RET_DIM, RET_DIM), jnp.float32)
    yc_f, sc_f = retention_scan(qc, kc, vc, log_gamma, s0)
    yc_b, sc_b = retention_scan(flip(qc), flip(kc), flip(vc), log_gamma, s0)
    y_f, _ = retention_scan(q, k, v, log_gamma, sc_f)
    y_b, _ = retention_scan(flip(q), flip(k), flip(v), log_gamma, sc_b)
    lat = jax.nn.silu(gf) * head_rms(y_f) + jax.nn.silu(gb) * head_rms(flip(y_b))
    if not need_ctx:
        return lat, None
    ctx_out = jax.nn.silu(gfc) * head_rms(yc_f) + jax.nn.silu(gbc) * head_rms(flip(yc_b))
    return lat, ctx_out

def rwkv_prepare(u, w0, w2, a0, a2, g2, k_k, k_a, r_k):
    u = u.astype(jnp.float32)
    B, T, _ = u.shape
    r, k, v, wl_f, wl_b, al, gl_f, gl_b = split_cols(u, RWKV_SPLITS)
    heads = lambda t: t.reshape(B, T, RWKV_HEADS, RWKV_DIM)

    def decay(wl, w0_d, w2_d):
        w_log = -jax.nn.softplus(-(w0_d + jnp.tanh(wl) @ w2_d)) - 0.5
        return heads(jnp.exp(-jnp.exp(w_log)))

    iclr = jax.nn.sigmoid(a0 + al @ a2)
    kk = heads(k * k_k)
    kk = kk / jnp.maximum(jnp.linalg.norm(kk, axis=-1, keepdims=True), 1e-12)
    k_mod = heads(k * (1.0 + (iclr - 1.0) * k_a))
    r, v = heads(r), heads(v)
    bonus = (jnp.sum(r * k_mod * r_k.reshape(RWKV_HEADS, RWKV_DIM), axis=-1, keepdims=True) * v).reshape(B, T, -1)
    g_f = jax.nn.sigmoid(gl_f) @ g2[0]
    g_b = jax.nn.sigmoid(gl_b) @ g2[1]
    return (r, decay(wl_f, w0[0], w2[0]), decay(wl_b, w0[1], w2[1]), k_mod, v, -kk, kk * heads(iclr), g_f, g_b, bonus)

def rwkv7_scan(r, w, k, v, a, b, s0):
    def step(S, inp):
        r_t, w_t, k_t, v_t, a_t, b_t = inp
        sa = jnp.einsum('bhvk,bhk->bhv', S, a_t)
        S = S * w_t[:, :, None, :] + sa[..., None] * b_t[:, :, None, :] + v_t[..., None] * k_t[:, :, None, :]
        return S, jnp.einsum('bhvk,bhk->bhv', S, r_t)

    xs = tuple(jnp.moveaxis(t, 1, 0) for t in (r, w, k, v, a, b))
    S_fin, ys = lax.scan(step, s0, xs)
    return jnp.moveaxis(ys, 0, 1), S_fin

def rwkv_group_norm(y, w, b):
    mu = jnp.mean(y, axis=-1, keepdims=True)
    var = jnp.mean((y - mu) ** 2, axis=-1, keepdims=True)
    yn = ((y - mu) * lax.rsqrt(var + RWKV_GN_EPS)).reshape(y.shape[0], y.shape[1], -1)
    return yn * w + b

def rwkv_group(rw, rwc, w0, w2, a0, a2, g2, k_k, k_a, r_k, lnx_w, lnx_b, need_ctx):
    r, w_f, w_b, k, v, a, b, g_f, g_b, bonus = rwkv_prepare(rw, w0, w2, a0, a2, g2, k_k, k_a, r_k)
    rc, wc_f, wc_b, kc, vc, ac, bc, gc_f, gc_b, bonus_c = rwkv_prepare(rwc, w0, w2, a0, a2, g2, k_k, k_a, r_k)
    s0 = jnp.zeros((rw.shape[0], RWKV_HEADS, RWKV_DIM, RWKV_DIM), jnp.float32)
    yc_f, sc_f = rwkv7_scan(rc, wc_f, kc, vc, ac, bc, s0)
    yc_b, sc_b = rwkv7_scan(*[flip(t) for t in (rc, wc_b, kc, vc, ac, bc)], s0)
    y_f, _ = rwkv7_scan(r, w_f, k, v, a, b, sc_f)
    y_b, _ = rwkv7_scan(*[flip(t) for t in (r, w_b, k, v, a, b)], sc_b)
    lat = g_f * (rwkv_group_norm(y_f, lnx_w, lnx_b) + bonus) + g_b * (rwkv_group_norm(flip(y_b), lnx_w, lnx_b) + bonus)
    if not need_ctx:
        return lat, None
    ctx_out = (gc_f * (rwkv_group_norm(yc_f, lnx_w, lnx_b) + bonus_c)
               + gc_b * (rwkv_group_norm(flip(yc_b), lnx_w, lnx_b) + bonus_c))
    return lat, ctx_out

def token_mix(h, hc, w_in, conv_w, w0, w2, a0, a2, g2, k_k, k_a, r_k, lnx_w, lnx_b, w_out, need_ctx):
    u, uc = h @ w_in, hc @ w_in
    ret_lat, ret_ctx = retention_group(u[..., :RET_COLS], uc[..., :RET_COLS], need_ctx)
    rw = depthwise_conv(u[..., RET_COLS:], conv_w)
    rwc = depthwise_conv(uc[..., RET_COLS:], conv_w)
    rwkv_lat, rwkv_ctx = rwkv_group(rw, rwc, w0, w2, a0, a2, g2, k_k, k_a, r_k, lnx_w, lnx_b, need_ctx)
    lat = jnp.concatenate([ret_lat, rwkv_lat], axis=-1).astype(h.dtype) @ w_out
    if not need_ctx:
        return lat, None
    ctx_out = jnp.concatenate([ret_ctx, rwkv_ctx], axis=-1).astype(hc.dtype) @ w_out
    return lat, ctx_out

def ec_moe(h, w_router, w_gate, w_up, w_down):
    B, T, D = h.shape
    cap = max(1, EC_CAPACITY * T // N_EXPERTS)
    affinity = jax.nn.softmax((h @ w_router).astype(jnp.float32), axis=-1)
    gate_vals, tok_idx = lax.top_k(jnp.swapaxes(affinity, 1, 2), cap)
    xs = jax.vmap(lambda hb, ib: hb[ib])(h, tok_idx)
    hid = jax.nn.silu(jnp.einsum('becd,edf->becf', xs, w_gate)) * jnp.einsum('becd,edf->becf', xs, w_up)
    ye = jnp.einsum('becf,efd->becd', hid, w_down) * gate_vals[..., None].astype(h.dtype)
    return jax.vmap(lambda yb, ib: jnp.zeros((T, D), yb.dtype).at[ib.reshape(-1)].add(yb.reshape(-1, D)))(ye, tok_idx)

def first_inputs(seed: int = 0) -> dict:
    key = jax.random.key(seed)
    ks = jax.random.split(key, 24)
    nrm = lambda k, shape, s: s * jax.random.normal(k, shape, jnp.float32)
    L, D, W, E, F = DEPTH, D_MODEL, RWKV_WIDTH, N_EXPERTS, D_EXPERT
    return {
        'x': nrm(ks[0], (BATCH, SEQ, D), 1.0),
        'c': nrm(ks[1], (BATCH, D), 1.0),
        'ctx': nrm(ks[2], (BATCH, CTX_LEN, D), 1.0),
        'c_ctx': nrm(ks[3], (D,), 1.0),
        'w_mod': nrm(ks[4], (L, D, 6 * D), 0.5 * D ** -0.5),
        'b_mod': nrm(ks[5], (L, 6 * D), 0.02),
        'norm_gains': 1.0 + nrm(ks[6], (L, 4, D), 0.1),
        'w_in': nrm(ks[7], (L, D, D_IN), D ** -0.5),
        'rwkv_conv': jnp.array([0.3, 1.0, 0.3], jnp.float32)[None, :, None] + nrm(ks[8], (L, CONV_W, RWKV_COLS), 0.05),
        'rwkv_w0': jnp.linspace(-6.0, -1.0, W, dtype=jnp.float32) + nrm(ks[9], (L, 2, W), 0.1),
        'rwkv_w2': nrm(ks[10], (L, 2, DECAY_LORA, W), 0.5 * DECAY_LORA ** -0.5),
        'rwkv_a0': nrm(ks[11], (L, W), 0.1),
        'rwkv_a2': nrm(ks[12], (L, ICLR_LORA, W), 0.5 * ICLR_LORA ** -0.5),
        'rwkv_g2': nrm(ks[13], (L, 2, GATE_LORA, W), GATE_LORA ** -0.5),
        'rwkv_k_k': 0.85 + nrm(ks[14], (L, W), 0.05),
        'rwkv_k_a': 1.0 + nrm(ks[15], (L, W), 0.05),
        'rwkv_r_k': nrm(ks[16], (L, W), 0.1),
        'rwkv_lnx_w': 1.0 + nrm(ks[17], (L, W), 0.1),
        'rwkv_lnx_b': nrm(ks[18], (L, W), 0.02),
        'w_out': nrm(ks[19], (L, D_MIX, D), D_MIX ** -0.5),
        'w_router': nrm(ks[20], (L, D, E), D ** -0.5),
        'w_gate': nrm(ks[21], (L, E, D, F), D ** -0.5),
        'w_up': nrm(ks[22], (L, E, D, F), D ** -0.5),
        'w_down': nrm(ks[23], (L, E, F, D), F ** -0.5),
    }

def first_block(x, c, ctx, c_ctx, w_mod, b_mod, norm_gains, w_in, rwkv_conv, rwkv_w0, rwkv_w2, rwkv_a0, rwkv_a2,
              rwkv_g2, rwkv_k_k, rwkv_k_a, rwkv_r_k, rwkv_lnx_w, rwkv_lnx_b, w_out, w_router, w_gate, w_up, w_down):
    for i in range(DEPTH):
        need_ctx = i < DEPTH - 1
        sh1, sc1, gt1, sh2, sc2, gt2 = jnp.split((jax.nn.silu(c) @ w_mod[i] + b_mod[i])[:, None, :], 6, axis=-1)
        csh1, csc1, cgt1, csh2, csc2, cgt2 = jnp.split(jax.nn.silu(c_ctx) @ w_mod[i] + b_mod[i], 6, axis=-1)
        g_pre_mix, g_post_mix, g_pre_ffn, g_post_ffn = norm_gains[i]
        h = rms_norm(x, g_pre_mix) * (1.0 + sc1) + sh1
        hc = rms_norm(ctx, g_pre_mix) * (1.0 + csc1) + csh1
        mix, mix_c = token_mix(h, hc, w_in[i], rwkv_conv[i], rwkv_w0[i], rwkv_w2[i], rwkv_a0[i], rwkv_a2[i],
                               rwkv_g2[i], rwkv_k_k[i], rwkv_k_a[i], rwkv_r_k[i], rwkv_lnx_w[i], rwkv_lnx_b[i],
                               w_out[i], need_ctx)
        x = x + gt1 * rms_norm(mix, g_post_mix)
        h2 = rms_norm(x, g_pre_ffn) * (1.0 + sc2) + sh2
        x = x + gt2 * rms_norm(ec_moe(h2, w_router[i], w_gate[i], w_up[i], w_down[i]), g_post_ffn)
        if need_ctx:
            ctx = ctx + cgt1 * rms_norm(mix_c, g_post_mix)
            hc2 = rms_norm(ctx, g_pre_ffn) * (1.0 + csc2) + csh2
            ctx = ctx + cgt2 * rms_norm(ec_moe(hc2, w_router[i], w_gate[i], w_up[i], w_down[i]), g_post_ffn)
    return x


DEPTH_2 = 2

HEAD_DIM = 64
N_MIXERS = 4
GROUP_WIDTH = D_MODEL // N_MIXERS
N_HEADS = GROUP_WIDTH // HEAD_DIM
ROPE_THETA = 10000.0
EPS = 1e-6
Q_BLOCK = 128
NEG_INF = -1e30

NSA_CMP_LEN = 32
NSA_CMP_STRIDE = 16
NSA_SLC_LEN = 64
NSA_TOP_N = 16
NSA_WINDOW = 512
NSA_FORCED_LOCAL = 2

DIFF_HALF = HEAD_DIM // 2

MLSTM_CHUNK = 64
MLSTM_CONV = 4

DILATED_PATTERNS = ((128, 1), (512, 4), (2048, 16))
DILATED_PAD = 2048

D_FF = ((8 * D_MODEL + 3 * 256 - 1) // (3 * 256)) * 256

IN_SPLITS = (
    GROUP_WIDTH,
    HEAD_DIM, HEAD_DIM,
    HEAD_DIM, HEAD_DIM,
    HEAD_DIM, HEAD_DIM,
    3 * N_HEADS,
    GROUP_WIDTH, GROUP_WIDTH, GROUP_WIDTH,
    GROUP_WIDTH, GROUP_WIDTH,
    N_HEADS, N_HEADS, GROUP_WIDTH,
    GROUP_WIDTH, GROUP_WIDTH, GROUP_WIDTH,
)
D_IN_2 = sum(IN_SPLITS)


def rmsnorm(x, g):
    xf = x.astype(jnp.float32)
    y = xf * lax.rsqrt(jnp.mean(xf * xf, axis=-1, keepdims=True) + EPS)
    return (y * g.astype(jnp.float32)).astype(x.dtype)

def rope_tables(seq, dim):
    inv = 1.0 / (ROPE_THETA ** (jnp.arange(0, dim, 2, dtype=jnp.float32) / dim))
    ang = jnp.arange(seq, dtype=jnp.float32)[:, None] * inv[None, :]
    return jnp.cos(ang), jnp.sin(ang)

def apply_rope(x, cos, sin):
    shape = (cos.shape[0],) + (1,) * (x.ndim - 3) + (cos.shape[1],)
    c, s = cos.reshape(shape), sin.reshape(shape)
    xf = x.astype(jnp.float32)
    half = x.shape[-1] // 2
    x1, x2 = xf[..., :half], xf[..., half:]
    return jnp.concatenate([x1 * c - x2 * s, x1 * s + x2 * c], axis=-1).astype(x.dtype)

def masked_softmax(s, mask, return_lse=False):
    s = jnp.where(mask, s.astype(jnp.float32), NEG_INF)
    m = jnp.max(s, axis=-1, keepdims=True)
    e = jnp.where(mask, jnp.exp(s - m), 0.0)
    z = jnp.sum(e, axis=-1, keepdims=True)
    z_safe = jnp.where(z > 0, z, 1.0)
    p = e / z_safe
    if return_lse:
        return p, (m + jnp.log(z_safe))[..., 0]
    return p

def sweep_query_blocks(fn, seq):
    out = lax.map(fn, jnp.arange(seq // Q_BLOCK) * Q_BLOCK)
    out = jnp.moveaxis(out, 0, 1)
    return out.reshape((out.shape[0], seq) + out.shape[3:])

def nsa_mixer(q, k_cmp, v_cmp, k_slc, v_slc, k_win, v_win, gate_pre, cmp_pos, cmp_w, cos, sin):
    bsz, seq = q.shape[0], q.shape[1]
    scale = HEAD_DIM ** -0.5
    t_pos = jnp.arange(seq)

    n_cmp = (seq - NSA_CMP_LEN) // NSA_CMP_STRIDE + 1
    blk_idx = np.arange(n_cmp)[:, None] * NSA_CMP_STRIDE + np.arange(NSA_CMP_LEN)[None, :]

    def compress(t, pos_emb, w):
        blocks = t[:, blk_idx] + pos_emb
        return blocks.reshape(bsz, n_cmp, NSA_CMP_LEN * HEAD_DIM) @ w

    kc = compress(k_cmp, cmp_pos[0], cmp_w[0])
    vc = compress(v_cmp, cmp_pos[1], cmp_w[1])
    cmp_end = jnp.arange(n_cmp) * NSA_CMP_STRIDE + NSA_CMP_LEN - 1
    cmp_mask = cmp_end[None, :] <= t_pos[:, None]
    p_cmp = masked_softmax(jnp.einsum('bshd,bnd->bhsn', q, kc) * scale, cmp_mask)
    o_cmp = jnp.einsum('bhsn,bnd->bshd', p_cmp.astype(vc.dtype), vc)

    n_slc = seq // NSA_SLC_LEN
    top_n = min(NSA_TOP_N, n_slc)
    ratio_s, ratio_c = NSA_SLC_LEN // NSA_CMP_STRIDE, NSA_CMP_LEN // NSA_CMP_STRIDE
    jj = np.arange(n_slc)[:, None, None]
    src = ratio_s * jj - np.arange(ratio_s)[None, :, None] - np.arange(ratio_c)[None, None, :]
    ok = (src >= 0) & (src < n_cmp)
    cmp_to_slc = np.zeros((n_cmp, n_slc), np.float32)
    np.add.at(cmp_to_slc, (np.where(ok, src, 0), np.broadcast_to(jj, src.shape)), ok.astype(np.float32))
    importance = jnp.einsum('bhsn,nj->bsj', p_cmp, jnp.asarray(cmp_to_slc))
    blk = jnp.arange(n_slc)[None, :]
    cur = (t_pos // NSA_SLC_LEN)[:, None]
    forced = (blk == 0) | ((blk <= cur) & (blk > cur - NSA_FORCED_LOCAL))
    score = jnp.where(blk > cur, -1.0e6, jnp.where(forced, 1.0e6, importance))
    _, sel_idx = lax.top_k(score, top_n)
    sel_valid = sel_idx <= cur[None]

    q_rot = apply_rope(q, cos, sin)
    ks = apply_rope(k_slc, cos, sin).reshape(bsz, n_slc, NSA_SLC_LEN, HEAD_DIM)
    vs = v_slc.reshape(bsz, n_slc, NSA_SLC_LEN, HEAD_DIM)
    pad = ((0, 0), (NSA_WINDOW, 0), (0, 0))
    kw = jnp.pad(apply_rope(k_win, cos, sin), pad)
    vw = jnp.pad(v_win, pad)
    b_idx = jnp.arange(bsz)[:, None, None]
    n_sel_keys = top_n * NSA_SLC_LEN

    def block(s0):
        qb = lax.dynamic_slice_in_dim(q_rot, s0, Q_BLOCK, axis=1)
        tq = s0 + jnp.arange(Q_BLOCK)
        idx = lax.dynamic_slice_in_dim(sel_idx, s0, Q_BLOCK, axis=1)
        valid = lax.dynamic_slice_in_dim(sel_valid, s0, Q_BLOCK, axis=1)
        kg = ks[b_idx, idx].reshape(bsz, Q_BLOCK, n_sel_keys, HEAD_DIM)
        vg = vs[b_idx, idx].reshape(bsz, Q_BLOCK, n_sel_keys, HEAD_DIM)
        kpos = (idx[..., None] * NSA_SLC_LEN + jnp.arange(NSA_SLC_LEN)).reshape(bsz, Q_BLOCK, n_sel_keys)
        kvalid = jnp.repeat(valid, NSA_SLC_LEN, axis=-1) & (kpos <= tq[None, :, None])
        p = masked_softmax(jnp.einsum('bqhd,bqkd->bhqk', qb, kg) * scale, kvalid[:, None])
        o_slc = jnp.einsum('bhqk,bqkd->bqhd', p.astype(vg.dtype), vg)
        kwb = lax.dynamic_slice_in_dim(kw, s0, NSA_WINDOW + Q_BLOCK, axis=1)
        vwb = lax.dynamic_slice_in_dim(vw, s0, NSA_WINDOW + Q_BLOCK, axis=1)
        wpos = s0 - NSA_WINDOW + jnp.arange(NSA_WINDOW + Q_BLOCK)
        wmask = (wpos[None, :] <= tq[:, None]) & (wpos[None, :] > tq[:, None] - NSA_WINDOW) & (wpos[None, :] >= 0)
        p = masked_softmax(jnp.einsum('bqhd,bkd->bhqk', qb, kwb) * scale, wmask)
        o_win = jnp.einsum('bhqk,bkd->bqhd', p.astype(vwb.dtype), vwb)
        return jnp.stack([o_slc, o_win], axis=2)

    o_sw = sweep_query_blocks(block, seq)
    g = jax.nn.sigmoid(gate_pre.astype(jnp.float32)).reshape(bsz, seq, 3, N_HEADS, 1).astype(q.dtype)
    o = g[:, :, 0] * o_cmp + g[:, :, 1] * o_sw[:, :, 0] + g[:, :, 2] * o_sw[:, :, 1]
    return o.reshape(bsz, seq, GROUP_WIDTH)

def diff_mixer(q, k, v, lam_vecs, sub_g, lam_init, cos, sin):
    bsz, seq = q.shape[0], q.shape[1]
    q = apply_rope(q, cos, sin)
    k = apply_rope(k, cos, sin)
    lv = lam_vecs.astype(jnp.float32)
    lam = jnp.exp(jnp.sum(lv[0] * lv[1])) - jnp.exp(jnp.sum(lv[2] * lv[3])) + lam_init
    scale = DIFF_HALF ** -0.5
    kpos = jnp.arange(seq)

    def block(s0):
        qb = lax.dynamic_slice_in_dim(q, s0, Q_BLOCK, axis=1)
        tq = s0 + jnp.arange(Q_BLOCK)
        s = jnp.einsum('bqhcd,bkhcd->bhcqk', qb, k) * scale
        p = masked_softmax(s, kpos[None, :] <= tq[:, None])
        a = p[:, :, 0] - lam * p[:, :, 1]
        return jnp.einsum('bhqk,bkhd->bqhd', a.astype(v.dtype), v)

    o = sweep_query_blocks(block, seq)
    o = rmsnorm(o, sub_g) * (1.0 - lam_init)
    return o.reshape(bsz, seq, GROUP_WIDTH)

def mlstm_mixer(u, v, i_pre, f_pre, o_pre, conv_w, conv_b, wq, wk, gate_b, head_g):
    bsz, seq = u.shape[0], u.shape[1]
    f32 = jnp.float32
    uc = lax.conv_general_dilated(u, conv_w[:, None, :], window_strides=(1,),
                                  padding=[(MLSTM_CONV - 1, 0)],
                                  dimension_numbers=('NWC', 'WIO', 'NWC'),
                                  feature_group_count=GROUP_WIDTH) + conv_b
    uc = jax.nn.silu(uc).reshape(bsz, seq, N_HEADS, HEAD_DIM)
    q = jnp.einsum('bshd,hde->bhse', uc, wq).astype(f32)
    k = jnp.einsum('bshd,hde->bhse', uc, wk).astype(f32) * (HEAD_DIM ** -0.5)
    vv = v.reshape(bsz, seq, N_HEADS, HEAD_DIM).transpose(0, 2, 1, 3).astype(f32)
    gb = gate_b.astype(f32)
    ig = (i_pre.astype(f32) + gb[0]).transpose(0, 2, 1)
    lf = jax.nn.log_sigmoid(f_pre.astype(f32) + gb[1]).transpose(0, 2, 1)

    nc, L = seq // MLSTM_CHUNK, MLSTM_CHUNK
    q = q.reshape(bsz, N_HEADS, nc, L, HEAD_DIM)
    k = k.reshape(bsz, N_HEADS, nc, L, HEAD_DIM)
    vv = vv.reshape(bsz, N_HEADS, nc, L, HEAD_DIM)
    ig = ig.reshape(bsz, N_HEADS, nc, L)
    b = jnp.cumsum(lf.reshape(bsz, N_HEADS, nc, L), axis=-1)
    causal = jnp.tril(jnp.ones((L, L), dtype=bool))
    dmat = jnp.where(causal, b[..., :, None] - b[..., None, :] + ig[..., None, :], NEG_INF)

    a = b[..., -1]
    g_end = a[..., None] - b + ig
    m_loc = jnp.max(g_end, axis=-1)
    w_end = jnp.exp(g_end - m_loc[..., None])
    c_loc = jnp.einsum('bhcl,bhclv,bhclk->bhcvk', w_end, vv, k)
    n_loc = jnp.einsum('bhcl,bhclk->bhck', w_end, k)

    def step(carry, xs):
        c_st, n_st, m_st = carry
        a_c, m_l, c_l, n_l = xs
        m_new = jnp.maximum(a_c + m_st, m_l)
        decay = jnp.exp(a_c + m_st - m_new)
        fresh = jnp.exp(m_l - m_new)
        c_new = decay[..., None, None] * c_st + fresh[..., None, None] * c_l
        n_new = decay[..., None] * n_st + fresh[..., None] * n_l
        return (c_new, n_new, m_new), (c_st, n_st, m_st)

    init = (jnp.zeros((bsz, N_HEADS, HEAD_DIM, HEAD_DIM), f32),
            jnp.zeros((bsz, N_HEADS, HEAD_DIM), f32),
            jnp.zeros((bsz, N_HEADS), f32))
    xs = (jnp.moveaxis(a, 2, 0), jnp.moveaxis(m_loc, 2, 0),
          jnp.moveaxis(c_loc, 2, 0), jnp.moveaxis(n_loc, 2, 0))
    _, (c_in, n_in, m_in) = lax.scan(step, init, xs)
    c_in = jnp.moveaxis(c_in, 0, 2)
    n_in = jnp.moveaxis(n_in, 0, 2)
    m_in = jnp.moveaxis(m_in, 0, 2)

    inter = b + m_in[..., None]
    m_t = jnp.maximum(inter, jnp.max(dmat, axis=-1))
    e_inter = jnp.exp(inter - m_t)
    s_qk = jnp.einsum('bhctd,bhcsd->bhcts', q, k) * jnp.exp(dmat - m_t[..., None])
    num = (e_inter[..., None] * jnp.einsum('bhcvk,bhctk->bhctv', c_in, q)
           + jnp.einsum('bhcts,bhcsv->bhctv', s_qk, vv))
    den = e_inter * jnp.einsum('bhck,bhctk->bhct', n_in, q) + jnp.sum(s_qk, axis=-1)
    h = num / jnp.maximum(jnp.abs(den), jnp.exp(-m_t))[..., None]
    h = h.reshape(bsz, N_HEADS, seq, HEAD_DIM).transpose(0, 2, 1, 3)
    h = rmsnorm(h, head_g.reshape(N_HEADS, HEAD_DIM))
    h = h * jax.nn.sigmoid(o_pre.astype(f32)).reshape(bsz, seq, N_HEADS, HEAD_DIM)
    return h.reshape(bsz, seq, GROUP_WIDTH).astype(u.dtype)

def dilated_mixer(q, k, v, cos, sin):
    bsz, seq = q.shape[0], q.shape[1]
    q = apply_rope(q, cos, sin)
    k = apply_rope(k, cos, sin)
    pad = ((0, 0), (DILATED_PAD, 0), (0, 0), (0, 0))
    kp, vp = jnp.pad(k, pad), jnp.pad(v, pad)
    scale = HEAD_DIM ** -0.5

    def block(s0):
        qb = lax.dynamic_slice_in_dim(q, s0, Q_BLOCK, axis=1)
        tq = s0 + jnp.arange(Q_BLOCK)
        kseg = lax.dynamic_slice_in_dim(kp, s0, DILATED_PAD + Q_BLOCK, axis=1)
        vseg = lax.dynamic_slice_in_dim(vp, s0, DILATED_PAD + Q_BLOCK, axis=1)
        outs, lses = [], []
        for window, dil in DILATED_PATTERNS:
            n_keys = window // dil + 1
            rel = np.arange(Q_BLOCK)[:, None] + DILATED_PAD - np.arange(n_keys)[None, :] * dil
            kg, vg = kseg[:, rel], vseg[:, rel]
            kpos = tq[:, None] - jnp.arange(n_keys)[None, :] * dil
            s = jnp.einsum('bqhd,bqjhd->bhqj', qb, kg) * scale
            p, lse = masked_softmax(s, kpos >= 0, return_lse=True)
            outs.append(jnp.einsum('bhqj,bqjhd->bqhd', p.astype(vg.dtype), vg))
            lses.append(jnp.transpose(lse, (0, 2, 1)))
        alpha = jax.nn.softmax(jnp.stack(lses, axis=0), axis=0)
        return jnp.einsum('gbqh,gbqhd->bqhd', alpha.astype(q.dtype), jnp.stack(outs, axis=0))

    o = sweep_query_blocks(block, seq)
    return o.reshape(bsz, seq, GROUP_WIDTH)

def second_inputs(seed: int = 0) -> dict:
    key = jax.random.key(seed)
    k = jax.random.split(key, 20)
    f32 = jnp.float32

    def normal(kk, shape, scale):
        return jax.random.normal(kk, shape, f32) * scale

    def gain(kk, shape):
        return 1.0 + 0.02 * jax.random.normal(kk, shape, f32)

    forget_bias = jnp.linspace(3.0, 6.0, N_HEADS, dtype=f32)
    mlstm_gate_b = jnp.stack([normal(k[10], (DEPTH_2, N_HEADS), 0.1),
                              forget_bias + normal(k[11], (DEPTH_2, N_HEADS), 0.1)], axis=1)
    return {
        'x': normal(k[0], (BATCH, SEQ, D_MODEL), 1.0),
        'norm_mix': gain(k[1], (DEPTH_2, D_MODEL)),
        'w_in': normal(k[2], (DEPTH_2, D_MODEL, D_IN_2), D_MODEL ** -0.5),
        'nsa_cmp_pos': normal(k[3], (DEPTH_2, 2, NSA_CMP_LEN, HEAD_DIM), 0.1),
        'nsa_cmp_w': normal(k[4], (DEPTH_2, 2, NSA_CMP_LEN * HEAD_DIM, HEAD_DIM), (NSA_CMP_LEN * HEAD_DIM) ** -0.5),
        'diff_lambda': normal(k[5], (DEPTH_2, 4, DIFF_HALF), 0.1),
        'diff_norm': gain(k[6], (DEPTH_2, HEAD_DIM)),
        'mlstm_conv_w': normal(k[7], (DEPTH_2, MLSTM_CONV, GROUP_WIDTH), MLSTM_CONV ** -0.5),
        'mlstm_conv_b': normal(k[8], (DEPTH_2, GROUP_WIDTH), 0.02),
        'mlstm_wq': normal(k[9], (DEPTH_2, N_HEADS, HEAD_DIM, HEAD_DIM), HEAD_DIM ** -0.5),
        'mlstm_wk': normal(k[12], (DEPTH_2, N_HEADS, HEAD_DIM, HEAD_DIM), HEAD_DIM ** -0.5),
        'mlstm_gate_b': mlstm_gate_b,
        'mlstm_norm': gain(k[13], (DEPTH_2, GROUP_WIDTH)),
        'w_out': normal(k[14], (DEPTH_2, D_MODEL, D_MODEL), D_MODEL ** -0.5),
        'norm_ffn': gain(k[15], (DEPTH_2, D_MODEL)),
        'w_gate': normal(k[16], (DEPTH_2, D_MODEL, D_FF), D_MODEL ** -0.5),
        'w_up': normal(k[17], (DEPTH_2, D_MODEL, D_FF), D_MODEL ** -0.5),
        'w_down': normal(k[18], (DEPTH_2, D_FF, D_MODEL), D_FF ** -0.5),
        'norm_final': gain(k[19], (D_MODEL,)),
    }

def second_block(x, norm_mix, w_in, nsa_cmp_pos, nsa_cmp_w, diff_lambda, diff_norm,
              mlstm_conv_w, mlstm_conv_b, mlstm_wq, mlstm_wk, mlstm_gate_b, mlstm_norm,
              w_out, norm_ffn, w_gate, w_up, w_down, norm_final):
    bsz, seq, _ = x.shape
    cos64, sin64 = rope_tables(seq, HEAD_DIM)
    cos32, sin32 = rope_tables(seq, DIFF_HALF)
    offsets = [int(o) for o in np.cumsum(IN_SPLITS)[:-1]]

    def heads(t):
        return t.reshape(bsz, seq, N_HEADS, HEAD_DIM)

    for layer in range(DEPTH_2):
        h = rmsnorm(x, norm_mix[layer])
        z = h @ w_in[layer]
        (a_q, a_kc, a_vc, a_ks, a_vs, a_kw, a_vw, a_g,
         b_q, b_k, b_v, c_u, c_v, c_i, c_f, c_o, d_q, d_k, d_v) = jnp.split(z, offsets, axis=-1)
        o_a = nsa_mixer(heads(a_q), a_kc, a_vc, a_ks, a_vs, a_kw, a_vw, a_g,
                        nsa_cmp_pos[layer], nsa_cmp_w[layer], cos64, sin64)
        lam_init = 0.8 - 0.6 * math.exp(-0.3 * layer)
        o_b = diff_mixer(b_q.reshape(bsz, seq, N_HEADS, 2, DIFF_HALF),
                         b_k.reshape(bsz, seq, N_HEADS, 2, DIFF_HALF), heads(b_v),
                         diff_lambda[layer], diff_norm[layer], lam_init, cos32, sin32)
        o_c = mlstm_mixer(c_u, c_v, c_i, c_f, c_o, mlstm_conv_w[layer], mlstm_conv_b[layer],
                          mlstm_wq[layer], mlstm_wk[layer], mlstm_gate_b[layer], mlstm_norm[layer])
        o_d = dilated_mixer(heads(d_q), heads(d_k), heads(d_v), cos64, sin64)
        x = x + jnp.concatenate([o_a, o_b, o_c, o_d], axis=-1) @ w_out[layer]
        h = rmsnorm(x, norm_ffn[layer])
        x = x + (jax.nn.silu(h @ w_gate[layer]) * (h @ w_up[layer])) @ w_down[layer]
    return rmsnorm(x, norm_final)


def setup_inputs(seed=0):
    out = dict(first_inputs(seed))
    for name, value in second_inputs(seed + 1).items():
        if name != "x":
            out[name + "_2"] = value
    return out


def reference(
    x, c, ctx, c_ctx, w_mod, b_mod, norm_gains, w_in, rwkv_conv, rwkv_w0, rwkv_w2, rwkv_a0,
    rwkv_a2, rwkv_g2, rwkv_k_k, rwkv_k_a, rwkv_r_k, rwkv_lnx_w, rwkv_lnx_b, w_out, w_router,
    w_gate, w_up, w_down, norm_mix_2, w_in_2, nsa_cmp_pos_2, nsa_cmp_w_2, diff_lambda_2,
    diff_norm_2, mlstm_conv_w_2, mlstm_conv_b_2, mlstm_wq_2, mlstm_wk_2, mlstm_gate_b_2,
    mlstm_norm_2, w_out_2, norm_ffn_2, w_gate_2, w_up_2, w_down_2, norm_final_2,
):
    x = first_block(
        x, c, ctx, c_ctx, w_mod, b_mod, norm_gains, w_in, rwkv_conv, rwkv_w0, rwkv_w2, rwkv_a0,
        rwkv_a2, rwkv_g2, rwkv_k_k, rwkv_k_a, rwkv_r_k, rwkv_lnx_w, rwkv_lnx_b, w_out, w_router,
        w_gate, w_up, w_down,
    )
    return second_block(
        x, norm_mix_2, w_in_2, nsa_cmp_pos_2, nsa_cmp_w_2, diff_lambda_2, diff_norm_2,
        mlstm_conv_w_2, mlstm_conv_b_2, mlstm_wq_2, mlstm_wk_2, mlstm_gate_b_2, mlstm_norm_2,
        w_out_2, norm_ffn_2, w_gate_2, w_up_2, w_down_2, norm_final_2,
    )


_drawn_inputs = setup_inputs


def setup_inputs(seed=0):
    import zlib

    import numpy as np

    out = dict(_drawn_inputs(seed))
    spreads = {}
    factors = {'rwkv_lnx_b': 5.495,
     'diff_norm_2': 5.199,
     'mlstm_conv_b_2': 4.265,
     'mlstm_norm_2': 7.881,
     'norm_ffn_2': 3.16,
     'nsa_cmp_pos_2': 3.262}
    for name, (base, spread) in spreads.items():
        noise = np.random.default_rng([zlib.crc32(name.encode()), seed]).standard_normal(out[name].shape)
        drawn = base * np.exp(spread * noise) if base else spread * noise
        out[name] = jnp.asarray(drawn.astype(out[name].dtype))
    for name, factor in factors.items():
        out[name] = (out[name] * factor).astype(out[name].dtype)
    return out
```

```python
from contextlib import ExitStack

import numpy as np

import concourse.bass as bass
from concourse import mybir

ALU = mybir.AluOpType
ACT = mybir.ActivationFunctionType
AX = mybir.AxisListType.X
F32 = mybir.dt.float32

P = 128
D = 1024
T = 256
KT = D // P
TT = T // P
NB = 5
NX = 3
SLOT = 4096
CTX, LAT = 0, 1
H = 8
HD = 64
C = 64
EPS = 1e-6
GN_EPS = 64e-5
NEG = -1e30
NE = 16
CAP = 2 * T // NE

STREAM = (
    [("w_mod", i) for i in range(4)]
    + [("w_in", i) for i in range(9)]
    + [("w_mod", 4), ("w_mod", 5), ("w_out", 0), ("w_out", 1)]
    + [("w_mod", i) for i in range(6, 12)]
    + [("w_moe", i) for i in range(6 * NE)]
)
FF = 2816
NFT = FF // P
FCH = 6
for _l in range(2):
    STREAM += [("w_in_2", 7 * _l + i) for i in range(7)] + [("w_out_2", 2 * _l + i) for i in range(2)]
    for _i in range(FCH):
        STREAM += [("w_gate_2", FCH * _l + _i), ("w_up_2", FCH * _l + _i)]
    STREAM += [("w_down_2", FCH * _l + _i) for _i in range(FCH)]


class Arena:

    def __init__(self, nc, words):
        self.t = nc.alloc_sbuf_tensor("arena", [P, words], F32)
        self.low, self.high = 0, words

    def view(self, at, shape):
        n = int(np.prod(shape))
        v = self.t[:, at:at + n]
        names = "abcd"[:len(shape)]
        if len(shape) > 1:
            v = v.rearrange(f"p ({' '.join(names)}) -> p {' '.join(names)}",
                            **{names[i]: shape[i] for i in range(len(shape))})
        return v

    def keep(self, *shape):
        at = self.low
        self.low += int(np.prod(shape))
        assert self.low <= self.high, (self.low, self.high)
        return self.view(at, shape)

    def temp(self, *shape):
        self.high -= int(np.prod(shape))
        assert self.low <= self.high, (self.low, self.high)
        return self.view(self.high, shape)


class WeightStream:

    def __init__(self, nc, arrays):
        self.arrays = arrays
        self.ring = nc.alloc_sbuf_tensor("weight_ring", [P, NB, SLOT], F32)
        self.landed = [nc.alloc_semaphore(f"weights_landed_{i}") for i in range(NB + NX)]
        self.used = nc.alloc_semaphore("weight_slot_used")
        self.loaded = 0
        self.read = 0
        self.reads_to = 0
        self.extra = None
        first = STREAM.index(("w_moe", 0))
        end = first + 6 * NE
        turns = NB + NX
        assert (end - first) % turns == 0
        place = []
        for n in range(len(STREAM)):
            if n < first:
                place.append(n % NB)
            elif n < end:
                at = (n - first) % turns
                place.append((first + at) % NB if at < NB else at)
            else:
                place.append((first + n - end) % NB)
        self.place = place
        self.before = [max((m for m in range(n) if place[m] == place[n]), default=-1) for n in range(len(STREAM))]
        self.count = [place[:n + 1].count(place[n]) for n in range(len(STREAM))]

    def slot(self, n):
        at = self.place[n]
        return self.ring[:, at, :] if at < NB else self.extra[:, at - NB, :]

    def load_to(self, sp, end):
        for n in range(self.loaded, min(end, len(STREAM))):
            if self.before[n] >= 0:
                sp.wait_ge(self.used, self.before[n] + 1)
            name, i = STREAM[n]
            sp.dma_start(self.slot(n), self.arrays[name][i]).then_inc(self.landed[self.place[n]], 16)
            self.loaded = n + 1

    def load_ahead(self, sp, n):
        self.reads_to += n
        self.load_to(sp, self.reads_to + NB)

    def take(self, pe):
        n = self.read
        pe.wait_ge(self.landed[self.place[n]], 16 * self.count[n])
        self.read += 1
        return self.slot(n).rearrange("p (k n) -> p k n", n=512)


def chain(engine, sem):
    count = [0]

    def link(instruction):
        instruction.then_inc(sem, 1)
        count[0] += 1
        engine.wait_ge(sem, count[0])

    return link


def modulate_and_norm(nc, K):
    A, W = K.A, K.W
    top = A.high
    x_ctx, x_lat = A.temp(TT, D), A.temp(TT, D)
    h = A.temp(2 * TT, D)
    cT = A.temp(KT * 2)
    cond = A.temp(2 * KT, P)
    gain = A.temp(D)
    brow = A.temp(2 * D)
    gmod = A.temp(2, D)
    shift = A.temp(2, D)
    sumsq = A.temp(4)
    rstd = A.temp(4)
    ms = A.temp(4)
    root = A.temp(4)
    with nc.cleanup_on_exit():
        in_small = K.sem("conditioning_landed")
        in_x = K.sem("x_landed")
        ones_set = K.sem("ones_set")
        silu_done = K.sem("silu_done")
        cond_ready = K.sem("cond_ready")
        mod_ready = K.sem("mod_ready")
        mod_read = K.sem("mod_read")
        squares = K.sem("squares_summed")
        ms_ready = K.sem("mean_squares_ready")
        root_ready = K.sem("root_ready")
        h_ready = K.sem("h_ready")
        hT_made = K.sem("hT_made")
        hT_read = K.sem("hT_read")
        dve_step = K.sem("dve_step")

        with nc.Block() as block:
            @block.sync
            def _(sp):
                sp.dma_start(cT, K.dram["cT"]).then_inc(in_small, 16)
                sp.dma_start(brow[0:1, :], K.dram["b_mod"][:, 0:2 * D]).then_inc(in_small, 16)
                sp.dma_start(gain, K.dram["norm_gains"][0, :].partition_broadcast(P)).then_inc(in_small, 16)
                sp.dma_start(K.ident, K.dram["ident"]).then_inc(in_small, 16)
                sp.dma_start(x_ctx, K.dram["ctx"].rearrange("(t p) d -> p t d", p=P)).then_inc(in_x, 16)
                sp.dma_start(x_lat, K.dram["x"].rearrange("(t p) d -> p t d", p=P)).then_inc(in_x, 16)
                W.load_to(sp, NB)
                W.load_ahead(sp, 4)

            @block.gpsimd
            def _(pool):
                nc.gpsimd.memset(K.ones, 1.0).then_inc(ones_set, 1)
                pool.wait_ge(ones_set, 1)
                nc.gpsimd.memset(K.head_ones, 0.0).then_inc(ones_set, 1)
                pool.wait_ge(ones_set, 2)
                for i in range(2):
                    nc.gpsimd.memset(K.head_ones[i * HD:(i + 1) * HD, i * HD:(i + 1) * HD], 1.0).then_inc(ones_set, 1)

            @block.scalar
            def _(act):
                act.wait_ge(in_small, 64)
                nc.scalar.activation(cT, cT, ACT.Silu).then_inc(silu_done, 1)
                act.wait_ge(in_x, 32)
                for j in range(4):
                    src = x_ctx[:, j, :] if j < 2 else x_lat[:, j - 2, :]
                    nc.scalar.activation(h[:, j, :], src, ACT.Square, accum_out=sumsq[:, j:j + 1]).then_inc(squares, 1)
                act.wait_ge(ms_ready, 1)
                nc.scalar.activation(root, ms, ACT.Sqrt).then_inc(root_ready, 1)
                for j in range(4):
                    for q in range(2):
                        n = 2 * j + q
                        act.wait_ge(hT_made, n + 1)
                        nc.scalar.activation(K.hT[:, 4 * q:4 * q + 4, P * j:P * j + P],
                                             K.ps[:, n % 4, :].rearrange("p (k t) -> p k t", t=P),
                                             ACT.Copy).then_inc(hT_read, 1)

            @block.vector
            def _(dve):
                link = chain(dve, dve_step)
                dve.wait_ge(silu_done, 1)
                nc.vector.tensor_copy(cond, cT.unsqueeze(2).broadcast_to([P, 2 * KT, P])).then_inc(cond_ready, 1)
                dve.wait_ge(squares, 4)
                nc.vector.tensor_scalar(ms, sumsq, 1.0 / D, EPS, ALU.mult, ALU.add).then_inc(ms_ready, 1)
                dve.wait_ge(root_ready, 1)
                link(nc.vector.reciprocal(rstd, root))
                for n in range(8):
                    dve.wait_ge(mod_ready, n + 1)
                    c, s = n // 2, n % 2
                    half = slice(512 * (c % 2), 512 * (c % 2) + 512)
                    if c < 2:
                        link(nc.vector.tensor_copy(shift[:, s, half], K.ps[:, n, :]))
                    else:
                        nc.vector.scalar_tensor_tensor(gmod[:, s, half], K.ps[:, n, :], 1.0, gain[:, half],
                                                       ALU.add, ALU.mult).then_inc(mod_read, 1)
                dve.wait_ge(mod_read, 4)
                for j in range(4):
                    src = x_ctx[:, j, :] if j < 2 else x_lat[:, j - 2, :]
                    link(nc.vector.scalar_tensor_tensor(h[:, j, :], src, rstd[:, j:j + 1], gmod[:, j // 2, :],
                                                        ALU.mult, ALU.mult))
                    nc.vector.tensor_tensor(h[:, j, :], h[:, j, :], shift[:, j // 2, :], ALU.add).then_inc(h_ready, 1)

            @block.tensor
            def _(pe):
                pe.wait_ge(in_small, 64)
                pe.wait_ge(ones_set, 4)
                pe.wait_ge(cond_ready, 1)
                for c in range(4):
                    w = W.take(pe)
                    for s in range(2):
                        bank = K.ps[:, 2 * c + s, :]
                        for k in range(KT):
                            last = nc.tensor.matmul(bank, cond[:, s * KT + k, :], w[:, k, :], start=(k == 0), stop=False)
                        if s == 1:
                            last.then_inc(W.used, 1)
                        nc.tensor.matmul(bank, K.ones[0:1, :], brow[0:1, 512 * c:512 * c + 512],
                                         start=False, stop=True).then_inc(mod_ready, 1)
                for j in range(4):
                    pe.wait_ge(h_ready, j + 1)
                    if j == 0:
                        pe.wait_ge(mod_read, 4)
                    for q in range(2):
                        n = 2 * j + q
                        if n >= 4:
                            pe.wait_ge(hT_read, n - 3)
                        for k in range(4):
                            last = nc.tensor.transpose(K.ps[:, n % 4, P * k:P * k + P],
                                                       h[:, j, P * (4 * q + k):P * (4 * q + k + 1)], K.ident)
                        last.then_inc(hT_made, 1)
    A.high = top


def project_in(nc, K):
    A, W = K.A, K.W
    K.qT = A.keep(4, T)
    K.kT = A.keep(4, T)
    K.v_tok = A.keep(TT, 512)
    K.kc_tok = A.keep(TT, 512)
    K.vc_tok = A.keep(TT, 512)
    K.gateT = A.keep(4, 2, T)
    conv = A.keep(16, 3)
    hT = K.hT

    jobs = []
    for b in range(4):
        jobs.append((0, "T", b, K.qT[:, b, :], "copy"))
    for b in range(4):
        jobs.append((1, "T", b, K.kT[:, b, :], "scaled"))
    for t in range(2):
        jobs.append((1, "tok", t, K.kc_tok[:, t, :], "scaled"))
    for t in range(4):
        jobs.append((2, "tok", t, (K.vc_tok if t < 2 else K.v_tok)[:, t % 2, :], "copy"))
    for b in range(4):
        jobs.append((3, "T", b, K.gateT[:, b, 0, :], "silu"))
    for b in range(4):
        jobs.append((4, "T", b, K.gateT[:, b, 1, :], "silu"))
    for b in range(4):
        jobs.append((5, "T", b, K.rT[:, b, :], "conv"))
    for b in range(4):
        jobs.append((6, "TT", b, K.rkT[:, b, :], "conv"))
    for b in range(4):
        jobs.append((7, "TT", b, K.rvT[:, b, :], "conv"))
    jobs.append((8, "TT", 0, K.wlT, "conv"))
    jobs.append((8, "TT", 1, K.alT, "conv"))
    jobs.append((8, "T", 2, K.glT[:, 0, :], "conv"))
    jobs.append((8, "T", 3, K.glT[:, 1, :], "conv"))
    taken = [sum((j[4] == "conv") == (jobs[n][4] == "conv") for j in jobs[:n + 1]) for n in range(len(jobs))]

    with nc.cleanup_on_exit():
        in_conv = K.sem("conv_weights_landed")
        projected = K.sem("projected")
        act_took = K.sem("act_took")
        dve_took = K.sem("dve_took")
        dve_step = K.sem("dve_step")
        with nc.Block() as block:
            @block.sync
            def _(sp):
                sp.dma_start(conv, K.dram["rwkv_conv"]).then_inc(in_conv, 16)
                W.load_ahead(sp, 9)

            @block.tensor
            def _(pe):
                slot = -1
                for n, (s, kind, b, dst, how) in enumerate(jobs):
                    if s != slot:
                        w, slot = W.take(pe), s
                    if n >= 8:
                        pe.wait_ge(dve_took if jobs[n - 8][4] == "conv" else act_took, taken[n - 8])
                    bank = K.ps[:, n % 8, :]
                    for k in range(KT):
                        if kind == "tok":
                            last = nc.tensor.matmul(bank, hT[:, k, P * b:P * b + P], w[:, k, :],
                                                    start=(k == 0), stop=(k == KT - 1))
                        elif kind == "T":
                            last = nc.tensor.matmul(bank[:, 0:T], w[:, k, P * b:P * b + P], hT[:, k, T:2 * T],
                                                    start=(k == 0), stop=(k == KT - 1))
                        else:
                            last = nc.tensor.matmul(bank, w[:, k, P * b:P * b + P], hT[:, k, :],
                                                    start=(k == 0), stop=(k == KT - 1))
                        if k == 0 and n and jobs[n - 1][0] != s:
                            last.then_inc(W.used, 1)
                    last.then_inc(projected, 1)
                pe.wait_ge(projected, len(jobs))
                nc.tensor.nop().then_inc(W.used, 1)

            @block.scalar
            def _(act):
                for n, (s, kind, b, dst, how) in enumerate(jobs):
                    if how == "conv":
                        continue
                    act.wait_ge(projected, n + 1)
                    src = K.ps[:, n % 8, 0:T] if kind == "T" else K.ps[:, n % 8, :]
                    nc.scalar.activation(dst, src, ACT.Silu if how == "silu" else ACT.Copy,
                                         scale=HD ** -0.5 if how == "scaled" else 1.0).then_inc(act_took, 1)

            @block.vector
            def _(dve):
                link = chain(dve, dve_step)
                dve.wait_ge(in_conv, 16)
                for n, (s, kind, b, dst, how) in enumerate(jobs):
                    if how != "conv":
                        continue
                    dve.wait_ge(projected, n + 1)
                    w = conv[:, 4 * (s - 5) + b, :]
                    ns = 1 if kind == "T" else 2
                    u = K.ps[:, n % 8, 0:T * ns].rearrange("p (s t) -> p s t", s=ns)
                    o = dst.rearrange("p (s t) -> p s t", s=ns)
                    link(nc.vector.tensor_scalar(o, u, w[:, 1:2], None, ALU.mult))
                    link(nc.vector.scalar_tensor_tensor(o[:, :, 1:T], u[:, :, 0:T - 1], w[:, 0:1], o[:, :, 1:T],
                                                        ALU.mult, ALU.add))
                    nc.vector.scalar_tensor_tensor(o[:, :, 0:T - 1], u[:, :, 1:T], w[:, 2:3], o[:, :, 0:T - 1],
                                                   ALU.mult, ALU.add).then_inc(dve_took, 1)
    A.high += KT * 2 * T


def retention(nc, K):
    A = K.A
    top = A.high
    cos, sin, swap = A.temp(T), A.temp(T), A.temp(P)
    decay_f, decay_b = A.temp(H, T), A.temp(H, T)
    q_decay = A.temp(2, 4, T)
    k_decay = A.temp(2, TT, H)
    q_dec = q_decay
    state = A.temp(2, 4, P)
    k_dec, turned = A.temp(2, TT, 512), A.temp(2, 512)
    probs = A.view(A.high, (2, 2, 2, 3 * P))
    square, root = A.temp(2, 512), A.temp(2, 512)
    eps = A.temp(1)
    parts = {0: ((0, 0, T, 0), (1, P, T, T)), 1: ((0, 0, P, 0), (1, 0, T, P))}

    with nc.cleanup_on_exit():
        in_rope, in_tables = K.sem("rope_landed"), K.sem("tables_landed")
        swapped, rotated = K.sem("swapped"), K.sem("rotated")
        eps_set, dve_step = K.sem("eps_set"), K.sem("dve_step")
        k_decayed, state_made, state_kept = K.sem("k_decayed"), K.sem("state_made"), K.sem("state_kept")
        scored, masked = K.sem("scored"), K.sem("masked")
        y_made, squared, summed, rooted, y_used = (K.sem(n) for n in ("y_made", "squared", "summed", "rooted", "y_used"))
        with nc.Block() as block:
            @block.sync
            def _(sp):
                for dst, name in ((cos, "rope_cos"), (sin, "rope_sin"), (swap, "swap64")):
                    sp.dma_start(dst, K.dram[name]).then_inc(in_rope, 16)
                for dst, name in ((decay_f, "ret_decay_f"), (decay_b, "ret_decay_b"), (q_decay, "ret_q_decay"),
                                  (k_decay, "ret_k_decay")):
                    sp.dma_start(dst, K.dram[name]).then_inc(in_tables, 16)

            @block.gpsimd
            def _(pool):
                nc.gpsimd.memset(eps, EPS).then_inc(eps_set, 1)

            @block.tensor
            def _(pe):
                pe.wait_ge(in_rope, 48)
                for n in range(4):
                    x = (K.qT if n < 2 else K.kT)[:, 2 * (n % 2):2 * (n % 2) + 2, :]
                    nc.tensor.matmul(K.ps[:, n, :], swap, x, start=True, stop=True).then_inc(swapped, 1)
                for d in range(2):
                    pe.wait_ge(k_decayed, d + 1)
                    for b in range(4):
                        for t in range(TT):
                            last = nc.tensor.matmul(K.ps[:, 4 + d, P * b:P * b + P], k_dec[:, d, t, P * b:P * b + P],
                                                    K.vc_tok[:, t, P * b:P * b + P], start=(t == 0), stop=(t == TT - 1))
                    last.then_inc(state_made, 1)
                pe.wait_ge(rotated, 4)

                def scores(b):
                    if b >= 2:
                        pe.wait_ge(masked, 2 * (b - 1))
                    for i in range(2):
                        rows = slice(HD * i, HD * i + HD)
                        for t in range(TT):
                            last = nc.tensor.matmul(K.ps[:, 2 * (b % 2) + i, T * t:T * t + T],
                                                    K.kT[rows, b, P * t:P * t + P], K.qT[rows, b, :],
                                                    start=True, stop=True)
                        last.then_inc(scored, 1)

                scores(0)
                pe.wait_ge(state_kept, 2)
                for b in range(4):
                    if b < 3:
                        scores(b + 1)
                    if b >= 2:
                        pe.wait_ge(y_used, b - 1)
                    pe.wait_ge(masked, 2 * b + 2)
                    for d in range(2):
                        y = K.ps[:, 4 + b % 2, T * d:T * d + T]
                        nc.tensor.matmul(y, state[:, d, b, :], q_dec[:, d, b, :], start=True, stop=False,
                                         skip_group_check=True)
                        for i in range(2):
                            for t, t0, t1, at in parts[d]:
                                last = nc.tensor.matmul(y[HD * i:HD * i + HD, t0:t1],
                                                        K.v_tok[:, t, P * b + HD * i:P * b + HD * i + HD],
                                                        probs[:, b % 2, i, d, at:at + t1 - t0],
                                                        start=False, stop=(t == 1), skip_group_check=True)
                    last.then_inc(y_made, 1)
                    pe.wait_ge(squared, b + 1)
                    nc.tensor.matmul(K.ps[:, 6 + b % 2, :], K.head_ones, square[:, b % 2, :],
                                     start=True, stop=True).then_inc(summed, 1)

            @block.scalar
            def _(act):
                act.wait_ge(eps_set, 1)
                for b in range(4):
                    act.wait_ge(y_made, b + 1)
                    nc.scalar.activation(square[:, b % 2, :], K.ps[:, 4 + b % 2, :], ACT.Square).then_inc(squared, 1)
                    act.wait_ge(summed, b + 1)
                    if b >= 2:
                        act.wait_ge(y_used, b - 1)
                    nc.scalar.activation(root[:, b % 2, :], K.ps[:, 6 + b % 2, :], ACT.Sqrt, bias=eps[:, 0:1],
                                         scale=1.0 / HD).then_inc(rooted, 1)

            @block.vector
            def _(dve):
                link = chain(dve, dve_step)
                dve.wait_ge(in_tables, 64)
                for d in range(2):
                    for t in range(TT):
                        last = nc.vector.tensor_tensor(
                            k_dec[:, d, t, :].rearrange("p (h e) -> p h e", e=HD),
                            K.kc_tok[:, t, :].rearrange("p (h e) -> p h e", e=HD),
                            k_decay[:, d, t, :].unsqueeze(2).broadcast_to([P, H, HD]), ALU.mult)
                        if t == 1:
                            last.then_inc(k_decayed, 1)
                for n in range(4):
                    x = (K.qT if n < 2 else K.kT)[:, 2 * (n % 2):2 * (n % 2) + 2, :]
                    wide = [P, 2, T]
                    dve.wait_ge(swapped, n + 1)
                    link(nc.vector.tensor_tensor(turned[:, n % 2, :].rearrange("p (b t) -> p b t", b=2),
                                                 K.ps[:, n, :].rearrange("p (b t) -> p b t", b=2),
                                                 sin.unsqueeze(1).broadcast_to(wide), ALU.mult))
                    link(nc.vector.tensor_tensor(x, x, cos.unsqueeze(1).broadcast_to(wide), ALU.mult))
                    nc.vector.tensor_tensor(x, x, turned[:, n % 2, :].rearrange("p (b t) -> p b t", b=2),
                                            ALU.add).then_inc(rotated, 1)
                dve.wait_ge(rotated, 4)
                for d in range(2):
                    link(nc.vector.tensor_tensor(q_dec[:, d], K.qT, q_decay[:, d], ALU.mult))
                    dve.wait_ge(state_made, d + 1)
                    nc.vector.tensor_tensor(state[:, d], K.ps[:, 4 + d, :].rearrange("p (b v) -> p b v", v=P),
                                            K.head_ones.unsqueeze(1).broadcast_to([P, 4, P]),
                                            ALU.mult).then_inc(state_kept, 1)

                def mask(b):
                    for i in range(2):
                        h = 2 * b + i
                        dve.wait_ge(scored, h + 1)
                        if b >= 2:
                            dve.wait_ge(y_made, b - 1)
                        s = K.ps[:, 2 * (b % 2) + i, :]
                        p = probs[:, b % 2, i]
                        nc.vector.tensor_tensor(p[:, 0, 0:T], s[:, 0:T], decay_f[:, h, :], ALU.mult)
                        nc.vector.tensor_tensor(p[:, 0, T:3 * P], s[:, T + P:2 * T], decay_f[:, h, 0:P], ALU.mult)
                        nc.vector.tensor_tensor(p[:, 1, 0:P], s[:, 0:P], decay_b[:, h, P:T], ALU.mult)
                        nc.vector.tensor_tensor(p[:, 1, P:3 * P], s[:, T:2 * T], decay_b[:, h, :],
                                                ALU.mult).then_inc(masked, 1)

                mask(0)
                for b in range(4):
                    if b < 3:
                        mask(b + 1)
                    dve.wait_ge(rooted, b + 1)
                    n = square[:, b % 2, :]
                    link(nc.vector.reciprocal(root[:, b % 2, :], root[:, b % 2, :]))
                    nc.vector.tensor_tensor(n, K.ps[:, 4 + b % 2, :], root[:, b % 2, :], ALU.mult).then_inc(y_used, 1)
                    dve.wait_ge(y_used, b + 1)
                    link(nc.vector.tensor_tensor(n, n, K.gateT[:, b].rearrange("p d t -> p (d t)"), ALU.mult))
                    link(nc.vector.tensor_tensor(K.mixT[:, b, :], n[:, 0:T], n[:, T:2 * T], ALU.add))
    A.high = top
    A.low = K.after_mixT


def rwkv_constants(nc, K):
    A = K.A
    K.rwkv_low = A.low
    K.w0, K.w2, K.a2 = A.keep(H), A.keep(512), A.keep(512)
    K.g2 = A.keep(2, 512)
    K.vecs = A.keep(3, 4)
    K.dup_vecs = A.keep(3, H)
    K.masks = A.keep(9, C)
    K.reset = A.keep(2, T)
    K.stateT = A.keep(H, HD)
    K.fold = A.keep(HD)
    K.gn_eps = A.keep(1)
    with nc.cleanup_on_exit():
        landed, cleared, folded = K.sem("landed"), K.sem("cleared"), K.sem("folded")
        with nc.Block() as block:
            @block.sync
            def _(sp):
                small = ((K.w0, "rwkv_w0"), (K.w2, "rwkv_w2"), (K.a2[0:HD, :], "rwkv_a2"), (K.g2, "rwkv_g2"),
                         (K.vecs, "rwkv_vecs"), (K.dup_vecs, "rwkv_dup_vecs"), (K.masks, "rwkv_masks"))
                for dst, name in small:
                    sp.dma_start(dst, K.dram[name]).then_inc(landed, 16)
                sp.wait_ge(landed, 16 * len(small))

            @block.gpsimd
            def _(pool):
                nc.gpsimd.memset(K.stateT, 0.0)
                nc.gpsimd.memset(K.gn_eps, GN_EPS)
                nc.gpsimd.memset(K.reset, 1.0).then_inc(cleared, 1)
                pool.wait_ge(cleared, 1)
                nc.gpsimd.memset(K.reset.rearrange("p a (c t) -> p (a c) t", t=C)[:, :, 0:1], 0.0)

            @block.vector
            def _(dve):
                nc.vector.tensor_tensor(K.fold, K.ident[:, 0:HD], K.ident[:, HD:P], ALU.add).then_inc(folded, 1)


def rwkv_prepare_stage(nc, K, s):
    A = K.A
    lat = s == LAT
    if lat:
        K.bonus = A.keep(H, T)
    K.dup_low = A.low
    K.da, K.db, K.dk, K.dv = (A.keep(H, T) for _ in range(4))
    K.dr = A.keep(H, T) if lat else None
    K.tot = A.keep(4, H)
    top = A.high
    inc, exc, einc = (A.temp(2, 2, T) for _ in range(3))
    kmod, bb, kk = (A.view(A.high + 4 * T * n, (4, T)) for n in range(3))
    iclr, t = A.temp(4, T), A.temp(4, T)
    sg = A.temp(H, T)
    tok = slice(T * s, T * s + T)
    k, v = K.rkT[:, :, tok], K.rvT[:, :, tok]
    wl, al = K.wlT[:, tok], K.alT[0:HD, tok]
    spread = lambda i: K.vecs[:, i, :].unsqueeze(2).broadcast_to([P, 4, T])
    pair = lambda x, p: x[:, 2 * p:2 * p + 2, :]
    RATE = float(np.exp(-0.5))

    with nc.cleanup_on_exit():
        tanhed, al_made, z_made, iclr_ready, sg_ready = (K.sem(f"s{s}_{n}") for n in
                                                         ("tanhed", "al_made", "z_made", "iclr_ready", "sg_ready"))
        sq_ready, ss_made, root_ready = (K.sem(f"s{s}_{n}") for n in ("sq_ready", "ss_made", "root_ready"))
        ready = {n: K.sem(f"s{s}_{n}_ready") for n in "abk"}
        dup = {n: K.sem(f"s{s}_{n}_dup_landed") for n in "abkvr"}
        sums_ready, exp_ready, scaled, dve_step = (K.sem(f"s{s}_{n}") for n in
                                                   ("sums_ready", "exp_ready", "scaled", "dve_step"))
        if lat:
            gl_ready, prod_ready, bonus_made = (K.sem(f"s{s}_{n}") for n in ("gl_ready", "prod_ready", "bonus_made"))
        with nc.Block() as block:
            @block.sync
            def _(sp):
                def both_halves(dst, src, sem):
                    for i in range(2):
                        for d in range(2):
                            to = dst[HD * d:HD * d + HD].rearrange("p (b i) t -> p b i t", i=2)[:, :, i, :]
                            sp.dma_start(to, src[HD * i:HD * i + HD]).then_inc(sem, 16)

                both_halves(K.dv, v, dup["v"])
                if lat:
                    both_halves(K.dr, K.rT, dup["r"])
                sp.wait_ge(ready["a"], 1)
                both_halves(K.da, kk, dup["a"])
                sp.wait_ge(ready["b"], 1)
                both_halves(K.db, bb, dup["b"])
                sp.wait_ge(ready["k"], 1)
                both_halves(K.dk, kmod, dup["k"])
                for n in "abkvr" if lat else "abkv":
                    sp.wait_ge(dup[n], 64)

            @block.tensor
            def _(pe):
                for b in range(4):
                    last = nc.tensor.matmul(K.ps[:, b // 2, T * (b % 2):T * (b % 2) + T], K.a2[0:HD, P * b:P * b + P],
                                            al, start=True, stop=True)
                last.then_inc(al_made, 1)
                pe.wait_ge(tanhed, 1)
                for p in range(4):
                    for j in range(2):
                        for d in range(2):
                            rows = slice(HD * d, HD * d + HD)
                            h = 2 * p + j
                            last = nc.tensor.matmul(K.ps[rows, 4 + p, T * j:T * j + T], K.w2[rows, HD * h:HD * h + HD],
                                                    wl[rows], start=True, stop=True)
                    last.then_inc(z_made, 1)
                pe.wait_ge(sq_ready, 1)
                for i in range(2):
                    last = nc.tensor.matmul(K.ps[:, 2 + i, :], K.head_ones, t[:, 2 * i:2 * i + 2, :],
                                            start=True, stop=True)
                last.then_inc(ss_made, 1)
                if lat:
                    pe.wait_ge(sg_ready, 8)
                    for p in range(4):
                        pe.wait_ge(prod_ready, 1)
                        nc.tensor.matmul(K.ps[:, 4 + p, :], K.head_ones, pair(K.bonus, p),
                                         start=True, stop=True).then_inc(bonus_made, 1)

            @block.scalar
            def _(act):
                nc.scalar.activation(wl, wl, ACT.Tanh).then_inc(tanhed, 1)
                act.wait_ge(al_made, 1)
                for b in range(4):
                    nc.scalar.activation(iclr[:, b, :], K.ps[:, b // 2, T * (b % 2):T * (b % 2) + T], ACT.Sigmoid,
                                         bias=K.vecs[:, 0, b:b + 1]).then_inc(iclr_ready, 1)
                for h in range(H):
                    act.wait_ge(z_made, h // 2 + 1)
                    nc.scalar.activation(sg[:, h, :], K.ps[:, 4 + h // 2, T * (h % 2):T * (h % 2) + T], ACT.Sigmoid,
                                         bias=K.w0[:, h:h + 1]).then_inc(sg_ready, 1)
                if lat:
                    nc.scalar.activation(K.glT, K.glT, ACT.Sigmoid).then_inc(gl_ready, 1)
                act.wait_ge(ss_made, 1)
                for i in range(2):
                    nc.scalar.activation(t[:, 2 * i:2 * i + 2, :], K.ps[:, 2 + i, :].rearrange("p (b t) -> p b t", t=T),
                                         ACT.Sqrt).then_inc(root_ready, 1)
                for p in range(4):
                    act.wait_ge(sums_ready, p + 1)
                    if p == 3:
                        nc.scalar.activation(K.tot, K.tot, ACT.Exp, scale=-RATE)
                    if p >= 2:
                        act.wait_ge(scaled, p - 1)
                    nc.scalar.activation(einc[:, p % 2], inc[:, p % 2], ACT.Exp, scale=-RATE).then_inc(exp_ready, 1)
                    nc.scalar.activation(exc[:, p % 2], exc[:, p % 2], ACT.Exp, scale=-RATE).then_inc(exp_ready, 1)
                    act.wait_ge(exp_ready, 3 * p + 2)
                    nc.scalar.activation(inc[:, p % 2], inc[:, p % 2], ACT.Exp, scale=RATE).then_inc(exp_ready, 1)

            @block.vector
            def _(dve):
                link = chain(dve, dve_step)
                link(nc.vector.tensor_tensor(kk, k, spread(1), ALU.mult))
                nc.vector.tensor_tensor(t, kk, kk, ALU.mult).then_inc(sq_ready, 1)
                dve.wait_ge(root_ready, 2)
                link(nc.vector.tensor_scalar(t, t, 1e-12, None, ALU.max))
                link(nc.vector.reciprocal(t, t))
                nc.vector.scalar_tensor_tensor(kk, kk, -1.0, t, ALU.mult, ALU.mult).then_inc(ready["a"], 1)
                dve.wait_ge(ready["a"], 1)
                dve.wait_ge(iclr_ready, 4)
                nc.vector.scalar_tensor_tensor(bb, kk, -1.0, iclr, ALU.mult, ALU.mult).then_inc(ready["b"], 1)
                dve.wait_ge(ready["b"], 1)
                link(nc.vector.scalar_tensor_tensor(iclr, iclr, -1.0, spread(2), ALU.add, ALU.mult))
                nc.vector.scalar_tensor_tensor(kmod, iclr, 1.0, k, ALU.add, ALU.mult).then_inc(ready["k"], 1)
                for n in "ab":
                    dve.wait_ge(dup[n], 64)
                dve.wait_ge(dup["k"], 64)
                if lat:
                    dve.wait_ge(dup["r"], 64)
                    dve.wait_ge(dup["v"], 64)
                    link(nc.vector.tensor_tensor(K.bonus, K.dr, K.dup_vecs[:, 0, :].unsqueeze(2)
                                                 .broadcast_to([P, H, T]), ALU.mult))
                    nc.vector.tensor_tensor(K.bonus, K.bonus, K.dk, ALU.mult).then_inc(prod_ready, 1)
                    for p in range(4):
                        dve.wait_ge(bonus_made, p + 1)
                        link(nc.vector.tensor_tensor(pair(K.bonus, p), K.ps[:, 4 + p, :]
                                                     .rearrange("p (j t) -> p j t", t=T), pair(K.dv, p), ALU.mult))
                lo, hi = slice(0, HD), slice(HD, P)

                def sums(p):
                    i, e = inc[:, p % 2], exc[:, p % 2]
                    dve.wait_ge(sg_ready, 2 * p + 2)
                    if p >= 2:
                        dve.wait_ge(scaled, p - 1)
                    g = pair(sg, p)
                    link(nc.vector.tensor_tensor_scan(i.rearrange("p a t -> p (a t)"),
                                                      K.reset.rearrange("p a t -> p (a t)"),
                                                      g.rearrange("p a t -> p (a t)"), 0.0, ALU.mult, ALU.add))
                    by_chunk = i.rearrange("p a (c t) -> p a c t", t=C)
                    ends = by_chunk[:, :, :, C - 1]
                    to = K.tot.rearrange("p c h -> p h c")[:, 2 * p:2 * p + 2, :]
                    link(nc.vector.tensor_copy(to[lo], ends[lo]))
                    link(nc.vector.tensor_copy(to[hi], ends[hi][:, :, ::-1]))
                    link(nc.vector.tensor_tensor(e[lo], i[lo], g[lo], ALU.subtract))
                    for j in range(2):
                        link(nc.vector.tensor_tensor(e[hi, j].rearrange("p (c t) -> p c t", t=C),
                                                     by_chunk[hi, j, :, C - 1:C].broadcast_to([HD, 4, C]),
                                                     by_chunk[hi, j], ALU.subtract))
                    nc.vector.tensor_tensor(i[hi], e[hi], g[hi], ALU.add).then_inc(sums_ready, 1)

                sums(0)
                for p in range(4):
                    if p < 3:
                        sums(p + 1)
                    dve.wait_ge(exp_ready, 3 * p + 3)
                    if lat:
                        nc.vector.tensor_tensor(pair(K.dr, p), pair(K.dr, p), einc[:, p % 2], ALU.mult)
                    nc.vector.tensor_tensor(pair(K.da, p), pair(K.da, p), exc[:, p % 2], ALU.mult)
                    nc.vector.tensor_tensor(pair(K.dk, p), pair(K.dk, p), inc[:, p % 2], ALU.mult)
                    nc.vector.tensor_tensor(pair(K.db, p), pair(K.db, p), inc[:, p % 2], ALU.mult).then_inc(scaled, 1)
    A.high = top


def rwkv_chunks_stage(nc, K, s):
    A = K.A
    lat = s == LAT
    top = A.high
    vt, bt, kt, lak, tt = (A.temp(2, 512) for _ in range(5))
    arb, ark = (A.temp(2, 512), A.temp(2, 512)) if lat else (None, None)
    inv, u, lt, ltm = A.temp(512), A.temp(512), A.temp(512), A.temp(2, 512)
    x, sa = A.temp(512), A.temp(512)
    if lat:
        K.y = A.temp(H, T)
    LEVELS = 5
    prep = [("v", "act"), ("b", "act"), ("k", "act"), ("l", "dve"), ("lt", "dve"), ("lak", "dve")]
    if lat:
        prep += [("arb", "dve"), ("ark", "dve")]
    for m in range(LEVELS):
        prep += [(f"u{m}", "act")] + ([(f"t{m}", "dve")] if m < LEVELS - 1 else []) + [(f"tt{m}", "dve")]
    NP = len(prep)
    index = {name: n for n, (name, _) in enumerate(prep)}

    def taken(step, name):
        n = index[name]
        who = prep[n][1]
        per = sum(w == who for _, w in prep)
        return who, step * per + sum(w == who for _, w in prep[:n + 1])

    heads = lambda ap: ap.rearrange("p (h e) -> p h e", e=HD)
    mask = lambda i: K.masks[:, i, :].unsqueeze(1).broadcast_to([P, H, C])
    NS = T // C

    with nc.cleanup_on_exit():
        made = K.sem(f"c{s}_step_made")
        took = {"act": K.sem(f"c{s}_act_took"), "dve": K.sem(f"c{s}_dve_took")}
        lt_masked, lt_kept = K.sem(f"c{s}_lt_masked"), K.sem(f"c{s}_lt_kept")
        x_made, x_taken, sa_made, sa_taken = (K.sem(f"c{s}_{n}") for n in ("x_made", "x_taken", "sa_made", "sa_taken"))
        y_made, y_taken, s_made, s_taken = (K.sem(f"c{s}_{n}") for n in ("y_made", "y_taken", "s_made", "s_taken"))
        dve_step = K.sem(f"c{s}_dve_step")
        with nc.Block() as block:
            @block.tensor
            def _(pe):
                def at(step, d):
                    c = step if d == 0 else NS - 1 - step
                    return slice(C * c, C * c + C)

                def each(bank, lhs, rhs, start=True, stop=True):
                    for h in range(H):
                        for d in range(2):
                            rows = slice(HD * d, HD * d + HD)
                            last = nc.tensor.matmul(K.ps[rows, bank, HD * h:HD * h + HD], lhs(rows, d, h),
                                                    rhs(rows, d, h), start=start, stop=stop, skip_group_check=True)
                    return last

                def await_taken(step, name):
                    who, n = taken(step, name)
                    pe.wait_ge(took[who], n)

                def prepare(i, name):
                    par = i % 2
                    n = NP * i + index[name]
                    if n >= 5:
                        await_taken((n - 5) // NP, prep[(n - 5) % NP][0])
                    channels = lambda t: lambda rows, d, h: t[rows, h, at(i, d)]
                    square = lambda t: lambda rows, d, h: t[rows, HD * h:HD * h + HD]
                    unit = lambda rows, d, h: K.ident[rows, rows]
                    if name in ("v", "b", "k"):
                        lhs, rhs = channels({"v": K.dv, "b": K.db, "k": K.dk}[name]), unit
                    elif name == "l":
                        lhs, rhs = channels(K.da), channels(K.db)
                    elif name in ("lt", "lak"):
                        lhs, rhs = channels(K.db if name == "lt" else K.dk), channels(K.da)
                    elif name in ("arb", "ark"):
                        lhs, rhs = channels(K.db if name == "arb" else K.dk), channels(K.dr)
                    else:
                        m = int(name[-1])
                        if name[0] == "u":
                            pe.wait_ge(lt_masked, LEVELS * i + m + 1)
                            await_taken(i, f"t{m - 1}" if m else "l")
                            lhs, rhs = square(ltm[:, m % 2]), square(inv)
                        else:
                            await_taken(i, f"u{m}")
                            await_taken(i, f"tt{m - 1}" if m else "lt")
                            if name[1] == "t":
                                lhs, rhs = square(u), square(tt[:, par])
                            else:
                                lhs, rhs = square(tt[:, par]), square(u)
                    each(n % 5, lhs, rhs).then_inc(made, 1)

                def recur(i):
                    par = i % 2
                    square = lambda t: lambda rows, d, h: t[rows, HD * h:HD * h + HD]
                    st = lambda rows, d, h: K.stateT[rows, h, :]
                    if i:
                        pe.wait_ge(s_taken, i)
                    await_taken(i, "lak")
                    await_taken(i, "v")
                    for h in range(H):
                        for d in range(2):
                            rows = slice(HD * d, HD * d + HD)
                            cols = slice(HD * h, HD * h + HD)
                            nc.tensor.matmul(K.ps[rows, 5, cols], K.da[rows, h, at(i, d)], K.stateT[rows, h, :],
                                             start=True, stop=False, skip_group_check=True)
                            last = nc.tensor.matmul(K.ps[rows, 5, cols], lak[rows, par, cols], vt[rows, par, cols],
                                                    start=False, stop=True, skip_group_check=True)
                    last.then_inc(x_made, 1)
                    yield
                    pe.wait_ge(x_taken, i + 1)
                    await_taken(i, f"tt{LEVELS - 1}")
                    each(5, square(tt[:, par]), square(x)).then_inc(sa_made, 1)
                    yield
                    pe.wait_ge(sa_taken, i + 1)
                    await_taken(i, "k")
                    for h in range(H):
                        for d in range(2):
                            rows = slice(HD * d, HD * d + HD)
                            cols = slice(HD * h, HD * h + HD)
                            nc.tensor.matmul(K.ps[rows, 7, cols], bt[rows, par, cols], sa[rows, cols],
                                             start=True, stop=False, skip_group_check=True)
                            last = nc.tensor.matmul(K.ps[rows, 7, cols], kt[rows, par, cols], vt[rows, par, cols],
                                                    start=False, stop=True, skip_group_check=True)
                    if not lat:
                        last.then_inc(s_made, 1)
                        return
                    await_taken(i, "ark")
                    if i:
                        pe.wait_ge(y_taken, i)
                    for h in range(H):
                        for d in range(2):
                            rows = slice(HD * d, HD * d + HD)
                            cols = slice(HD * h, HD * h + HD)
                            out = K.ps[rows, 6, cols]
                            nc.tensor.matmul(out, K.stateT[rows, h, :], K.dr[rows, h, at(i, d)],
                                             start=True, stop=False, skip_group_check=True)
                            nc.tensor.matmul(out, sa[rows, cols], arb[rows, par, cols],
                                             start=False, stop=False, skip_group_check=True)
                            last = nc.tensor.matmul(out, vt[rows, par, cols], ark[rows, par, cols],
                                                    start=False, stop=True, skip_group_check=True)
                    last.then_inc(y_made, 1)

                for name, _ in prep:
                    prepare(0, name)
                for i in range(NS):
                    rest = [name for name, _ in prep] if i + 1 < NS else []
                    for _ in recur(i):
                        for name in rest[:8]:
                            prepare(i + 1, name)
                        rest = rest[8:]
                    for name in rest:
                        prepare(i + 1, name)

            @block.scalar
            def _(act):
                def take(i, name):
                    n = NP * i + index[name]
                    act.wait_ge(made, n + 1)
                    if name[0] == "u":
                        dst = u
                    else:
                        dst = {"v": vt, "b": bt, "k": kt}[name][:, i % 2]
                        if i >= 2:
                            act.wait_ge(y_made if lat else s_made, i - 1)
                    nc.scalar.activation(dst, K.ps[:, n % 5, :], ACT.Copy).then_inc(took["act"], 1)

                def seq(i):
                    act.wait_ge(x_made, i + 1)
                    nc.scalar.activation(x, K.ps[:, 5, :], ACT.Copy).then_inc(x_taken, 1)
                    yield
                    act.wait_ge(sa_made, i + 1)
                    nc.scalar.activation(sa, K.ps[:, 5, :], ACT.Copy).then_inc(sa_taken, 1)
                    yield
                    if lat:
                        act.wait_ge(y_made, i + 1)
                        for d in range(2):
                            rows = slice(HD * d, HD * d + HD)
                            c = i if d == 0 else NS - 1 - i
                            last = nc.scalar.activation(K.y[rows, :, C * c:C * c + C], heads(K.ps[rows, 6, :]), ACT.Copy)
                        last.then_inc(y_taken, 1)

                for name, who in prep:
                    if who == "act":
                        take(0, name)
                for i in range(NS):
                    rest = [p for p in prep] if i + 1 < NS else []
                    steps = seq(i)
                    next(steps)
                    for name, who in rest[:8]:
                        if who == "act":
                            take(i + 1, name)
                    next(steps)
                    for name, who in rest[8:16]:
                        if who == "act":
                            take(i + 1, name)
                    for _ in steps:
                        pass
                    for name, who in rest[16:]:
                        if who == "act":
                            take(i + 1, name)

            @block.gpsimd
            def _(pool):
                for i in range(NS):
                    for m in range(LEVELS):
                        if m == 0:
                            pool.wait_ge(lt_kept, i + 1)
                        if m >= 2:
                            pool.wait_ge(made, NP * i + index[f"u{m - 2}"] + 1)
                        nc.gpsimd.tensor_tensor(heads(ltm[:, m % 2]), heads(lt), mask(m + 2),
                                                ALU.mult).then_inc(lt_masked, 1)

            @block.vector
            def _(dve):
                link = chain(dve, dve_step)
                total = [0]

                def take(i, name):
                    par = i % 2
                    n = NP * i + index[name]
                    dve.wait_ge(made, n + 1)
                    src = K.ps[:, n % 5, :]
                    if name in ("lak", "arb", "ark", "lt") and i >= 2:
                        dve.wait_ge(y_made if lat else s_made, i - 1)
                    if name == "l":
                        link(nc.vector.tensor_tensor(heads(inv), heads(src), mask(0), ALU.mult))
                        done = nc.vector.tensor_tensor(heads(inv), heads(inv), unit_matrices(), ALU.add)
                    elif name == "lt":
                        if i:
                            dve.wait_ge(lt_masked, LEVELS * i)
                        nc.vector.tensor_copy(lt, src).then_inc(lt_kept, 1)
                        link(nc.vector.tensor_tensor(heads(tt[:, par]), heads(src), mask(1), ALU.mult))
                        done = nc.vector.tensor_tensor(heads(tt[:, par]), heads(tt[:, par]), unit_matrices(), ALU.add)
                    elif name == "lak":
                        done = nc.vector.tensor_tensor(heads(lak[:, par]), heads(src), mask(7), ALU.mult)
                    elif name in ("arb", "ark"):
                        dst = (arb if name == "arb" else ark)[:, par]
                        done = nc.vector.tensor_tensor(heads(dst), heads(src), mask(8), ALU.mult)
                    elif name[1] == "t":
                        done = nc.vector.tensor_tensor(tt[:, par], tt[:, par], src, ALU.add)
                    else:
                        done = nc.vector.tensor_tensor(inv, inv, src, ALU.add)
                    done.then_inc(took["dve"], 1)
                    total[0] += 1
                    dve.wait_ge(took["dve"], total[0])

                def unit_matrices():
                    return K.fold.unsqueeze(1).broadcast_to([P, H, C])

                for name, who in prep:
                    if who == "dve":
                        take(0, name)
                for i in range(NS):
                    rest = [p for p in prep] if i + 1 < NS else []
                    for name, who in rest[:16]:
                        if who == "dve":
                            take(i + 1, name)
                    dve.wait_ge(y_made if lat else s_made, i + 1)
                    st = K.stateT
                    link(nc.vector.tensor_tensor(st, st, heads(K.ps[:, 7, :]), ALU.add))
                    nc.vector.tensor_tensor(st, st, K.tot[:, i, :].unsqueeze(2).broadcast_to([P, H, HD]),
                                            ALU.mult).then_inc(s_taken, 1)
                    dve.wait_ge(s_taken, i + 1)
                    for name, who in rest[16:]:
                        if who == "dve":
                            take(i + 1, name)
    if not lat:
        A.high = top
        A.low = K.dup_low


def rwkv_context(nc, K):
    rwkv_prepare_stage(nc, K, CTX)
    rwkv_chunks_stage(nc, K, CTX)


def rwkv_latent(nc, K):
    rwkv_prepare_stage(nc, K, LAT)
    K.A.high = K.A.t.shape[1]
    rwkv_chunks_stage(nc, K, LAT)


def rwkv_output(nc, K):
    A = K.A
    y, bonus = K.y, K.bonus
    A.low = K.dup_low
    g = A.keep(H, T)
    sq, root = A.keep(H, T), A.keep(H, T)
    per_head = lambda i: K.dup_vecs[:, i, :].unsqueeze(2).broadcast_to([P, H, T])
    part = lambda ap, n: ap[:, 2 * n:2 * n + 2, :]
    bank = lambda n: K.ps[:, n, :].rearrange("p (h t) -> p h t", t=T)
    with nc.cleanup_on_exit():
        mean_made, centred, squared, var_made, rooted, z_ready, folded, dve_step = (K.sem("o_" + n) for n in (
            "mean_made", "centred", "squared", "var_made", "rooted", "z_ready", "folded", "dve_step"))
        g_made, g_taken = K.sem("o_g_made"), K.sem("o_g_taken")
        with nc.Block() as block:
            @block.tensor
            def _(pe):
                for n in range(4):
                    nc.tensor.matmul(bank(n), K.head_ones, part(y, n), start=True, stop=True).then_inc(mean_made, 1)
                for n in range(4):
                    pe.wait_ge(squared, n + 1)
                    nc.tensor.matmul(bank(4 + n), K.head_ones, part(sq, n), start=True, stop=True).then_inc(var_made, 1)
                for n in range(4):
                    pe.wait_ge(centred, n + 1)
                    for j in range(2):
                        for d in range(2):
                            h = 2 * n + j
                            last = nc.tensor.matmul(K.ps[HD * d:HD * d + HD, n, T * j:T * j + T],
                                                    K.g2[:, d, HD * h:HD * h + HD], K.glT[:, d, :],
                                                    start=True, stop=True)
                    last.then_inc(g_made, 1)
                pe.wait_ge(g_taken, 4)
                for n in range(4):
                    pe.wait_ge(z_ready, n + 1)
                    for i in range(2):
                        last = nc.tensor.matmul(K.ps[HD * i:HD * i + HD, n, 0:T], K.fold, y[:, 2 * n + i, :],
                                                start=True, stop=True)
                    last.then_inc(folded, 1)

            @block.scalar
            def _(act):
                for n in range(4):
                    act.wait_ge(centred, n + 1)
                    nc.scalar.activation(part(sq, n), part(y, n), ACT.Square).then_inc(squared, 1)
                for n in range(4):
                    act.wait_ge(var_made, n + 1)
                    nc.scalar.activation(part(root, n), bank(4 + n), ACT.Sqrt, bias=K.gn_eps[:, 0:1],
                                         scale=1.0 / HD).then_inc(rooted, 1)
                for n in range(4):
                    act.wait_ge(g_made, n + 1)
                    nc.scalar.activation(part(g, n), bank(n), ACT.Copy).then_inc(g_taken, 1)
                for n in range(4):
                    act.wait_ge(folded, n + 1)
                    nc.scalar.activation(K.mixT[:, 4 + n, :], K.ps[:, n, 0:T], ACT.Copy)

            @block.vector
            def _(dve):
                link = chain(dve, dve_step)
                for n in range(4):
                    dve.wait_ge(mean_made, n + 1)
                    nc.vector.scalar_tensor_tensor(part(y, n), bank(n), -1.0 / HD, part(y, n), ALU.mult,
                                                   ALU.add).then_inc(centred, 1)
                dve.wait_ge(squared, 4)
                link(nc.vector.tensor_tensor(y, y, per_head(1), ALU.mult))
                link(nc.vector.tensor_tensor(bonus, bonus, per_head(2), ALU.add))
                for n in range(4):
                    dve.wait_ge(rooted, n + 1)
                    link(nc.vector.reciprocal(part(root, n), part(root, n)))
                    link(nc.vector.tensor_tensor(part(y, n), part(y, n), part(root, n), ALU.mult))
                    link(nc.vector.tensor_tensor(part(y, n), part(y, n), part(bonus, n), ALU.add))
                    dve.wait_ge(g_taken, n + 1)
                    nc.vector.tensor_tensor(part(y, n), part(y, n), part(g, n), ALU.mult).then_inc(z_ready, 1)
    A.low = K.rwkv_low
    A.high = A.t.shape[1]


def mixers_out(nc, K):
    A, W = K.A, K.W
    K.x = A.keep(TT, D)
    K.gt2 = A.keep(D)
    K.base = A.low
    K.h2 = A.keep(TT, D)
    top = A.high
    cT = A.temp(KT * 2)
    cond = A.temp(KT, P)
    brow = A.temp(4 * D)
    gains = A.temp(3, D)
    gt1, g2, sh2 = A.temp(D), A.temp(D), A.temp(D)
    mix, junk = A.temp(TT, D), A.temp(D)
    sums, ms, root = A.temp(6), A.temp(4), A.temp(4)
    with nc.cleanup_on_exit():
        small, silued, cond_ready = K.sem("small_landed"), K.sem("silued"), K.sem("cond_ready")
        made, took, mix_kept, dve_step = K.sem("made"), K.sem("took"), K.sem("mix_kept"), K.sem("dve_step")
        ms_ready, rooted, x_ready, squared = K.sem("ms_ready"), K.sem("rooted"), K.sem("x_ready"), K.sem("squared")
        kinds = ["mod"] * 2 + ["mix"] * 4 + ["mod"] * 6
        with nc.Block() as block:
            @block.sync
            def _(sp):
                sp.dma_start(cT, K.dram["cT"]).then_inc(small, 16)
                sp.dma_start(brow[0:1, :], K.dram["b_mod"][:, 2 * D:6 * D]).then_inc(small, 16)
                for n in range(3):
                    sp.dma_start(gains[:, n, :], K.dram["norm_gains"][n + 1, :].partition_broadcast(P)).then_inc(small, 16)
                sp.dma_start(K.x, K.dram["x"].rearrange("(t p) d -> p t d", p=P)).then_inc(small, 16)
                W.load_ahead(sp, 10)

            @block.tensor
            def _(pe):
                pe.wait_ge(small, 96)
                pe.wait_ge(cond_ready, 1)
                j = 0
                for n in range(10):
                    w = W.take(pe)
                    if kinds[j] == "mix":
                        for t in range(TT):
                            for k in range(KT):
                                last = nc.tensor.matmul(K.ps[:, j % 8, :], K.mixT[:, k, P * t:P * t + P], w[:, k, :],
                                                        start=(k == 0), stop=(k == KT - 1))
                                if n and t == 0 and k == 0:
                                    last.then_inc(W.used, 1)
                            last.then_inc(made, 1)
                            j += 1
                    else:
                        if j >= 8:
                            prior = kinds[:j - 7]
                            pe.wait_ge(took, prior.count("mod"))
                            if prior.count("mix"):
                                pe.wait_ge(mix_kept, prior.count("mix"))
                        for k in range(KT):
                            last = nc.tensor.matmul(K.ps[:, j % 8, :], cond[:, k, :], w[:, k, :],
                                                    start=(k == 0), stop=False)
                            if n and k == 0:
                                last.then_inc(W.used, 1)
                        at = 512 * (n if n < 2 else n - 2)
                        nc.tensor.matmul(K.ps[:, j % 8, :], K.ones[0:1, :], brow[0:1, at:at + 512],
                                         start=False, stop=True).then_inc(made, 1)
                        j += 1
                pe.wait_ge(made, len(kinds))
                nc.tensor.nop().then_inc(W.used, 1)

            @block.scalar
            def _(act):
                act.wait_ge(small, 96)
                nc.scalar.activation(cT, cT, ACT.Silu).then_inc(silued, 1)
                for m in range(4):
                    n, t = m // 2, m % 2
                    act.wait_ge(made, m + 3)
                    if m:
                        act.wait_ge(mix_kept, m)
                    nc.scalar.activation(junk[:, 0:512], K.ps[:, 2 + m, :], ACT.Square,
                                         accum_out=sums[:, 2 * t + n:2 * t + n + 1])
                    nc.scalar.activation(mix[:, t, 512 * n:512 * n + 512], K.ps[:, 2 + m, :], ACT.Copy).then_inc(mix_kept, 1)
                act.wait_ge(ms_ready, 1)
                nc.scalar.activation(root[:, 0:2], ms[:, 0:2], ACT.Sqrt).then_inc(rooted, 1)
                for t in range(TT):
                    act.wait_ge(x_ready, t + 1)
                    nc.scalar.activation(mix[:, t, :], K.x[:, t, :], ACT.Square,
                                         accum_out=sums[:, 4 + t:5 + t]).then_inc(squared, 1)
                act.wait_ge(ms_ready, 2)
                nc.scalar.activation(root[:, 2:4], ms[:, 2:4], ACT.Sqrt).then_inc(rooted, 1)

            @block.vector
            def _(dve):
                link = chain(dve, dve_step)
                dve.wait_ge(silued, 1)
                nc.vector.tensor_copy(cond, cT[:, KT:2 * KT].unsqueeze(2).broadcast_to([P, KT, P])).then_inc(cond_ready, 1)
                count = 0
                for n in range(8):
                    j = n if n < 2 else n + 4
                    half = slice(512 * (n % 2), 512 * (n % 2) + 512)
                    dve.wait_ge(made, j + 1)
                    bank = K.ps[:, j % 8, :]
                    if n < 2:
                        ins = nc.vector.tensor_tensor(gt1[:, half], bank, gains[:, 0, half], ALU.mult)
                    elif n < 4:
                        ins = nc.vector.tensor_copy(sh2[:, half], bank)
                    elif n < 6:
                        ins = nc.vector.scalar_tensor_tensor(g2[:, half], bank, 1.0, gains[:, 1, half], ALU.add, ALU.mult)
                    else:
                        ins = nc.vector.tensor_tensor(K.gt2[:, half], bank, gains[:, 2, half], ALU.mult)
                    count += 1
                    ins.then_inc(took, 1)
                dve.wait_ge(took, count)
                dve.wait_ge(mix_kept, 4)
                link(nc.vector.tensor_tensor(ms[:, 0:2], sums[:, 0:4:2], sums[:, 1:4:2], ALU.add))
                nc.vector.tensor_scalar(ms[:, 0:2], ms[:, 0:2], 1.0 / D, EPS, ALU.mult, ALU.add).then_inc(ms_ready, 1)
                dve.wait_ge(rooted, 1)
                link(nc.vector.reciprocal(root[:, 0:2], root[:, 0:2]))
                for t in range(TT):
                    link(nc.vector.scalar_tensor_tensor(mix[:, t, :], mix[:, t, :], root[:, t:t + 1], gt1,
                                                        ALU.mult, ALU.mult))
                    nc.vector.tensor_tensor(K.x[:, t, :], K.x[:, t, :], mix[:, t, :], ALU.add).then_inc(x_ready, 1)
                dve.wait_ge(squared, 2)
                nc.vector.tensor_scalar(ms[:, 2:4], sums[:, 4:6], 1.0 / D, EPS, ALU.mult, ALU.add).then_inc(ms_ready, 1)
                dve.wait_ge(rooted, 2)
                link(nc.vector.reciprocal(root[:, 2:4], root[:, 2:4]))
                for t in range(TT):
                    link(nc.vector.scalar_tensor_tensor(K.h2[:, t, :], K.x[:, t, :], root[:, 2 + t:3 + t], g2,
                                                        ALU.mult, ALU.mult))
                    link(nc.vector.tensor_tensor(K.h2[:, t, :], K.h2[:, t, :], sh2, ALU.add))
    A.high = top


def route(nc, K):
    A = K.A
    K.xsT = A.keep(KT, NE * CAP)
    K.scatter = A.keep(NE, T)
    top = A.high
    wr = A.temp(KT, NE)
    earlier = A.temp(TT, T)
    places = A.temp(CAP)
    h2T = A.temp(KT, T)
    aff, rank, tie = A.temp(TT, NE), A.temp(TT, NE), A.temp(TT, NE)
    affT = A.temp(T)
    all_aff = A.temp(NE * T)
    sel, weighted = A.temp(TT, NE * CAP), A.temp(TT, NE * CAP)
    spread = A.temp(2, 4, P)
    by_expert = all_aff.rearrange("p (e t) -> p e t", t=T)
    top8, total = A.temp(TT), A.temp(TT)
    junk, junk2 = A.temp(T), A.temp(T)
    rows = nc.dram_tensor("affinity_rows", (NE, T), F32).ap()
    with nc.cleanup_on_exit():
        rows_stored = K.sem("rows_stored")
        landed, t_made, t_kept = K.sem("landed"), K.sem("h2T_made"), K.sem("h2T_kept")
        logits, maxed, expd, aff_ready = K.sem("logits"), K.sem("maxed"), K.sem("expd"), K.sem("aff_ready")
        affT_made, affT_kept, spread_landed = K.sem("affT_made"), K.sem("affT_kept"), K.sem("affinities_landed")
        sel_ready, gathered, gather_kept = K.sem("sel_ready"), K.sem("gathered"), K.sem("gather_kept")
        wide_ready, wide_made, wide_kept, dve_step = (K.sem("wide_ready"), K.sem("wide_made"), K.sem("wide_kept"),
                                                      K.sem("dve_step"))
        with nc.Block() as block:
            @block.sync
            def _(sp):
                for dst, name in ((wr, "w_router"), (earlier, "earlier"), (places, "places")):
                    sp.dma_start(dst, K.dram[name]).then_inc(landed, 16)
                sp.wait_ge(affT_kept, 1)
                sp.dma_start(rows, affT[0:NE, :]).then_inc(rows_stored, 16)
                sp.wait_ge(rows_stored, 16)
                sp.dma_start(all_aff, rows.rearrange("e t -> (e t)").partition_broadcast(P)).then_inc(spread_landed, 16)

            @block.tensor
            def _(pe):
                for n in range(4):
                    t, q = n // 2, n % 2
                    for k in range(4):
                        c = P * (4 * q + k)
                        last = nc.tensor.transpose(K.ps[:, n, P * k:P * k + P], K.h2[:, t, c:c + P], K.ident)
                    last.then_inc(t_made, 1)
                pe.wait_ge(landed, 48)
                pe.wait_ge(t_kept, 4)
                for t in range(TT):
                    for k in range(KT):
                        last = nc.tensor.matmul(K.ps[:, 4, NE * t:NE * t + NE], h2T[:, k, P * t:P * t + P], wr[:, k, :],
                                                start=(k == 0), stop=(k == KT - 1))
                last.then_inc(logits, 1)
                pe.wait_ge(aff_ready, 1)
                for t in range(TT):
                    last = nc.tensor.transpose(K.ps[0:NE, 5, P * t:P * t + P], aff[:, t, :], K.ident)
                last.then_inc(affT_made, 1)
                pe.wait_ge(sel_ready, 2)
                for d in range(KT):
                    if d >= 4:
                        pe.wait_ge(gather_kept, d - 3)
                    for t in range(TT):
                        last = nc.tensor.matmul(K.ps[:, d % 4, :], K.h2[:, t, P * d:P * d + P], sel[:, t, :],
                                                start=(t == 0), stop=(t == 1))
                    last.then_inc(gathered, 1)
                for n in range(8):
                    if n >= 4:
                        pe.wait_ge(wide_kept, n - 3)
                    pe.wait_ge(wide_ready, n + 1)
                    for k in range(4):
                        last = nc.tensor.transpose(K.ps[:, 4 + n % 4, P * k:P * k + P], spread[:, n % 2, k, :], K.ident)
                    last.then_inc(wide_made, 1)

            @block.scalar
            def _(act):
                for n in range(4):
                    t, q = n // 2, n % 2
                    act.wait_ge(t_made, n + 1)
                    nc.scalar.activation(h2T[:, 4 * q:4 * q + 4, P * t:P * t + P],
                                         K.ps[:, n, :].rearrange("p (k t) -> p k t", t=P), ACT.Copy).then_inc(t_kept, 1)
                act.wait_ge(maxed, 1)
                for t in range(TT):
                    nc.scalar.activation(aff[:, t, :], K.ps[:, 4, NE * t:NE * t + NE], ACT.Exp, bias=top8[:, t:t + 1],
                                         accum_out=total[:, t:t + 1]).then_inc(expd, 1)
                act.wait_ge(affT_made, 1)
                nc.scalar.activation(affT[0:NE, :], K.ps[0:NE, 5, 0:T], ACT.Copy).then_inc(affT_kept, 1)
                for d in range(KT):
                    act.wait_ge(gathered, d + 1)
                    nc.scalar.activation(K.xsT[:, d, :], K.ps[:, d % 4, :], ACT.Copy).then_inc(gather_kept, 1)
                for n in range(8):
                    t, q = n // 4, n % 4
                    act.wait_ge(wide_made, n + 1)
                    nc.scalar.activation(K.scatter[:, 4 * q:4 * q + 4, P * t:P * t + P],
                                         K.ps[:, 4 + n % 4, :].rearrange("p (k t) -> p k t", t=P),
                                         ACT.Copy).then_inc(wide_kept, 1)

            @block.vector
            def _(dve):
                link = chain(dve, dve_step)
                dve.wait_ge(logits, 1)
                nc.vector.tensor_reduce(top8, K.ps[:, 4, 0:TT * NE].rearrange("p (t e) -> p t e", e=NE), AX, ALU.max,
                                        negate=True).then_inc(maxed, 1)
                dve.wait_ge(expd, 2)
                link(nc.vector.reciprocal(total, total))
                nc.vector.tensor_tensor(aff, aff, total.unsqueeze(2).broadcast_to([P, TT, NE]),
                                        ALU.mult).then_inc(aff_ready, 1)
                dve.wait_ge(aff_ready, 1)
                dve.wait_ge(spread_landed, 16)
                for t in range(TT):
                    for e in range(NE):
                        mine = aff[:, t, e:e + 1]
                        nc.vector.tensor_scalar(junk, by_expert[:, e, :], mine, 0.0, ALU.is_gt, ALU.add,
                                                accum_out=rank[:, t, e:e + 1])
                        link(nc.vector.scalar_tensor_tensor(junk2, by_expert[:, e, :], mine, earlier[:, t, :],
                                                            ALU.is_equal, ALU.mult, accum_out=tie[:, t, e:e + 1]))
                    link(nc.vector.tensor_tensor(rank[:, t, :], rank[:, t, :], tie[:, t, :], ALU.add))
                    nc.vector.tensor_tensor(sel[:, t, :].rearrange("p (e c) -> p e c", c=CAP),
                                            rank[:, t, :].unsqueeze(2).broadcast_to([P, NE, CAP]),
                                            places.unsqueeze(1).broadcast_to([P, NE, CAP]),
                                            ALU.is_equal).then_inc(sel_ready, 1)
                dve.wait_ge(sel_ready, 2)
                for t in range(TT):
                    link(nc.vector.tensor_tensor(weighted[:, t, :].rearrange("p (e c) -> p e c", c=CAP),
                                                 sel[:, t, :].rearrange("p (e c) -> p e c", c=CAP),
                                                 aff[:, t, :].unsqueeze(2).broadcast_to([P, NE, CAP]), ALU.mult))
                for n in range(8):
                    t, q = n // 4, n % 4
                    if n >= 2:
                        dve.wait_ge(wide_made, n - 1)
                    w = weighted[:, t, P * q:P * q + P].rearrange("p (e c) -> p e c", c=CAP)
                    nc.vector.tensor_copy(spread[:, n % 2].rearrange("p e (r c) -> p e r c", c=CAP),
                                          w.unsqueeze(2).broadcast_to([P, 4, 4, CAP])).then_inc(wide_ready, 1)
    A.high = top


def experts(nc, K):
    A, W = K.A, K.W
    top = A.high
    W.extra = A.temp(NX, SLOT)
    gu = A.temp(512)
    gate = A.temp(2, 4, CAP)
    hidT = A.temp(2, 4, CAP)
    parts = A.temp(2, 512)
    y, junk = K.h2, A.temp(512)
    sums, ms, root = A.temp(4), A.temp(2), A.temp(2)
    with nc.cleanup_on_exit():
        gu_made, gu_kept, gu_turned, gated, hid_ready = (K.sem(n) for n in (
            "gu_made", "gu_kept", "gu_turned", "gated", "hid_ready"))
        down_made, parts_kept, y_made, y_kept = K.sem("down_made"), K.sem("parts_kept"), K.sem("y_made"), K.sem("y_kept")
        ms_ready, rooted, dve_step = K.sem("ms_ready"), K.sem("rooted"), K.sem("dve_step")
        strip = lambda j: slice(CAP * j, CAP * j + CAP)
        with nc.Block() as block:
            @block.sync
            def _(sp):
                W.load_ahead(sp, 6 * NE)

            @block.tensor
            def _(pe):
                def scatter(e):
                    pe.wait_ge(parts_kept, e + 1)
                    for t in range(TT):
                        for n in range(2):
                            last = nc.tensor.matmul(K.ps[:, 2 * t + n, :], K.scatter[:, e, P * t:P * t + P],
                                                    parts[:, n, :], start=(e == 0), stop=(e == NE - 1))
                    last.then_inc(y_made, 1)

                for e in range(NE):
                    ws = [W.take(pe) for _ in range(4)]
                    if e:
                        pe.wait_ge(gu_kept, e)
                    for k in range(KT):
                        for j in range(4):
                            last = nc.tensor.matmul(K.ps[strip(j), 4, :], K.xsT[:, k, CAP * e:CAP * e + CAP],
                                                    ws[j][:, k, :], start=(k == 0), stop=(k == KT - 1),
                                                    skip_group_check=True)
                    last.then_inc(gu_made, 1)
                    if e:
                        scatter(e - 1)
                    pe.wait_ge(gu_kept, e + 1)
                    if e:
                        pe.wait_ge(hid_ready, e)
                    for c in range(4):
                        last = nc.tensor.transpose(K.ps[:, 5, P * c:P * c + P], gu[:, P * c:P * c + P], K.ident)
                        if c == 0:
                            last.then_inc(W.used, 4)
                    last.then_inc(gu_turned, 1)
                    wd = [W.take(pe) for _ in range(2)]
                    pe.wait_ge(hid_ready, e + 1)
                    if e:
                        pe.wait_ge(parts_kept, e)
                    for n in range(2):
                        for i in range(2):
                            for j in range(4):
                                k = 2 * j + i
                                last = nc.tensor.matmul(K.ps[strip(j), 6 + n, :], hidT[:, k // 4, k % 4, :],
                                                        wd[n][:, k, :], start=(i == 0), stop=(i == 1),
                                                        skip_group_check=True)
                    last.then_inc(down_made, 1)
                    pe.wait_ge(down_made, e + 1)
                    nc.tensor.nop().then_inc(W.used, 2)
                scatter(NE - 1)

            @block.scalar
            def _(act):
                for e in range(NE):
                    act.wait_ge(gu_turned, e + 1)
                    turned = K.ps[:, 5, :].rearrange("p (c j t) -> p j c t", j=4, t=CAP)
                    nc.scalar.activation(gate, turned[:, 0:2], ACT.Silu).then_inc(gated, 1)
                    act.wait_ge(down_made, e + 1)
                    if e:
                        act.wait_ge(y_made, e)
                    for n in range(2):
                        last = nc.scalar.activation(parts[:, n, :], K.ps[:, 6 + n, :], ACT.Copy)
                    last.then_inc(parts_kept, 1)
                act.wait_ge(y_made, NE)
                for m in range(4):
                    t, n = m // 2, m % 2
                    if m:
                        act.wait_ge(y_kept, m)
                    nc.scalar.activation(junk[:, 0:512], K.ps[:, m, :], ACT.Square, accum_out=sums[:, m:m + 1])
                    nc.scalar.activation(y[:, t, 512 * n:512 * n + 512], K.ps[:, m, :], ACT.Copy).then_inc(y_kept, 1)
                act.wait_ge(ms_ready, 1)
                nc.scalar.activation(root, ms, ACT.Sqrt).then_inc(rooted, 1)

            @block.vector
            def _(dve):
                link = chain(dve, dve_step)
                for e in range(NE):
                    dve.wait_ge(gu_made, e + 1)
                    if e:
                        dve.wait_ge(gu_turned, e)
                    nc.vector.tensor_copy(gu, K.ps[:, 4, :]).then_inc(gu_kept, 1)
                    dve.wait_ge(gated, e + 1)
                    if e:
                        dve.wait_ge(down_made, e)
                    turned = K.ps[:, 5, :].rearrange("p (c j t) -> p j c t", j=4, t=CAP)
                    nc.vector.tensor_tensor(hidT, gate, turned[:, 2:4], ALU.mult).then_inc(hid_ready, 1)
                dve.wait_ge(y_kept, 4)
                link(nc.vector.tensor_tensor(ms, sums[:, 0:4:2], sums[:, 1:4:2], ALU.add))
                nc.vector.tensor_scalar(ms, ms, 1.0 / D, EPS, ALU.mult, ALU.add).then_inc(ms_ready, 1)
                dve.wait_ge(rooted, 1)
                link(nc.vector.reciprocal(root, root))
                for t in range(TT):
                    link(nc.vector.scalar_tensor_tensor(y[:, t, :], y[:, t, :], root[:, t:t + 1], K.gt2,
                                                        ALU.mult, ALU.mult))
                    link(nc.vector.tensor_tensor(K.x[:, t, :], K.x[:, t, :], y[:, t, :], ALU.add))
    A.high = top
    A.low = K.base


def attention_inputs(nc, K, layer):
    A, W = K.A, K.W
    A.low = K.base
    K.zT = A.keep(16, T)
    K.ztok = A.keep(TT, 1280)
    K.zhigh = A.high
    top = A.high
    gain, h, hT = A.temp(D), A.temp(TT, D), A.temp(KT, T)
    sums, ms, root = A.temp(2), A.temp(2), A.temp(2)
    jobs = [(n // 4, "T", n % 4, T, K.zT[:, n, :]) for n in range(16)]
    for i, width in enumerate((512, 512, 256)):
        jobs += [(4 + i, "tok", t, width, K.ztok[:, t, 512 * i:512 * i + width]) for t in range(TT)]
    with nc.cleanup_on_exit():
        landed, squared, ms_ready, rooted, h_ready = (K.sem(n) for n in (
            "gain_landed", "squared", "ms_ready", "rooted", "h_ready"))
        t_made, t_kept, made, act_took, dve_took, dve_step = (K.sem(n) for n in (
            "t_made", "t_kept", "made", "act_took", "dve_took", "dve_step"))
        with nc.Block() as block:
            @block.sync
            def _(sp):
                sp.dma_start(gain, K.dram["norm_mix_2"][layer].partition_broadcast(P)).then_inc(landed, 16)
                W.load_ahead(sp, 7)

            @block.tensor
            def _(pe):
                for n in range(4):
                    t, q = n // 2, n % 2
                    pe.wait_ge(h_ready, t + 1)
                    for k in range(4):
                        c = P * (4 * q + k)
                        last = nc.tensor.transpose(K.ps[:, n, P * k:P * k + P], h[:, t, c:c + P], K.ident)
                    last.then_inc(t_made, 1)
                pe.wait_ge(t_kept, 4)
                for n, (s, kind, b, width, dst) in enumerate(jobs):
                    if n == 0 or jobs[n - 1][0] != s:
                        w = W.take(pe)
                    if n >= 8:
                        pe.wait_ge(dve_took if n % 2 else act_took, (n - 8) // 2 + 1)
                    for k in range(KT):
                        if kind == "T":
                            last = nc.tensor.matmul(K.ps[:, n % 8, 0:T], w[:, k, P * b:P * b + P], hT[:, k, :],
                                                    start=(k == 0), stop=(k == KT - 1))
                        else:
                            last = nc.tensor.matmul(K.ps[:, n % 8, 0:width], hT[:, k, P * b:P * b + P],
                                                    w[:, k, 0:width], start=(k == 0), stop=(k == KT - 1))
                        if k == 0 and n and jobs[n - 1][0] != s:
                            last.then_inc(W.used, 1)
                    last.then_inc(made, 1)
                pe.wait_ge(made, len(jobs))
                nc.tensor.nop().then_inc(W.used, 1)

            @block.scalar
            def _(act):
                for t in range(TT):
                    nc.scalar.activation(h[:, t, :], K.x[:, t, :], ACT.Square, accum_out=sums[:, t:t + 1]).then_inc(squared, 1)
                act.wait_ge(ms_ready, 1)
                nc.scalar.activation(root, ms, ACT.Sqrt).then_inc(rooted, 1)
                for n in range(4):
                    t, q = n // 2, n % 2
                    act.wait_ge(t_made, n + 1)
                    nc.scalar.activation(hT[:, 4 * q:4 * q + 4, P * t:P * t + P],
                                         K.ps[:, n, :].rearrange("p (k t) -> p k t", t=P), ACT.Copy).then_inc(t_kept, 1)
                for n, (s, kind, b, width, dst) in enumerate(jobs):
                    if n % 2 == 0:
                        act.wait_ge(made, n + 1)
                        nc.scalar.activation(dst, K.ps[:, n % 8, 0:width], ACT.Copy).then_inc(act_took, 1)

            @block.vector
            def _(dve):
                link = chain(dve, dve_step)
                dve.wait_ge(squared, 2)
                nc.vector.tensor_scalar(ms, sums, 1.0 / D, EPS, ALU.mult, ALU.add).then_inc(ms_ready, 1)
                dve.wait_ge(rooted, 1)
                link(nc.vector.reciprocal(root, root))
                dve.wait_ge(landed, 16)
                for t in range(TT):
                    nc.vector.scalar_tensor_tensor(h[:, t, :], K.x[:, t, :], root[:, t:t + 1], gain,
                                                   ALU.mult, ALU.mult).then_inc(h_ready, 1)
                for n, (s, kind, b, width, dst) in enumerate(jobs):
                    if n % 2:
                        dve.wait_ge(made, n + 1)
                        nc.vector.tensor_copy(dst, K.ps[:, n % 8, 0:width]).then_inc(dve_took, 1)
    A.high = top


def mixer_preparation(nc, K, layer):
    A = K.A
    zT, ztok = K.zT, K.ztok
    K.qrot = A.keep(2, T)
    K.mq = A.keep(2, 2, T)
    K.kcT = A.keep(16)
    K.vc = A.keep(HD)
    K.gates = A.keep(TT, 12)
    K.fsum = A.keep(TT, 4)
    K.igate = A.keep(TT, 4)
    K.nlam = A.keep(1)
    K.sub_g = A.keep(HD)
    K.head_g = A.keep(256)
    top = A.high
    cos64, sin64, cos32, sin32 = (A.temp(T) for _ in range(4))
    swap64, swap32, tri = A.temp(P), A.temp(P), A.temp(P)
    turned = A.temp(2, 512)
    cmp_w, pos = A.temp(2, 32, HD), A.temp(2, 32)
    blocks = A.temp(2, 32, 15)
    conv, wqk = A.temp(2, 5), A.temp(2, 2, HD)
    uc = A.temp(2, T)
    gate_b, lam = A.temp(8), A.temp(P)
    f, fa, lam2 = A.temp(TT, 4), A.temp(TT, 4), A.temp(HD)
    lsum = A.temp(2)
    lam_init = 0.8 - 0.6 * float(np.exp(-0.3 * layer))
    turns = [(zT[:, 0:2, :], K.qrot, swap64, cos64, sin64), (zT[:, 4:6, :], zT[:, 4:6, :], swap64, cos64, sin64),
             (zT[:, 12:14, :], zT[:, 12:14, :], swap64, cos64, sin64), (zT[:, 14:16, :], zT[:, 14:16, :], swap64, cos64, sin64),
             (zT[:, 6:8, :], zT[:, 6:8, :], swap32, cos32, sin32), (zT[:, 8:10, :], zT[:, 8:10, :], swap32, cos32, sin32)]
    dram = K.dram
    tables = [(cos64, dram["cos64"]), (sin64, dram["sin64"]), (cos32, dram["cos32"]), (sin32, dram["sin32"]),
              (swap64, dram["swap64"]), (swap32, dram["swap32"]), (tri, dram["tri"])]
    params = [(cmp_w, dram["nsa_cmp_w_2"][layer]), (pos, dram["nsa_cmp_pos_2"][layer]), (conv, dram["mlstm_conv_2"][layer]),
              (wqk, dram["mlstm_wqk_2"][layer]), (gate_b, dram["mlstm_gate_b_2"][layer].partition_broadcast(P)),
              (lam, dram["diff_lambda_2"][layer].partition_broadcast(P)),
              (K.sub_g, dram["diff_norm_2"][layer].partition_broadcast(P)),
              (K.head_g, dram["mlstm_norm_2"][layer].partition_broadcast(P))]
    with nc.cleanup_on_exit():
        tables_in, params_in, swapped, rotated = (K.sem(n) for n in ("tables_in", "params_in", "swapped", "rotated"))
        blocks_ready, compressed, cmp_kept = K.sem("blocks_ready"), K.sem("compressed"), K.sem("cmp_kept")
        uc_conv, uc_ready, mqk_made = K.sem("uc_conv"), K.sem("uc_ready"), K.sem("mqk_made")
        f_abs, f_exp, f_ln, lf_ready, f_made, act_step, dve_step = (K.sem(n) for n in (
            "f_abs", "f_exp", "f_ln", "lf_ready", "f_made", "act_step", "dve_step"))
        lam_ready, lam_exp = K.sem("lam_ready"), K.sem("lam_exp")
        with nc.Block() as block:
            @block.sync
            def _(sp):
                for dst, src in tables:
                    sp.dma_start(dst, src).then_inc(tables_in, 16)
                for dst, src in params:
                    sp.dma_start(dst, src).then_inc(params_in, 16)

            @block.tensor
            def _(pe):
                pe.wait_ge(tables_in, 16 * len(tables))
                for n in range(4):
                    nc.tensor.matmul(K.ps[:, n, :], turns[n][2], turns[n][0], start=True, stop=True).then_inc(swapped, 1)
                pe.wait_ge(params_in, 16 * len(params))
                pe.wait_ge(blocks_ready, 1)
                for i in range(2):
                    rows = slice(HD * i, HD * i + HD)
                    for l in range(32):
                        nc.tensor.matmul(K.ps[rows, 4, 0:15], cmp_w[rows, 0, l, :], blocks[rows, 0, l, :],
                                         start=(l == 0), stop=(l == 31))
                for l in range(32):
                    last = nc.tensor.matmul(K.ps[0:15, 5, 0:HD], blocks[0:HD, 1, l, :], cmp_w[0:HD, 1, l, :],
                                            start=(l == 0), stop=(l == 31))
                last.then_inc(compressed, 1)
                for n in range(4, 6):
                    pe.wait_ge(rotated, n - 3)
                    nc.tensor.matmul(K.ps[:, n % 4, :], turns[n][2], turns[n][0], start=True, stop=True).then_inc(swapped, 1)
                pe.wait_ge(uc_ready, 1)
                for i in range(2):
                    for b in range(2):
                        for j in range(2):
                            rows = slice(HD * j, HD * j + HD)
                            last = nc.tensor.matmul(K.ps[rows, 6 + i, T * b:T * b + T], wqk[rows, i, b, :], uc[rows, b, :],
                                                    start=True, stop=True)
                last.then_inc(mqk_made, 1)
                pe.wait_ge(lf_ready, 1)
                pe.wait_ge(cmp_kept, 1)
                nc.tensor.matmul(K.ps[:, 4, 0:4], tri, f[:, 0, :], start=True, stop=True)
                nc.tensor.matmul(K.ps[:, 4, 4:8], K.ones, f[:, 0, :], start=True, stop=False)
                nc.tensor.matmul(K.ps[:, 4, 4:8], tri, f[:, 1, :], start=False, stop=True).then_inc(f_made, 1)

            @block.scalar
            def _(act):
                act.wait_ge(uc_conv, 1)
                nc.scalar.activation(uc, uc, ACT.Silu).then_inc(uc_ready, 1)
                nc.scalar.activation(K.gates, ztok[:, :, 128:140], ACT.Sigmoid)
                nc.scalar.activation(ztok[:, :, 768:1024], ztok[:, :, 768:1024], ACT.Sigmoid)
                act.wait_ge(compressed, 1)
                nc.scalar.activation(K.kcT[:, 0:15], K.ps[:, 4, 0:15], ACT.Copy)
                nc.scalar.activation(K.vc[0:15, :], K.ps[0:15, 5, 0:HD], ACT.Copy).then_inc(cmp_kept, 1)
                act.wait_ge(mqk_made, 1)
                nc.scalar.activation(K.mq[:, 0], K.ps[:, 6, :].rearrange("p (b t) -> p b t", t=T), ACT.Copy)
                nc.scalar.activation(K.mq[:, 1], K.ps[:, 7, :].rearrange("p (b t) -> p b t", t=T), ACT.Copy,
                                     scale=HD ** -0.5)
                act.wait_ge(f_abs, 1)
                nc.scalar.activation(fa, fa, ACT.Exp, scale=-1.0).then_inc(f_exp, 1)
                act.wait_ge(lam_ready, 1)
                nc.scalar.activation(lsum, lsum, ACT.Exp).then_inc(lam_exp, 1)
                act.wait_ge(f_exp, 1)
                nc.scalar.activation(fa, fa, ACT.Ln, bias=K.ones[:, 0:1]).then_inc(f_ln, 1)

            @block.vector
            def _(dve):
                link = chain(dve, dve_step)

                def rotate(n):
                    src, dst, _, cos, sin = turns[n]
                    wide = [P, 2, T]
                    dve.wait_ge(swapped, n + 1)
                    t = turned[:, n % 2, :].rearrange("p (b t) -> p b t", b=2)
                    link(nc.vector.tensor_tensor(t, K.ps[:, n % 4, :].rearrange("p (b t) -> p b t", b=2),
                                                 sin.unsqueeze(1).broadcast_to(wide), ALU.mult))
                    link(nc.vector.tensor_tensor(dst, src, cos.unsqueeze(1).broadcast_to(wide), ALU.mult))
                    nc.vector.tensor_tensor(dst, dst, t, ALU.add).then_inc(rotated, 1)

                dve.wait_ge(params_in, 16 * len(params))
                for i in range(2):
                    for half in range(2):
                        view = zT[:, 2 + i, 16 * half:16 * half + 240].rearrange("p (n l) -> p l n", l=16)
                        last = nc.vector.tensor_tensor(blocks[:, i, 16 * half:16 * half + 16, :], view,
                                                       pos[:, i, 16 * half:16 * half + 16].unsqueeze(2)
                                                       .broadcast_to([P, 16, 15]), ALU.add)
                last.then_inc(blocks_ready, 1)
                for b in range(2):
                    u, o = zT[:, 10 + b, :], uc[:, b, :]
                    link(nc.vector.tensor_scalar(o, u, conv[:, b, 3:4], conv[:, b, 4:5], ALU.mult, ALU.add))
                    for tap in range(3):
                        by = 3 - tap
                        ins = nc.vector.scalar_tensor_tensor(o[:, by:T], u[:, 0:T - by], conv[:, b, tap:tap + 1],
                                                             o[:, by:T], ALU.mult, ALU.add)
                        if b == 1 and tap == 2:
                            ins.then_inc(uc_conv, 1)
                        else:
                            link(ins)
                for n in range(4):
                    rotate(n)
                per_tile = lambda at: gate_b[:, at:at + 4].unsqueeze(1).broadcast_to([P, TT, 4])
                link(nc.vector.tensor_tensor(f, ztok[:, :, 144:148], per_tile(4), ALU.add))
                link(nc.vector.tensor_tensor(K.igate, ztok[:, :, 140:144], per_tile(0), ALU.add))
                link(nc.vector.tensor_scalar(fa, f, -1.0, None, ALU.mult))
                nc.vector.tensor_tensor(fa, fa, f, ALU.max).then_inc(f_abs, 1)
                for i in range(2):
                    link(nc.vector.tensor_tensor(lam2[:, 32 * i:32 * i + 32], lam[:, 64 * i:64 * i + 32],
                                                 lam[:, 64 * i + 32:64 * i + 64], ALU.mult))
                nc.vector.tensor_reduce(lsum, lam2.rearrange("p (i d) -> p i d", i=2), AX, ALU.add).then_inc(lam_ready, 1)
                link(nc.vector.tensor_scalar(f, f, 0.0, None, ALU.min))
                dve.wait_ge(f_ln, 1)
                nc.vector.tensor_tensor(f, f, fa, ALU.subtract).then_inc(lf_ready, 1)
                dve.wait_ge(lam_exp, 1)
                link(nc.vector.tensor_tensor(K.nlam, lsum[:, 1:2], lsum[:, 0:1], ALU.subtract))
                link(nc.vector.tensor_scalar(K.nlam, K.nlam, -lam_init, None, ALU.add))
                for n in range(4, 6):
                    rotate(n)
                dve.wait_ge(f_made, 1)
                link(nc.vector.tensor_copy(K.fsum, K.ps[:, 4, 0:8].rearrange("p (t h) -> p t h", h=4)))
                link(nc.vector.tensor_tensor(K.igate, K.igate, K.fsum, ALU.subtract))
    A.high = top


def attention(nc, K, layer):
    A = K.A
    zT, ztok = K.zT, K.ztok
    K.o = A.keep(TT, D)
    K.den = A.keep(TT, 4)
    K.em = A.keep(TT, 4)
    top = A.high
    bias = A.temp(2, TT, T)
    cmp_bias, cmp_on = A.temp(TT, 16), A.temp(TT, 16)
    scores = A.temp(2, 8, T)
    probsT = A.temp(2, 8, P)
    nmax, z, coef = A.temp(2, 8), A.temp(2, 8), A.temp(2, 4)
    tmp, negm = A.temp(256), A.temp(2, 4)
    units = [(kind, t) for kind in ("cmp", "slc", "win", "dil", "diff", "mlstm") for t in range(TT)]
    NU = len(units)
    heads_of = {"cmp": 4, "slc": 4, "win": 4, "dil": 4, "diff": 8, "mlstm": 4}
    wide = lambda u: units[u][0] in ("diff", "mlstm")
    base = lambda u: 0 if wide(u) else 2 * (u % 2)
    keys = lambda u: 16 if units[u][0] == "cmp" else P * (units[u][1] + 1)
    scale = {"cmp": HD ** -0.5, "slc": HD ** -0.5, "win": HD ** -0.5, "dil": HD ** -0.5, "diff": 32 ** -0.5}
    order = [0, 2, 1, 3]
    col = {"cmp": 0, "slc": 0, "win": 0, "diff": 256, "mlstm": 512, "dil": 768}

    with nc.cleanup_on_exit():
        masks_in, scored, scores_read, maxed, expd, p_ready = (K.sem(n) for n in (
            "masks_in", "scored", "scores_read", "maxed", "expd", "p_ready"))
        turned, pt_kept, pv_made, o_taken, dve_step, negm_ready = (K.sem(n) for n in (
            "turned", "pt_kept", "pv_made", "o_taken", "dve_step", "negm_ready"))
        with nc.Block() as block:
            @block.sync
            def _(sp):
                for dst, name in ((bias, "attn_bias"), (cmp_bias, "cmp_bias"), (cmp_on, "cmp_on")):
                    sp.dma_start(dst, K.dram[name]).then_inc(masks_in, 16)

            @block.tensor
            def _(pe):
                def score(u):
                    kind, t = units[u]
                    n = keys(u)
                    if u and (wide(u) or wide(u - 1)):
                        pe.wait_ge(scores_read, u)
                    elif u >= 2:
                        pe.wait_ge(scores_read, u - 1)
                    q = slice(P * t, P * t + P)
                    if kind == "diff":
                        for b in range(2):
                            for s in range(4):
                                rows = slice(32 * s, 32 * s + 32)
                                last = nc.tensor.matmul(K.ps[:, s, T * b:T * b + n], zT[rows, 6 + b, q], zT[rows, 8 + b, 0:n],
                                                        start=True, stop=True, tile_position=(32 * s, 0))
                    else:
                        for h in range(4):
                            rows = slice(HD * (h % 2), HD * (h % 2) + HD)
                            b = h // 2
                            lhs, rhs = {"cmp": lambda: (zT[rows, b, q], K.kcT[rows, 0:15]),
                                        "slc": lambda: (K.qrot[rows, b, q], zT[rows, 4, 0:n]),
                                        "win": lambda: (K.qrot[rows, b, q], zT[rows, 5, 0:n]),
                                        "dil": lambda: (zT[rows, 12 + b, q], zT[rows, 14 + b, 0:n]),
                                        "mlstm": lambda: (K.mq[rows, 0, b, q], K.mq[rows, 1, b, 0:n])}[kind]()
                            wid = 15 if kind == "cmp" else n
                            last = nc.tensor.matmul(K.ps[:, base(u) + h % 2, T * b:T * b + wid], lhs, rhs,
                                                    start=True, stop=True)
                    if kind == "mlstm":
                        for h in range(4):
                            for k in range(t + 1):
                                at = T * (h // 2) + P * k
                                last = nc.tensor.matmul(K.ps[:, 2 + h % 2, at:at + P],
                                                        K.igate[:, k, h:h + 1].broadcast_to([P, P]), K.ident,
                                                        start=True, stop=True)
                    last.then_inc(scored, 1)

                def turn(u):
                    kind, t = units[u]
                    pe.wait_ge(p_ready, u + 1)
                    if u:
                        pe.wait_ge(pt_kept, u)
                    for j in range(4):
                        if kind == "cmp":
                            last = nc.tensor.transpose(K.ps[0:16, 4, P * j:P * j + P], scores[:, u % 2, j, 0:16], K.ident)
                        else:
                            for k in range(t + 1):
                                n = (t + 1) * j + k
                                last = nc.tensor.transpose(K.ps[:, 4 + n // 4, P * (n % 4):P * (n % 4) + P],
                                                           scores[:, u % 2, j, P * k:P * k + P], K.ident)
                    last.then_inc(turned, 1)

                def values(u):
                    kind, t = units[u]
                    pe.wait_ge(pt_kept, u + 1)
                    if u >= 2:
                        pe.wait_ge(o_taken, u - 1)
                    bank = 6 + u % 2
                    for j in range(4):
                        h = order[j]
                        out = K.ps[:, bank, HD * h:HD * h + HD]
                        if kind == "cmp":
                            last = nc.tensor.matmul(out, probsT[0:15, u % 2, j, :], K.vc[0:15, :], start=True, stop=True)
                            continue
                        for k in range(t + 1):
                            v = {"slc": lambda: ztok[:, k, 0:64], "win": lambda: ztok[:, k, 64:128],
                                 "diff": lambda: ztok[:, k, 256 + HD * h:256 + HD * h + HD],
                                 "mlstm": lambda: ztok[:, k, 512 + HD * h:512 + HD * h + HD],
                                 "dil": lambda: ztok[:, k, 1024 + HD * h:1024 + HD * h + HD]}[kind]()
                            last = nc.tensor.matmul(out, probsT[:, u % 2, (t + 1) * j + k, :], v,
                                                    start=(k == 0), stop=(k == t))
                    last.then_inc(pv_made, 1)

                score(0)
                for u in range(NU):
                    if u + 1 < NU:
                        score(u + 1)
                    turn(u)
                    values(u)

            @block.scalar
            def _(act):
                def exps(u):
                    kind, t = units[u]
                    n = keys(u)
                    act.wait_ge(maxed, u + 1)
                    for j in range(heads_of[kind]):
                        s = scores[:, u % 2, j, 0:n]
                        if kind in ("cmp", "mlstm"):
                            last = nc.scalar.activation(s, s, ACT.Exp, bias=nmax[:, u % 2, j:j + 1])
                        else:
                            last = nc.scalar.activation(s, s, ACT.Exp, bias=nmax[:, u % 2, j:j + 1],
                                                        accum_out=z[:, u % 2, j:j + 1])
                    if kind == "mlstm":
                        last = nc.scalar.activation(K.em[:, t, :], negm[:, t, :], ACT.Exp)
                    last.then_inc(expd, 1)

                def keep(u):
                    kind, t = units[u]
                    act.wait_ge(turned, u + 1)
                    if u >= 2:
                        act.wait_ge(pv_made, u - 1)
                    if kind == "cmp":
                        last = nc.scalar.activation(probsT[0:16, u % 2, 0:4, :], K.ps[0:16, 4, :]
                                                    .rearrange("p (n q) -> p n q", q=P), ACT.Copy)
                    else:
                        for i in range(t + 1):
                            last = nc.scalar.activation(probsT[:, u % 2, 4 * i:4 * i + 4, :], K.ps[:, 4 + i, :]
                                                        .rearrange("p (n q) -> p n q", q=P), ACT.Copy)
                    last.then_inc(pt_kept, 1)

                exps(0)
                for u in range(NU):
                    if u + 1 < NU:
                        exps(u + 1)
                    keep(u)

            @block.vector
            def _(dve):
                link = chain(dve, dve_step)

                def maxima(u):
                    kind, t = units[u]
                    n, nh = keys(u), heads_of[kind]
                    dve.wait_ge(scored, u + 1)
                    if u >= 2:
                        dve.wait_ge(turned, u - 1)
                    s = scores[:, u % 2, 0:nh, 0:n]
                    if kind == "mlstm":
                        src = K.ps[:, 2:4, :].rearrange("p a (b t) -> p (a b) t", t=T)
                        link(nc.vector.scalar_tensor_tensor(s, src[:, :, 0:n], 1.0, bias[:, 0, t, 0:n].unsqueeze(1)
                                                            .broadcast_to([P, 4, n]), ALU.mult, ALU.add))
                        link(nc.vector.tensor_reduce(nmax[:, u % 2, 0:4], s, AX, ALU.max, negate=True))
                        link(nc.vector.tensor_scalar(nmax[:, u % 2, 0:4], nmax[:, u % 2, 0:4], 0.0, None, ALU.min))
                        by_head = nmax[:, u % 2, 0:4].rearrange("p (a b) -> p b a", a=2)
                        nc.vector.tensor_tensor(negm[:, t, :].rearrange("p (b a) -> p b a", a=2), by_head,
                                                K.fsum[:, t, :].rearrange("p (b a) -> p b a", a=2),
                                                ALU.subtract).then_inc(maxed, 1)
                        return
                    a = base(u)
                    src = K.ps[:, a:a + nh // 2, :].rearrange("p a (b t) -> p (a b) t", t=T)
                    if kind == "cmp":
                        link(nc.vector.memset(s[:, :, 15:16], NEG))
                        s, src, m = s[:, :, 0:15], src[:, :, 0:15], cmp_bias[:, t, 0:15]
                        n = 15
                    else:
                        src, m = src[:, :, 0:n], bias[:, 1 if kind == "dil" else 0, t, 0:n]
                    nc.vector.scalar_tensor_tensor(s, src, scale[kind], m.unsqueeze(1).broadcast_to([P, nh, n]),
                                                   ALU.mult, ALU.add).then_inc(scores_read, 1)
                    dve.wait_ge(scores_read, u + 1)
                    nc.vector.tensor_reduce(nmax[:, u % 2, 0:nh], s, AX, ALU.max, negate=True).then_inc(maxed, 1)

                def weigh(u):
                    kind, t = units[u]
                    n = keys(u)
                    dve.wait_ge(expd, u + 1)
                    s = scores[:, u % 2]
                    if kind == "cmp":
                        link(nc.vector.tensor_tensor(s[:, 0:4, 0:16], s[:, 0:4, 0:16], cmp_on[:, t, :].unsqueeze(1)
                                                     .broadcast_to([P, 4, 16]), ALU.mult))
                        link(nc.vector.tensor_reduce(z[:, u % 2, 0:4], s[:, 0:4, 0:16], AX, ALU.add))
                        nc.vector.tensor_scalar(z[:, u % 2, 0:4], z[:, u % 2, 0:4], 1e-30, None,
                                                ALU.max).then_inc(p_ready, 1)
                        dve.wait_ge(p_ready, u + 1)
                    elif kind == "diff":
                        zz = z[:, u % 2]
                        link(nc.vector.reciprocal(zz, zz))
                        for i in range(2):
                            at = 2 * (2 * i + 1)
                            link(nc.vector.tensor_scalar(zz[:, at:at + 2], zz[:, at:at + 2], K.nlam[:, 0:1], None, ALU.mult))
                        for i in range(2):
                            for b in range(2):
                                p0, p1 = 4 * i + b, 4 * i + 2 + b
                                link(nc.vector.tensor_scalar(s[:, p1, 0:n], s[:, p1, 0:n], zz[:, p1:p1 + 1], None, ALU.mult))
                                ins = nc.vector.scalar_tensor_tensor(s[:, 2 * i + b, 0:n], s[:, p0, 0:n], zz[:, p0:p0 + 1],
                                                                     s[:, p1, 0:n], ALU.mult, ALU.add)
                                if i == 1 and b == 1:
                                    ins.then_inc(p_ready, 1)
                                    dve.wait_ge(p_ready, u + 1)
                                else:
                                    link(ins)
                    elif kind == "mlstm":
                        qk = K.ps[:, 0:2, :].rearrange("p a (b t) -> p (a b) t", t=T)
                        nc.vector.tensor_tensor(s[:, 0:4, 0:n], s[:, 0:4, 0:n], qk[:, :, 0:n], ALU.mult).then_inc(scores_read, 1)
                        dve.wait_ge(scores_read, u + 1)
                        by_head = K.den[:, t, :].rearrange("p (b a) -> p a b", a=2)
                        nc.vector.tensor_reduce(by_head, s[:, 0:4, 0:n].rearrange("p (a b) t -> p a b t", a=2), AX,
                                                ALU.add).then_inc(p_ready, 1)
                        dve.wait_ge(p_ready, u + 1)
                    else:
                        link(nc.vector.reciprocal(z[:, u % 2, 0:4], z[:, u % 2, 0:4]))
                        nc.vector.tensor_copy(coef[:, u % 2, :].rearrange("p (b a) -> p a b", a=2),
                                              z[:, u % 2, 0:4].rearrange("p (a b) -> p a b", a=2)).then_inc(p_ready, 1)
                        dve.wait_ge(p_ready, u + 1)

                def output(u):
                    kind, t = units[u]
                    c = coef[:, u % 2, :]
                    if kind == "cmp":
                        link(nc.vector.reciprocal(z[:, u % 2, 0:4], z[:, u % 2, 0:4]))
                        link(nc.vector.tensor_copy(c.rearrange("p (b a) -> p a b", a=2),
                                                   z[:, u % 2, 0:4].rearrange("p (a b) -> p a b", a=2)))
                    if kind in ("cmp", "slc", "win"):
                        g = {"cmp": 0, "slc": 4, "win": 8}[kind]
                        link(nc.vector.tensor_tensor(c, c, K.gates[:, t, g:g + 4], ALU.mult))
                    dve.wait_ge(pv_made, u + 1)
                    dst = K.o[:, t, col[kind]:col[kind] + 256].rearrange("p (h e) -> p h e", e=HD)
                    src = K.ps[:, 6 + u % 2, 0:256].rearrange("p (h e) -> p h e", e=HD)
                    if kind in ("diff", "mlstm"):
                        nc.vector.tensor_copy(dst, src).then_inc(o_taken, 1)
                        return
                    by = c.unsqueeze(2).broadcast_to([P, 4, HD])
                    if kind in ("slc", "win"):
                        part = tmp.rearrange("p (h e) -> p h e", e=HD)
                        nc.vector.tensor_tensor(part, src, by, ALU.mult).then_inc(o_taken, 1)
                        dve.wait_ge(o_taken, u + 1)
                        link(nc.vector.tensor_tensor(dst, dst, part, ALU.add))
                    else:
                        nc.vector.tensor_tensor(dst, src, by, ALU.mult).then_inc(o_taken, 1)
                        dve.wait_ge(o_taken, u + 1)

                dve.wait_ge(masks_in, 48)
                maxima(0)
                for u in range(NU):
                    weigh(u)
                    if u + 1 < NU:
                        maxima(u + 1)
                    output(u)
    A.high = top


def attention_out(nc, K, layer):
    A, W = K.A, K.W
    top = A.high
    sq, den = A.temp(TT, 512), A.temp(TT, 4)
    ss, root = A.temp(TT, 8), A.temp(TT, 8)
    lam_init = 0.8 - 0.6 * float(np.exp(-0.3 * layer))
    ztok, o = K.ztok, K.o
    with nc.cleanup_on_exit():
        ms_ready, rooted, o_ready, t_made, t_kept, made, dve_step = (K.sem(n) for n in (
            "ms_ready", "rooted", "o_ready", "t_made", "t_kept", "made", "dve_step"))
        with nc.Block() as block:
            @block.sync
            def _(sp):
                W.load_ahead(sp, 2)

            @block.tensor
            def _(pe):
                pe.wait_ge(o_ready, 1)
                for n in range(4):
                    t, q = n // 2, n % 2
                    for k in range(4):
                        c = P * (4 * q + k)
                        last = nc.tensor.transpose(K.ps[:, n, P * k:P * k + P], o[:, t, c:c + P], K.ident)
                    last.then_inc(t_made, 1)
                pe.wait_ge(t_kept, 4)
                for n in range(2):
                    w = W.take(pe)
                    for t in range(TT):
                        for k in range(KT):
                            last = nc.tensor.matmul(K.ps[:, 4 + 2 * t + n, :], K.mixT[:, k, P * t:P * t + P], w[:, k, :],
                                                    start=(k == 0), stop=(k == KT - 1))
                            if n and t == 0 and k == 0:
                                last.then_inc(W.used, 1)
                        last.then_inc(made, 1)
                pe.wait_ge(made, 4)
                nc.tensor.nop().then_inc(W.used, 1)

            @block.scalar
            def _(act):
                act.wait_ge(ms_ready, 1)
                nc.scalar.activation(root, ss, ACT.Sqrt).then_inc(rooted, 1)
                for n in range(4):
                    t, q = n // 2, n % 2
                    act.wait_ge(t_made, n + 1)
                    nc.scalar.activation(K.mixT[:, 4 * q:4 * q + 4, P * t:P * t + P],
                                         K.ps[:, n, :].rearrange("p (k t) -> p k t", t=P), ACT.Copy).then_inc(t_kept, 1)

            @block.vector
            def _(dve):
                link = chain(dve, dve_step)
                heads = lambda ap: ap.rearrange("p (h e) -> p h e", e=HD)
                link(nc.vector.tensor_scalar(den, K.den, -1.0, None, ALU.mult))
                link(nc.vector.tensor_tensor(den, den, K.den, ALU.max))
                link(nc.vector.tensor_tensor(den, den, K.em, ALU.max))
                link(nc.vector.reciprocal(den, den))
                for t in range(TT):
                    h = heads(o[:, t, 512:768])
                    link(nc.vector.tensor_tensor(h, h, den[:, t, :].unsqueeze(2).broadcast_to([P, 4, HD]), ALU.mult))
                    both = o[:, t, 256:768]
                    link(nc.vector.tensor_tensor(sq[:, t, :], both, both, ALU.mult))
                    link(nc.vector.tensor_reduce(ss[:, t, :], heads(sq[:, t, :]), AX, ALU.add))
                nc.vector.tensor_scalar(ss, ss, 1.0 / HD, EPS, ALU.mult, ALU.add).then_inc(ms_ready, 1)
                dve.wait_ge(rooted, 1)
                link(nc.vector.reciprocal(root, root))
                link(nc.vector.tensor_scalar(root[:, :, 0:4], root[:, :, 0:4], 1.0 - lam_init, None, ALU.mult))
                link(nc.vector.tensor_tensor(ztok[:, :, 768:1024], ztok[:, :, 768:1024],
                                             K.head_g.unsqueeze(1).broadcast_to([P, TT, 256]), ALU.mult))
                for t in range(TT):
                    both = heads(o[:, t, 256:768])
                    link(nc.vector.tensor_tensor(both, both, root[:, t, :].unsqueeze(2).broadcast_to([P, 8, HD]), ALU.mult))
                    h = heads(o[:, t, 256:512])
                    link(nc.vector.tensor_tensor(h, h, K.sub_g.unsqueeze(1).broadcast_to([P, 4, HD]), ALU.mult))
                    ins = nc.vector.tensor_tensor(o[:, t, 512:768], o[:, t, 512:768], ztok[:, t, 768:1024], ALU.mult)
                    if t == 0:
                        link(ins)
                ins.then_inc(o_ready, 1)
                for m in range(4):
                    n, t = m // 2, m % 2
                    half = slice(512 * n, 512 * n + 512)
                    dve.wait_ge(made, m + 1)
                    nc.vector.tensor_tensor(K.x[:, t, half], K.x[:, t, half], K.ps[:, 4 + 2 * t + n, :], ALU.add)
    A.high = top


def feed_forward(nc, K, layer):
    A, W = K.A, K.W
    A.low = K.base
    top = A.high
    last_layer = layer == 1
    gain, h, hT = A.temp(D), A.temp(TT, D), A.temp(KT, T)
    gate = A.temp(4, T)
    hidT = A.temp(NFT, T)
    sums, ms, root = A.temp(4), A.temp(4), A.temp(4)
    final_gain = A.temp(D)
    with nc.cleanup_on_exit():
        landed, squared, ms_ready, rooted, h_ready = (K.sem(n) for n in (
            "gain_landed", "squared", "ms_ready", "rooted", "h_ready"))
        t_made, t_kept, made, gated, hid_ready, y_made, dve_step = (K.sem(n) for n in (
            "t_made", "t_kept", "made", "gated", "hid_ready", "y_made", "dve_step"))
        x_ready, out_ready = K.sem("x_ready"), K.sem("out_ready")
        with nc.Block() as block:
            @block.sync
            def _(sp):
                sp.dma_start(gain, K.dram["norm_ffn_2"][layer].partition_broadcast(P)).then_inc(landed, 16)
                sp.dma_start(final_gain, K.dram["norm_final_2"].partition_broadcast(P)).then_inc(landed, 16)
                W.load_ahead(sp, 3 * FCH)
                sp.wait_ge(landed, 32)
                if last_layer:
                    sp.wait_ge(out_ready, 2)
                    sp.dma_start(K.out.rearrange("(t p) d -> p t d", p=P), h).then_inc(K.out_stored, 16)
                    sp.wait_ge(K.out_stored, 16)

            @block.tensor
            def _(pe):
                for n in range(4):
                    t, q = n // 2, n % 2
                    pe.wait_ge(h_ready, t + 1)
                    for k in range(4):
                        c = P * (4 * q + k)
                        last = nc.tensor.transpose(K.ps[:, n, P * k:P * k + P], h[:, t, c:c + P], K.ident)
                    last.then_inc(t_made, 1)
                pe.wait_ge(t_kept, 4)
                for f in range(NFT):
                    if f % 4 == 0:
                        wg, wu = W.take(pe), W.take(pe)
                    if f >= 4:
                        pe.wait_ge(hid_ready, f - 3)
                    at = P * (f % 4)
                    for i, w in enumerate((wg, wu)):
                        for k in range(KT):
                            last = nc.tensor.matmul(K.ps[:, f % 4, T * i:T * i + T], w[:, k, at:at + P], hT[:, k, :],
                                                    start=(k == 0), stop=(k == KT - 1))
                            if f and f % 4 == 0 and i == 0 and k == 0:
                                last.then_inc(W.used, 2)
                    last.then_inc(made, 1)
                for f in range(NFT):
                    if f % 4 == 0:
                        wd = W.take(pe).rearrange("p k n -> p (k n)").rearrange("p (f d) -> p f d", d=D)
                    pe.wait_ge(hid_ready, f + 1)
                    for t in range(TT):
                        for n in range(2):
                            last = nc.tensor.matmul(K.ps[:, 4 + 2 * t + n, :], hidT[:, f, P * t:P * t + P],
                                                    wd[:, f % 4, 512 * n:512 * n + 512],
                                                    start=(f == 0), stop=(f == NFT - 1))
                            if f % 4 == 0 and t == 0 and n == 0:
                                last.then_inc(W.used, 1 if f else 2)
                last.then_inc(y_made, 1)
                pe.wait_ge(y_made, 1)
                nc.tensor.nop().then_inc(W.used, 1)

            @block.scalar
            def _(act):
                for t in range(TT):
                    nc.scalar.activation(h[:, t, :], K.x[:, t, :], ACT.Square, accum_out=sums[:, t:t + 1]).then_inc(squared, 1)
                act.wait_ge(ms_ready, 1)
                nc.scalar.activation(root[:, 0:2], ms[:, 0:2], ACT.Sqrt).then_inc(rooted, 1)
                for n in range(4):
                    t, q = n // 2, n % 2
                    act.wait_ge(t_made, n + 1)
                    nc.scalar.activation(hT[:, 4 * q:4 * q + 4, P * t:P * t + P],
                                         K.ps[:, n, :].rearrange("p (k t) -> p k t", t=P), ACT.Copy).then_inc(t_kept, 1)
                for f in range(NFT):
                    act.wait_ge(made, f + 1)
                    if f >= 4:
                        act.wait_ge(hid_ready, f - 3)
                    nc.scalar.activation(gate[:, f % 4, :], K.ps[:, f % 4, 0:T], ACT.Silu).then_inc(gated, 1)
                if last_layer:
                    for t in range(TT):
                        act.wait_ge(x_ready, 2 * t + 2)
                        nc.scalar.activation(h[:, t, :], K.x[:, t, :], ACT.Square, accum_out=sums[:, 2 + t:3 + t]).then_inc(squared, 1)
                    act.wait_ge(ms_ready, 2)
                    nc.scalar.activation(root[:, 2:4], ms[:, 2:4], ACT.Sqrt).then_inc(rooted, 1)

            @block.vector
            def _(dve):
                link = chain(dve, dve_step)
                dve.wait_ge(squared, 2)
                nc.vector.tensor_scalar(ms[:, 0:2], sums[:, 0:2], 1.0 / D, EPS, ALU.mult, ALU.add).then_inc(ms_ready, 1)
                dve.wait_ge(rooted, 1)
                link(nc.vector.reciprocal(root[:, 0:2], root[:, 0:2]))
                dve.wait_ge(landed, 32)
                for t in range(TT):
                    nc.vector.scalar_tensor_tensor(h[:, t, :], K.x[:, t, :], root[:, t:t + 1], gain,
                                                   ALU.mult, ALU.mult).then_inc(h_ready, 1)
                for f in range(NFT):
                    dve.wait_ge(gated, f + 1)
                    nc.vector.tensor_tensor(hidT[:, f, :], gate[:, f % 4, :], K.ps[:, f % 4, T:2 * T],
                                            ALU.mult).then_inc(hid_ready, 1)
                dve.wait_ge(y_made, 1)
                for t in range(TT):
                    for n in range(2):
                        half = slice(512 * n, 512 * n + 512)
                        nc.vector.tensor_tensor(K.x[:, t, half], K.x[:, t, half], K.ps[:, 4 + 2 * t + n, :],
                                                ALU.add).then_inc(x_ready, 1)
                if last_layer:
                    dve.wait_ge(squared, 4)
                    nc.vector.tensor_scalar(ms[:, 2:4], sums[:, 2:4], 1.0 / D, EPS, ALU.mult, ALU.add).then_inc(ms_ready, 1)
                    dve.wait_ge(rooted, 2)
                    link(nc.vector.reciprocal(root[:, 2:4], root[:, 2:4]))
                    for t in range(TT):
                        nc.vector.scalar_tensor_tensor(h[:, t, :], K.x[:, t, :], root[:, 2 + t:3 + t], final_gain,
                                                       ALU.mult, ALU.mult).then_inc(out_ready, 1)
    A.high = top


def layer_stages():
    return [(stage, layer) for layer in range(2)
            for stage in (attention_inputs, mixer_preparation, attention, attention_out, feed_forward)]


def first_and_second_block(nc, dram, out):
    K = Kept()
    K.nc, K.dram, K.out = nc, dram, out
    K.A = Arena(nc, 127 * 256)
    K.W = WeightStream(nc, dram)
    K.out_stored = nc.alloc_semaphore("out_stored")
    K.ps = nc.alloc_psum_tensor("psum", [P, 8, 512], F32)
    A = K.A
    K.ident = A.keep(P)
    K.ones = A.keep(P)
    K.head_ones = A.keep(P)
    K.mixT = A.keep(KT, T)
    K.glT = A.keep(2, T)
    K.after_mixT = A.low
    K.rT = A.temp(4, T)
    K.rkT = A.temp(4, 2 * T)
    K.rvT = A.temp(4, 2 * T)
    K.wlT = A.temp(2 * T)
    K.alT = A.temp(2 * T)
    K.hT = A.temp(KT, 2 * T)
    for n, stage in enumerate(STAGES):
        K.stage = n + 1
        if isinstance(stage, tuple):
            stage[0](nc, K, stage[1])
        else:
            stage(nc, K)


class Kept:

    stage = 0

    def sem(self, name):
        return self.nc.alloc_semaphore(f"stage{self.stage}_{name}")


STAGES = [modulate_and_norm, project_in, retention, rwkv_constants, rwkv_context, rwkv_latent, rwkv_output, mixers_out, route, experts] + layer_stages()


def slots(w, width=512):
    k, n = w.shape
    pad = -n % width
    if pad:
        w = np.concatenate([w, np.zeros((k, pad), w.dtype)], 1)
    m = (n + pad) // width
    return np.ascontiguousarray(w.reshape(k // P, P, m, width).transpose(2, 1, 0, 3)).reshape(m, P, -1)


def layout(i):
    a = {}
    f = {k: np.asarray(v) for k, v in i.items()}
    a["x"], a["ctx"] = f["x"][0], f["ctx"][0]
    a["cT"] = np.concatenate([f["c_ctx"].reshape(KT, P).T, f["c"][0].reshape(KT, P).T], 1)
    a["ident"] = np.eye(P, dtype=np.float32)
    a["b_mod"] = f["b_mod"]
    a["norm_gains"] = f["norm_gains"][0]
    a["w_mod"] = slots(f["w_mod"][0])
    wi = f["w_in"][0]
    at = np.cumsum([0, 512, 512, 512, 64, 64, 64, 128, 128])
    piece = lambda w, n: w[..., at[n]:at[n + 1]]
    rw = wi[:, 2560:]
    doubled = lambda w: np.concatenate([piece(w, n) for n in (0, 1, 2, 3, 4, 5, 5, 6, 7)], -1)
    a["w_in"] = slots(np.concatenate([wi[:, :2560], doubled(rw)], 1))
    a["rwkv_conv"] = doubled(f["rwkv_conv"][0]).reshape(3, 16, P).transpose(2, 1, 0)
    by_channel = lambda v: v.reshape(4, P).T
    a["rwkv_w0"] = f["rwkv_w0"][0].reshape(2, H, HD).transpose(0, 2, 1).reshape(P, H)
    a["rwkv_w2"] = f["rwkv_w2"][0].reshape(P, 512)
    a["rwkv_a2"] = f["rwkv_a2"][0]
    a["rwkv_g2"] = f["rwkv_g2"][0].transpose(1, 0, 2)
    a["rwkv_vecs"] = np.stack([by_channel(f[n][0]) for n in
                               ("rwkv_a0", "rwkv_k_k", "rwkv_k_a")], 1)
    by_head = lambda v: np.concatenate([v.reshape(H, HD).T] * 2, 0)
    a["rwkv_dup_vecs"] = np.stack([by_head(f[n][0]) for n in ("rwkv_r_k", "rwkv_lnx_w", "rwkv_lnx_b")], 1)
    a["w_out"] = slots(f["w_out"][0])
    wg, wu, wd = (f[n][0] for n in ("w_gate", "w_up", "w_down"))
    a["w_moe"] = np.concatenate([np.stack([slots(w[e]) for e in range(NE)]) for w in (wg, wu, wd)], 1).reshape(6 * NE, P, -1)
    a["w_router"] = f["w_router"][0].reshape(KT, P, NE).transpose(1, 0, 2)
    second = [second_layout(f, layer) for layer in range(2)]
    for name in second[0]:
        a[name] = np.stack([s[name] for s in second])
    for name in ("w_in_2", "w_out_2", "w_gate_2", "w_up_2", "w_down_2"):
        a[name] = a[name].reshape(-1, P, SLOT)
    a["norm_mix_2"], a["norm_ffn_2"], a["norm_final_2"] = f["norm_mix_2"], f["norm_ffn_2"], f["norm_final_2"]
    a.update(tables())
    return a


def second_layout(f, layer):
    w = f["w_in_2"][layer]
    names = ["aq", "kc", "vc", "ks", "vs", "kw", "vw", "ag", "bq", "bk", "bv", "cu", "cv", "ci", "cf", "co", "dq", "dk", "dv"]
    sizes = [256, 64, 64, 64, 64, 64, 64, 12, 256, 256, 256, 256, 256, 4, 4, 256, 256, 256, 256]
    at = np.cumsum([0] + sizes)
    col = {n: w[:, at[i]:at[i + 1]] for i, n in enumerate(names)}
    pad = np.zeros((D, 108), w.dtype)
    order = ["aq", "kc", "kc", "vc", "vc", "ks", "ks", "kw", "kw", "bq", "bk", "cu", "dq", "dk"]
    by_token = [col[n] for n in ("vs", "vw", "ag", "ci", "cf")] + [pad] + [col[n] for n in ("bv", "cv", "co", "dv")]
    twice = lambda v: np.concatenate([v, v], 0)
    cmp_w = f["nsa_cmp_w_2"][layer].reshape(2, 32, HD, HD).transpose(2, 0, 1, 3)
    conv = np.concatenate([f["mlstm_conv_w_2"][layer], f["mlstm_conv_b_2"][layer][None]], 0)
    wqk = np.stack([f["mlstm_wq_2"][layer], f["mlstm_wk_2"][layer]]).reshape(2, 2, 2, HD, HD)
    down = np.concatenate([f["w_down_2"][layer], np.zeros((2 * P, D), w.dtype)]).reshape(FCH, 4, P, D)
    return {
        "w_in_2": slots(np.concatenate([col[n] for n in order] + by_token, 1)),
        "w_out_2": slots(f["w_out_2"][layer]),
        "w_gate_2": slots(f["w_gate_2"][layer]),
        "w_up_2": slots(f["w_up_2"][layer]),
        "w_down_2": down.transpose(0, 2, 1, 3),
        "nsa_cmp_w_2": twice(cmp_w),
        "nsa_cmp_pos_2": twice(f["nsa_cmp_pos_2"][layer].transpose(2, 0, 1)),
        "mlstm_conv_2": conv.reshape(5, 2, P).transpose(2, 1, 0),
        "mlstm_wqk_2": wqk.transpose(2, 3, 0, 1, 4).reshape(P, 2, 2, HD),
        "mlstm_gate_b_2": f["mlstm_gate_b_2"][layer].reshape(8),
        "diff_lambda_2": f["diff_lambda_2"][layer].reshape(P),
        "diff_norm_2": f["diff_norm_2"][layer],
        "mlstm_norm_2": f["mlstm_norm_2"][layer],
    }


def tables():
    t = {}
    n = np.arange(T, dtype=np.float32)
    freq = 10000.0 ** (-np.arange(16, dtype=np.float32) / 16)
    ang = np.concatenate([np.floor(n / 64)[:, None] * freq, (n % 64)[:, None] * freq], 1)
    lane = np.arange(P)
    sign = np.where(lane % 64 < 32, -1.0, 1.0)[:, None]
    t["rope_cos"] = np.cos(ang).T[lane % 32]
    t["rope_sin"] = np.sin(ang).T[lane % 32] * sign
    t["swap64"] = (lane[:, None] == (lane ^ 32)[None, :])
    log_gamma = np.log1p(-np.exp2(-5.0 - np.arange(H)))
    s, q = np.arange(P)[:, None, None], np.arange(T)[None, None, :]
    g = log_gamma[None, :, None]
    power = lambda e: np.where(e >= 0, np.exp(np.maximum(e, 0) * g), 0.0)
    t["ret_decay_f"] = power(q - s)
    t["ret_decay_b"] = power(P + s - q)
    head = 2 * np.arange(4)[None, :, None] + (lane >= 64)[:, None, None]
    lg = log_gamma[head]
    t["ret_q_decay"] = np.stack([np.exp((q + 1) * lg), np.exp((T - q) * lg)], 1)
    j = np.arange(TT)[None, :, None] * P + lane[:, None, None]
    lg = log_gamma[None, None, :]
    t["ret_k_decay"] = np.stack([np.exp((T - 1 - j) * lg), np.exp(j * lg)], 1)
    i, j = np.arange(C)[:, None], np.arange(C)[None, :]
    joins = lambda m, r, c: (r // (2 * m) == c // (2 * m)) & (r // m % 2 == 1) & (c // m % 2 == 0)
    fwd = [joins(1, i, j)] + [joins(2 ** n, j, i) for n in range(6)] + [j > i, j >= i]
    bwd = [joins(1, j, i)] + [joins(2 ** n, i, j) for n in range(6)] + [j < i, j <= i]
    t["rwkv_masks"] = np.concatenate([np.stack(fwd, 1), np.stack(bwd, 1)], 0)
    for dim in (64, 32):
        inv = 1.0 / (10000.0 ** (np.arange(0, dim, 2, dtype=np.float32) / dim))
        ang = (n[:, None] * inv[None, :]).T[lane % (dim // 2)]
        t[f"cos{dim}"] = np.cos(ang)
        t[f"sin{dim}"] = np.sin(ang) * np.where(lane % dim < dim // 2, -1.0, 1.0)[:, None]
    t["swap32"] = (lane[:, None] == (lane ^ 16)[None, :])
    t["tri"] = lane[:, None] <= lane[None, :]
    back = (np.arange(TT)[None, :, None] * P + lane[:, None, None]) - np.arange(T)[None, None, :]
    times = sum(((back >= 0) & (back <= window) & (back % step == 0)).astype(int)
                for window, step in ((128, 1), (512, 4), (2048, 16)))
    t["attn_bias"] = np.stack([np.where(back >= 0, 0.0, NEG), np.where(times > 0, np.log(np.maximum(times, 1)), NEG)], 1)
    seen = (np.arange(16) * 16 + 31)[None, None, :] <= np.arange(TT)[None, :, None] * P + lane[:, None, None]
    seen[:, :, 15] = False
    t["cmp_bias"], t["cmp_on"] = np.where(seen, 0.0, NEG), seen
    t["earlier"] = np.arange(T)[None, None, :] < (np.arange(TT)[None, :, None] * P + lane[:, None, None])
    t["places"] = np.tile(np.arange(CAP), (P, 1))
    return {k: np.ascontiguousarray(v, dtype=np.float32) for k, v in t.items()}


def kernel(**inputs):
    import concourse.bacc as bacc
    from concourse.bass_utils import run_bass_kernel_spmd

    nc = bacc.Bacc("TRN2", target_bir_lowering=False, num_devices=1)
    arrays, dram = {}, {}
    for name, a in layout(inputs).items():
        a = np.ascontiguousarray(a)
        arrays[f"in_{name}"] = a
        dram[name] = nc.dram_tensor(f"in_{name}", a.shape, mybir.dt.from_np(a.dtype), kind="ExternalInput").ap()
    out = nc.dram_tensor("out_0", (T, D), F32, kind="ExternalOutput").ap()
    first_and_second_block(nc, dram, out)
    r = run_bass_kernel_spmd(nc, [arrays], core_ids=[0])
    return r.results[0]["out_0"].reshape(1, T, D)
```

```python
from contextlib import ExitStack

import numpy as np

import concourse.bass as bass
from concourse import mybir

ALU = mybir.AluOpType
ACT = mybir.ActivationFunctionType
AX = mybir.AxisListType.X
F32 = mybir.dt.float32

P = 128
D = 1024
T = 256
KT = D // P
TT = T // P
NB = 5
NX = 3
SLOT = 4096
CTX, LAT = 0, 1
H = 8
HD = 64
C = 64
EPS = 1e-6
GN_EPS = 64e-5
NEG = -1e30
NE = 16
CAP = 2 * T // NE

STREAM = (
    [("w_mod", i) for i in range(4)]
    + [("w_in", i) for i in range(9)]
    + [("w_mod", 4), ("w_mod", 5), ("w_out", 0), ("w_out", 1)]
    + [("w_mod", i) for i in range(6, 12)]
    + [("w_moe", i) for i in range(6 * NE)]
)
FF = 2816
NFT = FF // P
FCH = 6
for _l in range(2):
    STREAM += [("w_in_2", 7 * _l + i) for i in range(7)] + [("w_out_2", 2 * _l + i) for i in range(2)]
    for _i in range(FCH):
        STREAM += [("w_gate_2", FCH * _l + _i), ("w_up_2", FCH * _l + _i)]
    STREAM += [("w_down_2", FCH * _l + _i) for _i in range(FCH)]


class Arena:

    def __init__(self, nc, words):
        self.t = nc.alloc_sbuf_tensor("arena", [P, words], F32)
        self.low, self.high = 0, words

    def view(self, at, shape):
        n = int(np.prod(shape))
        v = self.t[:, at:at + n]
        names = "abcd"[:len(shape)]
        if len(shape) > 1:
            v = v.rearrange(f"p ({' '.join(names)}) -> p {' '.join(names)}",
                            **{names[i]: shape[i] for i in range(len(shape))})
        return v

    def keep(self, *shape):
        at = self.low
        self.low += int(np.prod(shape))
        assert self.low <= self.high, (self.low, self.high)
        return self.view(at, shape)

    def temp(self, *shape):
        self.high -= int(np.prod(shape))
        assert self.low <= self.high, (self.low, self.high)
        return self.view(self.high, shape)


class WeightStream:

    def __init__(self, nc, arrays):
        self.arrays = arrays
        self.ring = nc.alloc_sbuf_tensor("weight_ring", [P, NB, SLOT], F32)
        self.landed = [nc.alloc_semaphore(f"weights_landed_{i}") for i in range(NB + NX)]
        self.used = nc.alloc_semaphore("weight_slot_used")
        self.loaded = 0
        self.read = 0
        self.reads_to = 0
        self.extra = None
        first = STREAM.index(("w_moe", 0))
        end = first + 6 * NE
        turns = NB + NX
        assert (end - first) % turns == 0
        place = []
        for n in range(len(STREAM)):
            if n < first:
                place.append(n % NB)
            elif n < end:
                at = (n - first) % turns
                place.append((first + at) % NB if at < NB else at)
            else:
                place.append((first + n - end) % NB)
        self.place = place
        self.before = [max((m for m in range(n) if place[m] == place[n]), default=-1) for n in range(len(STREAM))]
        self.count = [place[:n + 1].count(place[n]) for n in range(len(STREAM))]

    def slot(self, n):
        at = self.place[n]
        return self.ring[:, at, :] if at < NB else self.extra[:, at - NB, :]

    def load_to(self, sp, end):
        for n in range(self.loaded, min(end, len(STREAM))):
            if self.before[n] >= 0:
                sp.wait_ge(self.used, self.before[n] + 1)
            name, i = STREAM[n]
            sp.dma_start(self.slot(n), self.arrays[name][i]).then_inc(self.landed[self.place[n]], 16)
            self.loaded = n + 1

    def load_ahead(self, sp, n):
        self.reads_to += n
        self.load_to(sp, self.reads_to + NB)

    def take(self, pe):
        n = self.read
        pe.wait_ge(self.landed[self.place[n]], 16 * self.count[n])
        self.read += 1
        return self.slot(n).rearrange("p (k n) -> p k n", n=512)


def chain(engine, sem):
    count = [0]

    def link(instruction):
        instruction.then_inc(sem, 1)
        count[0] += 1
        engine.wait_ge(sem, count[0])

    return link


def partial_modulation(nc, K, bank, cond, w, bias, used):
    for k in range(4):
        if k == 0:
            nc.tensor.matmul(bank[0:32], K.ones[0:1, 0:32], bias, start=True, stop=False, tile_position=(0, 0),
                             skip_group_check=True)
        nc.tensor.matmul(bank[32 * k:32 * k + 32], cond[:, k, :], w[:, k, :], start=(k > 0), stop=False,
                         tile_position=(0, 32 * k), skip_group_check=True)
    for k in range(4, KT):
        s = k - 4
        last = nc.tensor.matmul(bank[32 * s:32 * s + 32], cond[:, k, :], w[:, k, :], start=False, stop=True,
                                tile_position=(0, 32 * s), skip_group_check=True)
        if s == 0 and used is not None:
            last.then_inc(used, 1)
    return last


def modulate_and_norm(nc, K):
    A, W = K.A, K.W
    top = A.high
    x_ctx, x_lat = A.temp(TT, D), A.temp(TT, D)
    h = A.temp(2 * TT, D)
    cT = A.temp(KT * 2)
    cond = A.temp(KT, 32)
    part = A.temp(2, 512)
    gain = A.temp(D)
    brow = A.temp(2 * D)
    gmod = A.temp(2, D)
    shift = A.temp(2, D)
    sumsq = A.temp(4)
    rstd = A.temp(4)
    ms = A.temp(4)
    root = A.temp(4)
    with nc.cleanup_on_exit():
        in_small = K.sem("conditioning_landed")
        in_x = K.sem("x_landed")
        ones_set = K.sem("ones_set")
        silu_done = K.sem("silu_done")
        cond_ready = K.sem("cond_ready")
        part_made = K.sem("part_made")
        part_kept = K.sem("part_kept")
        sel_ready = K.sem("sel_ready")
        mod_ready = K.sem("mod_ready")
        mod_read = K.sem("mod_read")
        squares = K.sem("squares_summed")
        ms_ready = K.sem("mean_squares_ready")
        root_ready = K.sem("root_ready")
        h_ready = K.sem("h_ready")
        hT_made = K.sem("hT_made")
        hT_read = K.sem("hT_read")
        dve_step = K.sem("dve_step")

        with nc.Block() as block:
            @block.sync
            def _(sp):
                sp.dma_start(cT, K.dram["cT"]).then_inc(in_small, 16)
                sp.dma_start(brow[0:1, :], K.dram["b_mod"][:, 0:2 * D]).then_inc(in_small, 16)
                sp.dma_start(gain, K.dram["norm_gains"][0, :].partition_broadcast(P)).then_inc(in_small, 16)
                sp.dma_start(K.ident, K.dram["ident"]).then_inc(in_small, 16)
                sp.dma_start(x_ctx, K.dram["ctx"].rearrange("(t p) d -> p t d", p=P)).then_inc(in_x, 16)
                sp.dma_start(x_lat, K.dram["x"].rearrange("(t p) d -> p t d", p=P)).then_inc(in_x, 16)
                W.load_to(sp, NB)
                W.load_ahead(sp, 4)

            @block.gpsimd
            def _(pool):
                nc.gpsimd.memset(K.ones, 1.0).then_inc(ones_set, 1)
                pool.wait_ge(ones_set, 1)
                nc.gpsimd.memset(K.head_ones, 0.0).then_inc(ones_set, 1)
                pool.wait_ge(ones_set, 2)
                for i in range(2):
                    nc.gpsimd.memset(K.head_ones[i * HD:(i + 1) * HD, i * HD:(i + 1) * HD], 1.0).then_inc(ones_set, 1)

            @block.scalar
            def _(act):
                act.wait_ge(in_small, 64)
                nc.scalar.activation(cT, cT, ACT.Silu).then_inc(silu_done, 1)
                act.wait_ge(in_x, 32)
                for j in range(4):
                    src = x_ctx[:, j, :] if j < 2 else x_lat[:, j - 2, :]
                    nc.scalar.activation(h[:, j, :], src, ACT.Square, accum_out=sumsq[:, j:j + 1]).then_inc(squares, 1)
                for c in range(4):
                    act.wait_ge(part_made, c + 1)
                    if c >= 2:
                        act.wait_ge(mod_ready, 2 * (c - 1))
                    nc.scalar.activation(part[:, c % 2, :], K.ps[:, 2 * c, :], ACT.Copy).then_inc(part_kept, 1)
                act.wait_ge(ms_ready, 1)
                nc.scalar.activation(root, ms, ACT.Sqrt).then_inc(root_ready, 1)
                for j in range(4):
                    for q in range(2):
                        n = 2 * j + q
                        act.wait_ge(hT_made, n + 1)
                        nc.scalar.activation(K.hT[:, 4 * q:4 * q + 4, P * j:P * j + P],
                                             K.ps[:, n % 4, :].rearrange("p (k t) -> p k t", t=P),
                                             ACT.Copy).then_inc(hT_read, 1)

            @block.vector
            def _(dve):
                link = chain(dve, dve_step)
                dve.wait_ge(silu_done, 1)
                for s in range(2):
                    ins = nc.vector.tensor_copy(cond[:, :, 16 * s:16 * s + 16],
                                                cT[:, KT * s:KT * s + KT].unsqueeze(2).broadcast_to([P, KT, 16]))
                    ins.then_inc(cond_ready, 1)
                nc.vector.tensor_reduce(K.sel, K.ident.rearrange("p (k i c) -> p i c k", i=2, c=16)[:, :, 0, :], AX,
                                        ALU.add).then_inc(sel_ready, 1)
                dve.wait_ge(squares, 4)
                nc.vector.tensor_scalar(ms, sumsq, 1.0 / D, EPS, ALU.mult, ALU.add).then_inc(ms_ready, 1)
                dve.wait_ge(root_ready, 1)
                link(nc.vector.reciprocal(rstd, root))
                for n in range(8):
                    dve.wait_ge(mod_ready, n + 1)
                    c, s = n // 2, n % 2
                    half = slice(512 * (c % 2), 512 * (c % 2) + 512)
                    if c < 2:
                        link(nc.vector.tensor_copy(shift[:, s, half], K.ps[:, n, :]))
                    else:
                        nc.vector.scalar_tensor_tensor(gmod[:, s, half], K.ps[:, n, :], 1.0, gain[:, half],
                                                       ALU.add, ALU.mult).then_inc(mod_read, 1)
                dve.wait_ge(mod_read, 4)
                for j in range(4):
                    src = x_ctx[:, j, :] if j < 2 else x_lat[:, j - 2, :]
                    link(nc.vector.scalar_tensor_tensor(h[:, j, :], src, rstd[:, j:j + 1], gmod[:, j // 2, :],
                                                        ALU.mult, ALU.mult))
                    nc.vector.tensor_tensor(h[:, j, :], h[:, j, :], shift[:, j // 2, :], ALU.add).then_inc(h_ready, 1)

            @block.tensor
            def _(pe):
                pe.wait_ge(in_small, 64)
                pe.wait_ge(ones_set, 4)
                pe.wait_ge(cond_ready, 2)

                def combine(c):
                    pe.wait_ge(part_kept, c + 1)
                    for s in range(2):
                        nc.tensor.matmul(K.ps[:, 2 * c + s, :], K.sel[:, s:s + 1].broadcast_to([P, P]), part[:, c % 2, :],
                                         start=True, stop=True).then_inc(mod_ready, 1)

                for c in range(4):
                    partial_modulation(nc, K, K.ps[:, 2 * c, :], cond, W.take(pe), brow[0:1, 512 * c:512 * c + 512],
                                       W.used if c else None).then_inc(part_made, 1)
                    if c == 0:
                        pe.wait_ge(sel_ready, 1)
                    else:
                        combine(c - 1)
                combine(3)
                pe.wait_ge(mod_ready, 8)
                nc.tensor.nop().then_inc(W.used, 1)
                for j in range(4):
                    pe.wait_ge(h_ready, j + 1)
                    if j == 0:
                        pe.wait_ge(mod_read, 4)
                    for q in range(2):
                        n = 2 * j + q
                        if n >= 4:
                            pe.wait_ge(hT_read, n - 3)
                        for k in range(4):
                            last = nc.tensor.transpose(K.ps[:, n % 4, P * k:P * k + P],
                                                       h[:, j, P * (4 * q + k):P * (4 * q + k + 1)], K.ident)
                        last.then_inc(hT_made, 1)
    A.high = top


def project_in(nc, K):
    A, W = K.A, K.W
    K.qT = A.keep(4, T)
    K.kT = A.keep(4, T)
    K.v_tok = A.keep(TT, 512)
    K.kc_tok = A.keep(TT, 512)
    K.vc_tok = A.keep(TT, 512)
    K.gateT = A.keep(4, 2, T)
    conv = A.keep(16, 3)
    hT = K.hT

    jobs = []
    for b in range(4):
        jobs.append((0, "T", b, K.qT[:, b, :], "copy"))
    for b in range(4):
        jobs.append((1, "T", b, K.kT[:, b, :], "scaled"))
    for t in range(2):
        jobs.append((1, "tok", t, K.kc_tok[:, t, :], "scaled"))
    for t in range(4):
        jobs.append((2, "tok", t, (K.vc_tok if t < 2 else K.v_tok)[:, t % 2, :], "copy"))
    for b in range(4):
        jobs.append((3, "T", b, K.gateT[:, b, 0, :], "silu"))
    for b in range(4):
        jobs.append((4, "T", b, K.gateT[:, b, 1, :], "silu"))
    for b in range(4):
        jobs.append((5, "T", b, K.rT[:, b, :], "conv"))
    for b in range(4):
        jobs.append((6, "TT", b, K.rkT[:, b, :], "conv"))
    for b in range(4):
        jobs.append((7, "TT", b, K.rvT[:, b, :], "conv"))
    jobs.append((8, "TT", 0, K.wlT, "conv"))
    jobs.append((8, "TT", 1, K.alT, "conv"))
    jobs.append((8, "T", 2, K.glT[:, 0, :], "conv"))
    jobs.append((8, "T", 3, K.glT[:, 1, :], "conv"))
    taken = [sum((j[4] == "conv") == (jobs[n][4] == "conv") for j in jobs[:n + 1]) for n in range(len(jobs))]

    with nc.cleanup_on_exit():
        in_conv = K.sem("conv_weights_landed")
        projected = K.sem("projected")
        act_took = K.sem("act_took")
        dve_took = K.sem("dve_took")
        dve_step = K.sem("dve_step")
        with nc.Block() as block:
            @block.sync
            def _(sp):
                sp.dma_start(conv, K.dram["rwkv_conv"]).then_inc(in_conv, 16)
                W.load_ahead(sp, 9)

            @block.tensor
            def _(pe):
                slot = -1
                for n, (s, kind, b, dst, how) in enumerate(jobs):
                    if s != slot:
                        w, slot = W.take(pe), s
                    if n >= 8:
                        pe.wait_ge(dve_took if jobs[n - 8][4] == "conv" else act_took, taken[n - 8])
                    bank = K.ps[:, n % 8, :]
                    for k in range(KT):
                        if kind == "tok":
                            last = nc.tensor.matmul(bank, hT[:, k, P * b:P * b + P], w[:, k, :],
                                                    start=(k == 0), stop=(k == KT - 1))
                        elif kind == "T":
                            last = nc.tensor.matmul(bank[:, 0:T], w[:, k, P * b:P * b + P], hT[:, k, T:2 * T],
                                                    start=(k == 0), stop=(k == KT - 1))
                        else:
                            last = nc.tensor.matmul(bank, w[:, k, P * b:P * b + P], hT[:, k, :],
                                                    start=(k == 0), stop=(k == KT - 1))
                        if k == 0 and n and jobs[n - 1][0] != s:
                            last.then_inc(W.used, 1)
                    last.then_inc(projected, 1)
                pe.wait_ge(projected, len(jobs))
                nc.tensor.nop().then_inc(W.used, 1)

            @block.scalar
            def _(act):
                for n, (s, kind, b, dst, how) in enumerate(jobs):
                    if how == "conv":
                        continue
                    act.wait_ge(projected, n + 1)
                    src = K.ps[:, n % 8, 0:T] if kind == "T" else K.ps[:, n % 8, :]
                    nc.scalar.activation(dst, src, ACT.Silu if how == "silu" else ACT.Copy,
                                         scale=HD ** -0.5 if how == "scaled" else 1.0).then_inc(act_took, 1)

            @block.vector
            def _(dve):
                link = chain(dve, dve_step)
                dve.wait_ge(in_conv, 16)
                for n, (s, kind, b, dst, how) in enumerate(jobs):
                    if how != "conv":
                        continue
                    dve.wait_ge(projected, n + 1)
                    w = conv[:, 4 * (s - 5) + b, :]
                    ns = 1 if kind == "T" else 2
                    u = K.ps[:, n % 8, 0:T * ns].rearrange("p (s t) -> p s t", s=ns)
                    o = dst.rearrange("p (s t) -> p s t", s=ns)
                    link(nc.vector.tensor_scalar(o, u, w[:, 1:2], None, ALU.mult))
                    link(nc.vector.scalar_tensor_tensor(o[:, :, 1:T], u[:, :, 0:T - 1], w[:, 0:1], o[:, :, 1:T],
                                                        ALU.mult, ALU.add))
                    nc.vector.scalar_tensor_tensor(o[:, :, 0:T - 1], u[:, :, 1:T], w[:, 2:3], o[:, :, 0:T - 1],
                                                   ALU.mult, ALU.add).then_inc(dve_took, 1)
    A.high += KT * 2 * T


def retention(nc, K):
    A = K.A
    top = A.high
    cos, sin, swap = A.temp(T), A.temp(T), A.temp(P)
    decay_f, decay_b = A.temp(H, T), A.temp(H, T)
    q_decay = A.temp(2, 4, T)
    k_decay = A.temp(2, TT, H)
    q_dec = q_decay
    state = A.temp(2, 4, P)
    k_dec, turned = A.temp(2, TT, 512), A.temp(2, 512)
    probs = A.view(A.high, (2, 2, 2, 3 * P))
    square, root = A.temp(2, 512), A.temp(2, 512)
    eps = A.temp(1)
    parts = {0: ((0, 0, T, 0), (1, P, T, T)), 1: ((0, 0, P, 0), (1, 0, T, P))}

    with nc.cleanup_on_exit():
        in_rope, in_tables = K.sem("rope_landed"), K.sem("tables_landed")
        swapped, rotated = K.sem("swapped"), K.sem("rotated")
        eps_set, dve_step = K.sem("eps_set"), K.sem("dve_step")
        k_decayed, state_made, state_kept = K.sem("k_decayed"), K.sem("state_made"), K.sem("state_kept")
        scored, masked = K.sem("scored"), K.sem("masked")
        y_made, squared, summed, rooted, y_used = (K.sem(n) for n in ("y_made", "squared", "summed", "rooted", "y_used"))
        with nc.Block() as block:
            @block.sync
            def _(sp):
                for dst, name in ((cos, "rope_cos"), (sin, "rope_sin"), (swap, "swap64")):
                    sp.dma_start(dst, K.dram[name]).then_inc(in_rope, 16)
                for dst, name in ((decay_f, "ret_decay_f"), (decay_b, "ret_decay_b"), (q_decay, "ret_q_decay"),
                                  (k_decay, "ret_k_decay")):
                    sp.dma_start(dst, K.dram[name]).then_inc(in_tables, 16)

            @block.gpsimd
            def _(pool):
                nc.gpsimd.memset(eps, EPS).then_inc(eps_set, 1)

            @block.tensor
            def _(pe):
                pe.wait_ge(in_rope, 48)
                for n in range(4):
                    x = (K.qT if n < 2 else K.kT)[:, 2 * (n % 2):2 * (n % 2) + 2, :]
                    nc.tensor.matmul(K.ps[:, n, :], swap, x, start=True, stop=True).then_inc(swapped, 1)
                for d in range(2):
                    pe.wait_ge(k_decayed, d + 1)
                    for b in range(4):
                        for t in range(TT):
                            last = nc.tensor.matmul(K.ps[:, 4 + d, P * b:P * b + P], k_dec[:, d, t, P * b:P * b + P],
                                                    K.vc_tok[:, t, P * b:P * b + P], start=(t == 0), stop=(t == TT - 1))
                    last.then_inc(state_made, 1)
                pe.wait_ge(rotated, 4)

                def scores(b):
                    if b >= 2:
                        pe.wait_ge(masked, 2 * (b - 1))
                    for i in range(2):
                        rows = slice(HD * i, HD * i + HD)
                        for t in range(TT):
                            last = nc.tensor.matmul(K.ps[:, 2 * (b % 2) + i, T * t:T * t + T],
                                                    K.kT[rows, b, P * t:P * t + P], K.qT[rows, b, :],
                                                    start=True, stop=True)
                        last.then_inc(scored, 1)

                scores(0)
                pe.wait_ge(state_kept, 2)
                for b in range(4):
                    if b < 3:
                        scores(b + 1)
                    if b >= 2:
                        pe.wait_ge(y_used, b - 1)
                    pe.wait_ge(masked, 2 * b + 2)
                    for d in range(2):
                        y = K.ps[:, 4 + b % 2, T * d:T * d + T]
                        nc.tensor.matmul(y, state[:, d, b, :], q_dec[:, d, b, :], start=True, stop=False,
                                         skip_group_check=True)
                        for i in range(2):
                            for t, t0, t1, at in parts[d]:
                                last = nc.tensor.matmul(y[HD * i:HD * i + HD, t0:t1],
                                                        K.v_tok[:, t, P * b + HD * i:P * b + HD * i + HD],
                                                        probs[:, b % 2, i, d, at:at + t1 - t0],
                                                        start=False, stop=(t == 1), skip_group_check=True)
                    last.then_inc(y_made, 1)
                    pe.wait_ge(squared, b + 1)
                    nc.tensor.matmul(K.ps[:, 6 + b % 2, :], K.head_ones, square[:, b % 2, :],
                                     start=True, stop=True).then_inc(summed, 1)

            @block.scalar
            def _(act):
                act.wait_ge(eps_set, 1)
                for b in range(4):
                    act.wait_ge(y_made, b + 1)
                    nc.scalar.activation(square[:, b % 2, :], K.ps[:, 4 + b % 2, :], ACT.Square).then_inc(squared, 1)
                    act.wait_ge(summed, b + 1)
                    if b >= 2:
                        act.wait_ge(y_used, b - 1)
                    nc.scalar.activation(root[:, b % 2, :], K.ps[:, 6 + b % 2, :], ACT.Sqrt, bias=eps[:, 0:1],
                                         scale=1.0 / HD).then_inc(rooted, 1)

            @block.vector
            def _(dve):
                link = chain(dve, dve_step)
                dve.wait_ge(in_tables, 64)
                for d in range(2):
                    for t in range(TT):
                        last = nc.vector.tensor_tensor(
                            k_dec[:, d, t, :].rearrange("p (h e) -> p h e", e=HD),
                            K.kc_tok[:, t, :].rearrange("p (h e) -> p h e", e=HD),
                            k_decay[:, d, t, :].unsqueeze(2).broadcast_to([P, H, HD]), ALU.mult)
                        if t == 1:
                            last.then_inc(k_decayed, 1)
                for n in range(4):
                    x = (K.qT if n < 2 else K.kT)[:, 2 * (n % 2):2 * (n % 2) + 2, :]
                    wide = [P, 2, T]
                    dve.wait_ge(swapped, n + 1)
                    link(nc.vector.tensor_tensor(turned[:, n % 2, :].rearrange("p (b t) -> p b t", b=2),
                                                 K.ps[:, n, :].rearrange("p (b t) -> p b t", b=2),
                                                 sin.unsqueeze(1).broadcast_to(wide), ALU.mult))
                    link(nc.vector.tensor_tensor(x, x, cos.unsqueeze(1).broadcast_to(wide), ALU.mult))
                    nc.vector.tensor_tensor(x, x, turned[:, n % 2, :].rearrange("p (b t) -> p b t", b=2),
                                            ALU.add).then_inc(rotated, 1)
                dve.wait_ge(rotated, 4)
                for d in range(2):
                    link(nc.vector.tensor_tensor(q_dec[:, d], K.qT, q_decay[:, d], ALU.mult))
                    dve.wait_ge(state_made, d + 1)
                    nc.vector.tensor_tensor(state[:, d], K.ps[:, 4 + d, :].rearrange("p (b v) -> p b v", v=P),
                                            K.head_ones.unsqueeze(1).broadcast_to([P, 4, P]),
                                            ALU.mult).then_inc(state_kept, 1)

                def mask(b):
                    for i in range(2):
                        h = 2 * b + i
                        dve.wait_ge(scored, h + 1)
                        if b >= 2:
                            dve.wait_ge(y_made, b - 1)
                        s = K.ps[:, 2 * (b % 2) + i, :]
                        p = probs[:, b % 2, i]
                        nc.vector.tensor_tensor(p[:, 0, 0:T], s[:, 0:T], decay_f[:, h, :], ALU.mult)
                        nc.vector.tensor_tensor(p[:, 0, T:3 * P], s[:, T + P:2 * T], decay_f[:, h, 0:P], ALU.mult)
                        nc.vector.tensor_tensor(p[:, 1, 0:P], s[:, 0:P], decay_b[:, h, P:T], ALU.mult)
                        nc.vector.tensor_tensor(p[:, 1, P:3 * P], s[:, T:2 * T], decay_b[:, h, :],
                                                ALU.mult).then_inc(masked, 1)

                mask(0)
                for b in range(4):
                    if b < 3:
                        mask(b + 1)
                    dve.wait_ge(rooted, b + 1)
                    n = square[:, b % 2, :]
                    link(nc.vector.reciprocal(root[:, b % 2, :], root[:, b % 2, :]))
                    nc.vector.tensor_tensor(n, K.ps[:, 4 + b % 2, :], root[:, b % 2, :], ALU.mult).then_inc(y_used, 1)
                    dve.wait_ge(y_used, b + 1)
                    link(nc.vector.tensor_tensor(n, n, K.gateT[:, b].rearrange("p d t -> p (d t)"), ALU.mult))
                    link(nc.vector.tensor_tensor(K.mixT[:, b, :], n[:, 0:T], n[:, T:2 * T], ALU.add))
    A.high = top
    A.low = K.after_mixT


def rwkv_constants(nc, K):
    A = K.A
    K.rwkv_low = A.low
    K.w0, K.w2, K.a2 = A.keep(H), A.keep(512), A.keep(512)
    K.g2 = A.keep(2, 512)
    K.vecs = A.keep(3, 4)
    K.dup_vecs = A.keep(3, H)
    K.masks = A.keep(8, C)
    K.reset = A.keep(2, T)
    K.stateT = A.keep(H, HD)
    K.fold = A.keep(HD)
    K.gn_eps = A.keep(1)
    with nc.cleanup_on_exit():
        landed, cleared, folded = K.sem("landed"), K.sem("cleared"), K.sem("folded")
        with nc.Block() as block:
            @block.sync
            def _(sp):
                small = ((K.w0, "rwkv_w0"), (K.w2, "rwkv_w2"), (K.a2[0:HD, :], "rwkv_a2"), (K.g2, "rwkv_g2"),
                         (K.vecs, "rwkv_vecs"), (K.dup_vecs, "rwkv_dup_vecs"), (K.masks, "rwkv_masks"))
                for dst, name in small:
                    sp.dma_start(dst, K.dram[name]).then_inc(landed, 16)
                sp.wait_ge(landed, 16 * len(small))

            @block.gpsimd
            def _(pool):
                nc.gpsimd.memset(K.stateT, 0.0)
                nc.gpsimd.memset(K.gn_eps, GN_EPS)
                nc.gpsimd.memset(K.reset, 1.0).then_inc(cleared, 1)
                pool.wait_ge(cleared, 1)
                nc.gpsimd.memset(K.reset.rearrange("p a (c t) -> p (a c) t", t=C)[:, :, 0:1], 0.0)

            @block.vector
            def _(dve):
                nc.vector.tensor_tensor(K.fold, K.ident[:, 0:HD], K.ident[:, HD:P], ALU.add).then_inc(folded, 1)


def rwkv_prepare_stage(nc, K, s):
    A = K.A
    lat = s == LAT
    K.dup_low = A.low
    K.da, K.db, K.dk, K.dv = (A.keep(H, T) for _ in range(4))
    K.dr = A.keep(H, T) if lat else None
    K.tot = A.keep(4, H)
    top = A.high
    inc, exc, einc = (A.temp(2, 2, T) for _ in range(3))
    kmod, bb, kk = (A.view(A.high + 4 * T * n, (4, T)) for n in range(3))
    iclr, t = A.temp(4, T), A.temp(4, T)
    sg = A.temp(H, T)
    tok = slice(T * s, T * s + T)
    k, v = K.rkT[:, :, tok], K.rvT[:, :, tok]
    wl, al = K.wlT[:, tok], K.alT[0:HD, tok]
    spread = lambda i: K.vecs[:, i, :].unsqueeze(2).broadcast_to([P, 4, T])
    pair = lambda x, p: x[:, 2 * p:2 * p + 2, :]
    RATE = float(np.exp(-0.5))

    with nc.cleanup_on_exit():
        tanhed, al_made, z_made, iclr_ready, sg_ready = (K.sem(f"s{s}_{n}") for n in
                                                         ("tanhed", "al_made", "z_made", "iclr_ready", "sg_ready"))
        sq_ready, ss_made, root_ready = (K.sem(f"s{s}_{n}") for n in ("sq_ready", "ss_made", "root_ready"))
        ready = {n: K.sem(f"s{s}_{n}_ready") for n in "abk"}
        dup = {n: K.sem(f"s{s}_{n}_dup_landed") for n in "abkvr"}
        sums_ready, exp_ready, scaled, dve_step = (K.sem(f"s{s}_{n}") for n in
                                                   ("sums_ready", "exp_ready", "scaled", "dve_step"))
        if lat:
            gl_ready = K.sem(f"s{s}_gl_ready")
        with nc.Block() as block:
            @block.sync
            def _(sp):
                def both_halves(dst, src, sem):
                    for i in range(2):
                        for d in range(2):
                            to = dst[HD * d:HD * d + HD].rearrange("p (b i) t -> p b i t", i=2)[:, :, i, :]
                            sp.dma_start(to, src[HD * i:HD * i + HD]).then_inc(sem, 16)

                both_halves(K.dv, v, dup["v"])
                if lat:
                    both_halves(K.dr, K.rT, dup["r"])
                sp.wait_ge(ready["a"], 1)
                both_halves(K.da, kk, dup["a"])
                sp.wait_ge(ready["b"], 1)
                both_halves(K.db, bb, dup["b"])
                sp.wait_ge(ready["k"], 1)
                both_halves(K.dk, kmod, dup["k"])
                for n in "abkvr" if lat else "abkv":
                    sp.wait_ge(dup[n], 64)

            @block.tensor
            def _(pe):
                for b in range(4):
                    last = nc.tensor.matmul(K.ps[:, b // 2, T * (b % 2):T * (b % 2) + T], K.a2[0:HD, P * b:P * b + P],
                                            al, start=True, stop=True)
                last.then_inc(al_made, 1)
                pe.wait_ge(tanhed, 1)
                for p in range(4):
                    for j in range(2):
                        for d in range(2):
                            rows = slice(HD * d, HD * d + HD)
                            h = 2 * p + j
                            last = nc.tensor.matmul(K.ps[rows, 4 + p, T * j:T * j + T], K.w2[rows, HD * h:HD * h + HD],
                                                    wl[rows], start=True, stop=True)
                    last.then_inc(z_made, 1)
                pe.wait_ge(sq_ready, 1)
                for i in range(2):
                    last = nc.tensor.matmul(K.ps[:, 2 + i, :], K.head_ones, t[:, 2 * i:2 * i + 2, :],
                                            start=True, stop=True)
                last.then_inc(ss_made, 1)

            @block.scalar
            def _(act):
                nc.scalar.activation(wl, wl, ACT.Tanh).then_inc(tanhed, 1)
                act.wait_ge(al_made, 1)
                for b in range(4):
                    nc.scalar.activation(iclr[:, b, :], K.ps[:, b // 2, T * (b % 2):T * (b % 2) + T], ACT.Sigmoid,
                                         bias=K.vecs[:, 0, b:b + 1]).then_inc(iclr_ready, 1)
                for h in range(H):
                    act.wait_ge(z_made, h // 2 + 1)
                    nc.scalar.activation(sg[:, h, :], K.ps[:, 4 + h // 2, T * (h % 2):T * (h % 2) + T], ACT.Sigmoid,
                                         bias=K.w0[:, h:h + 1]).then_inc(sg_ready, 1)
                if lat:
                    nc.scalar.activation(K.glT, K.glT, ACT.Sigmoid).then_inc(gl_ready, 1)
                act.wait_ge(ss_made, 1)
                for i in range(2):
                    nc.scalar.activation(t[:, 2 * i:2 * i + 2, :], K.ps[:, 2 + i, :].rearrange("p (b t) -> p b t", t=T),
                                         ACT.Sqrt).then_inc(root_ready, 1)
                for p in range(4):
                    act.wait_ge(sums_ready, p + 1)
                    if p == 3:
                        nc.scalar.activation(K.tot, K.tot, ACT.Exp, scale=-RATE)
                    if p >= 2:
                        act.wait_ge(scaled, p - 1)
                    nc.scalar.activation(einc[:, p % 2], inc[:, p % 2], ACT.Exp, scale=-RATE).then_inc(exp_ready, 1)
                    nc.scalar.activation(exc[:, p % 2], exc[:, p % 2], ACT.Exp, scale=-RATE).then_inc(exp_ready, 1)
                    act.wait_ge(exp_ready, 3 * p + 2)
                    nc.scalar.activation(inc[:, p % 2], inc[:, p % 2], ACT.Exp, scale=RATE).then_inc(exp_ready, 1)

            @block.vector
            def _(dve):
                link = chain(dve, dve_step)
                link(nc.vector.tensor_tensor(kk, k, spread(1), ALU.mult))
                nc.vector.tensor_tensor(t, kk, kk, ALU.mult).then_inc(sq_ready, 1)
                dve.wait_ge(root_ready, 2)
                link(nc.vector.tensor_scalar(t, t, 1e-12, None, ALU.max))
                link(nc.vector.reciprocal(t, t))
                nc.vector.scalar_tensor_tensor(kk, kk, -1.0, t, ALU.mult, ALU.mult).then_inc(ready["a"], 1)
                dve.wait_ge(ready["a"], 1)
                dve.wait_ge(iclr_ready, 4)
                nc.vector.scalar_tensor_tensor(bb, kk, -1.0, iclr, ALU.mult, ALU.mult).then_inc(ready["b"], 1)
                dve.wait_ge(ready["b"], 1)
                link(nc.vector.scalar_tensor_tensor(iclr, iclr, -1.0, spread(2), ALU.add, ALU.mult))
                nc.vector.scalar_tensor_tensor(kmod, iclr, 1.0, k, ALU.add, ALU.mult).then_inc(ready["k"], 1)
                for n in "ab":
                    dve.wait_ge(dup[n], 64)
                dve.wait_ge(dup["k"], 64)
                dve.wait_ge(dup["v"], 64)
                if lat:
                    dve.wait_ge(dup["r"], 64)
                lo, hi = slice(0, HD), slice(HD, P)

                def sums(p):
                    i, e = inc[:, p % 2], exc[:, p % 2]
                    dve.wait_ge(sg_ready, 2 * p + 2)
                    if p >= 2:
                        dve.wait_ge(scaled, p - 1)
                    g = pair(sg, p)
                    link(nc.vector.tensor_tensor_scan(i.rearrange("p a t -> p (a t)"),
                                                      K.reset.rearrange("p a t -> p (a t)"),
                                                      g.rearrange("p a t -> p (a t)"), 0.0, ALU.mult, ALU.add))
                    by_chunk = i.rearrange("p a (c t) -> p a c t", t=C)
                    ends = by_chunk[:, :, :, C - 1]
                    to = K.tot.rearrange("p c h -> p h c")[:, 2 * p:2 * p + 2, :]
                    link(nc.vector.tensor_copy(to[lo], ends[lo]))
                    link(nc.vector.tensor_copy(to[hi], ends[hi][:, :, ::-1]))
                    link(nc.vector.tensor_tensor(e[lo], i[lo], g[lo], ALU.subtract))
                    for j in range(2):
                        link(nc.vector.tensor_tensor(e[hi, j].rearrange("p (c t) -> p c t", t=C),
                                                     by_chunk[hi, j, :, C - 1:C].broadcast_to([HD, 4, C]),
                                                     by_chunk[hi, j], ALU.subtract))
                    nc.vector.tensor_tensor(i[hi], e[hi], g[hi], ALU.add).then_inc(sums_ready, 1)

                sums(0)
                for p in range(4):
                    if p < 3:
                        sums(p + 1)
                    dve.wait_ge(exp_ready, 3 * p + 3)
                    if lat:
                        nc.vector.tensor_tensor(pair(K.dr, p), pair(K.dr, p), einc[:, p % 2], ALU.mult)
                    nc.vector.tensor_tensor(pair(K.da, p), pair(K.da, p), exc[:, p % 2], ALU.mult)
                    nc.vector.tensor_tensor(pair(K.dk, p), pair(K.dk, p), inc[:, p % 2], ALU.mult)
                    nc.vector.tensor_tensor(pair(K.db, p), pair(K.db, p), inc[:, p % 2], ALU.mult).then_inc(scaled, 1)
    A.high = top


def rwkv_chunks_stage(nc, K, s):
    A = K.A
    lat = s == LAT
    if lat:
        K.y = A.temp(H, T)
    top = A.high
    vt, bt, kt, lak, tt = (A.temp(2, 512) for _ in range(5))
    arb, ark = (A.temp(2, 512), A.temp(2, 512)) if lat else (None, None)
    l_sb, u, t_sb = A.temp(512), A.temp(512), A.temp(512)
    lm, tt_wide = A.temp(2, 512), A.temp(H, P)
    x, sa = A.temp(512), A.temp(512)
    LEVELS = 5
    NS = T // C
    prep = [("l", "dve"), ("lt", "dve"), ("tv", "act"), ("lak", "dve")]
    fill = [("tb", "act"), ("tk", "act")] + ([("arb", "dve"), ("ark", "dve")] if lat else [])
    for m in range(LEVELS):
        prep += [(f"{n}{m}{g}", "act" if n == "w" else "dve") for g in range(2) for n in "wu"]
        prep += [(f"p{m}0", "dve")] + fill[m:m + 1] + [(f"p{m}1", "dve")]
    NP = len(prep)
    index = {job[0]: n for n, job in enumerate(prep)}
    jobs = prep * NS
    others = [sum(job[0][0] != "w" for job in jobs[:n]) for n in range(len(jobs))]
    banks = [int(job[0][2]) if job[0][0] == "w" else 2 + others[n] % 3 for n, job in enumerate(jobs)]
    ordinal = [sum(other[1] == job[1] for other in jobs[:n + 1]) for n, job in enumerate(jobs)]
    before = [max((m for m in range(n) if banks[m] == banks[n]), default=-1) for n in range(len(jobs))]
    order = [("prepare", 0, name) for name, _ in prep]
    for i in range(NS):
        rest = [("prepare", i + 1, name) for name, _ in prep] if i + 1 < NS else []
        order += rest[:7] + [("x", i, "")] + rest[7:13] + [("sa", i, "")] + rest[13:19] + [("state", i, "")] + rest[19:]

    heads = lambda ap: ap.rearrange("p (h e) -> p h e", e=HD)
    mask = lambda i, rows: K.masks[rows, i, :].unsqueeze(1).broadcast_to([rows.stop - rows.start, H, C])
    whole = slice(0, P)
    half = (slice(0, HD), slice(HD, P))
    bank_of = lambda i, name: banks[NP * i + index[name]]
    made_at = lambda i, name: NP * i + index[name] + 1

    with nc.cleanup_on_exit():
        cleared, made = K.sem(f"c{s}_cleared"), K.sem(f"c{s}_made")
        took = {"act": K.sem(f"c{s}_act_took"), "dve": K.sem(f"c{s}_dve_took")}
        lm_ready = K.sem(f"c{s}_lm_ready")
        x_made, x_taken, sa_made, sa_taken = (K.sem(f"c{s}_{n}") for n in ("x_made", "x_taken", "sa_made", "sa_taken"))
        y_made, y_taken, s_made, s_taken = (K.sem(f"c{s}_{n}") for n in ("y_made", "y_taken", "s_made", "s_taken"))
        dve_step = K.sem(f"c{s}_dve_step")
        state_read = y_made if lat else s_made
        with nc.Block() as block:
            @block.tensor
            def _(pe):
                def chunk(step, d):
                    c = step if d == 0 else NS - 1 - step
                    return slice(C * c, C * c + C)

                def each(bank, *terms, group=range(H)):
                    for h in group:
                        for d in range(2):
                            rows = half[d]
                            for n, (lhs, rhs) in enumerate(terms):
                                last = nc.tensor.matmul(K.ps[rows, bank, HD * h:HD * h + HD], lhs(rows, d, h), rhs(rows, d, h),
                                                        start=n == 0, stop=n == len(terms) - 1, skip_group_check=True)
                    return last

                def await_taken(i, name):
                    n = NP * i + index[name]
                    pe.wait_ge(took[jobs[n][1]], ordinal[n])

                channels = lambda t, i: lambda rows, d, h: t[rows, h, chunk(i, d)]
                square = lambda t: lambda rows, d, h: t[rows, HD * h:HD * h + HD]
                inverse = lambda rows, d, h: tt_wide[rows, h, HD * d:HD * d + HD]
                state = lambda rows, d, h: K.stateT[rows, h, :]

                def prepare(i, name):
                    n = NP * i + index[name]
                    if before[n] >= 0:
                        pe.wait_ge(took[jobs[before[n]][1]], ordinal[before[n]])
                    bank = banks[n]
                    m, g = (int(name[1]), int(name[2])) if name[1:].isdigit() else (0, 0)
                    group = range(4 * g, 4 * g + 4)
                    if name in ("tv", "tb", "tk"):
                        src = {"tv": K.dv, "tb": K.db, "tk": K.dk}[name]
                        last = each(bank, (channels(src, i), lambda rows, d, h: K.ident[rows, rows]))
                    elif name[0] == "w":
                        await_taken(i, f"p{m - 1}{g}" if m else "lt")
                        for h in group:
                            last = nc.tensor.transpose(K.ps[:, bank, P * (h % 4):P * (h % 4) + P], tt_wide[:, h, :], K.ident)
                    elif name[0] == "u":
                        pe.wait_ge(lm_ready, LEVELS * i + m + 1)
                        last = each(bank, (square(lm[:, m % 2]), inverse), group=group)
                    elif name[0] == "p":
                        await_taken(i, f"w{m}{g}")
                        await_taken(i, f"u{m}{g}")
                        last = each(bank, (square(t_sb), square(u)), group=group)
                    else:
                        one, other = {"l": (K.da, K.db), "lt": (K.db, K.da), "lak": (K.dk, K.da),
                                      "arb": (K.db, K.dr), "ark": (K.dk, K.dr)}[name]
                        last = each(bank, (channels(one, i), channels(other, i)))
                    last.then_inc(made, 1)

                pe.wait_ge(cleared, 1)
                for what, i, name in order:
                    par = i % 2
                    if what == "prepare":
                        prepare(i, name)
                    elif what == "x":
                        if i:
                            pe.wait_ge(s_taken, i)
                        await_taken(i, "lak")
                        await_taken(i, "tv")
                        each(5, (channels(K.da, i), state), (square(lak[:, par]), square(vt[:, par]))).then_inc(x_made, 1)
                    elif what == "sa":
                        pe.wait_ge(x_taken, i + 1)
                        await_taken(i, f"p{LEVELS - 1}1")
                        each(5, (square(tt[:, par]), square(x))).then_inc(sa_made, 1)
                    else:
                        pe.wait_ge(sa_taken, i + 1)
                        await_taken(i, "tk")
                        each(7, (square(bt[:, par]), square(sa)), (square(kt[:, par]), square(vt[:, par]))).then_inc(s_made, 1)
                        if lat:
                            await_taken(i, "ark")
                            if i:
                                pe.wait_ge(y_taken, i)
                            each(6, (state, channels(K.dr, i)), (square(sa), square(arb[:, par])),
                                 (square(vt[:, par]), square(ark[:, par]))).then_inc(y_made, 1)

            @block.scalar
            def _(act):
                for what, i, name in order:
                    if what == "prepare":
                        if jobs[index[name]][1] != "act":
                            continue
                        act.wait_ge(made, made_at(i, name))
                        b = bank_of(i, name)
                        if name[0] == "w":
                            group = slice(4 * int(name[2]), 4 * int(name[2]) + 4)
                            for d in range(2):
                                both = K.ps[half[d], b, :].rearrange("p (h e) -> p h e", e=P)
                                last = nc.scalar.activation(heads(t_sb[half[d]])[:, group], both[:, :, HD * d:HD * d + HD], ACT.Copy)
                        else:
                            if i >= 2:
                                act.wait_ge(state_read, i - 1)
                            dst = {"tv": vt, "tb": bt, "tk": kt}[name][:, i % 2]
                            last = nc.scalar.activation(dst, K.ps[:, b, :], ACT.Copy)
                        last.then_inc(took["act"], 1)
                    elif what == "x":
                        act.wait_ge(x_made, i + 1)
                        nc.scalar.activation(x, K.ps[:, 5, :], ACT.Copy).then_inc(x_taken, 1)
                    elif what == "sa":
                        act.wait_ge(sa_made, i + 1)
                        nc.scalar.activation(sa, K.ps[:, 5, :], ACT.Copy).then_inc(sa_taken, 1)
                    elif lat:
                        act.wait_ge(y_made, i + 1)
                        for d in range(2):
                            c = i if d == 0 else NS - 1 - i
                            last = nc.scalar.activation(K.y[half[d], :, C * c:C * c + C], heads(K.ps[half[d], 6, :]), ACT.Copy)
                        last.then_inc(y_taken, 1)

            @block.gpsimd
            def _(pool):
                nc.gpsimd.memset(tt_wide, 0.0).then_inc(cleared, 1)
                for i in range(NS):
                    pool.wait_ge(took["dve"], ordinal[NP * i + index["l"]])
                    for m in range(LEVELS):
                        if m >= 2:
                            pool.wait_ge(made, made_at(i, f"u{m - 2}1"))
                        nc.gpsimd.tensor_tensor(heads(lm[:, m % 2]), heads(l_sb), mask(m, whole), ALU.mult).then_inc(lm_ready, 1)

            @block.vector
            def _(dve):
                link = chain(dve, dve_step)
                dve.wait_ge(cleared, 1)
                for what, i, name in order:
                    if what == "prepare":
                        n = NP * i + index[name]
                        if jobs[n][1] != "dve":
                            continue
                        dve.wait_ge(made, n + 1)
                        src = K.ps[:, banks[n], :]
                        t = tt[:, i % 2]
                        group = slice(4 * int(name[2]), 4 * int(name[2]) + 4) if name[0] in "up" else slice(0, H)
                        diagonal = lambda d: tt_wide[half[d], group, HD * d:HD * d + HD]
                        if i >= 2 and name in ("lak", "arb", "ark", "lt"):
                            dve.wait_ge(state_read, i - 1)
                        if name == "l":
                            if i:
                                dve.wait_ge(lm_ready, LEVELS * i)
                            done = nc.vector.tensor_copy(l_sb, src)
                        elif name == "lt":
                            link(nc.vector.tensor_tensor(heads(t), heads(src), mask(5, whole), ALU.mult))
                            for d in range(2):
                                done = nc.vector.tensor_tensor(diagonal(d), heads(t[half[d]]),
                                                               K.fold[half[d]].unsqueeze(1).broadcast_to([HD, H, C]), ALU.add)
                        elif name == "lak":
                            done = nc.vector.tensor_tensor(heads(lak[:, i % 2]), heads(src), mask(6, whole), ALU.mult)
                        elif name in ("arb", "ark"):
                            dst = (arb if name == "arb" else ark)[:, i % 2]
                            done = nc.vector.tensor_tensor(heads(dst), heads(src), mask(7, whole), ALU.mult)
                        elif name[0] == "u":
                            done = nc.vector.tensor_copy(heads(u)[:, group], heads(src)[:, group])
                        else:
                            m = int(name[1])
                            dve.wait_ge(took["dve"], ordinal[NP * i + index[f"p{m - 1}{name[2]}" if m else "lt"]])
                            for d in range(2):
                                to = diagonal(d) if m < LEVELS - 1 else heads(t[half[d]])[:, group]
                                done = nc.vector.tensor_tensor(to, diagonal(d), heads(src[half[d]])[:, group], ALU.add)
                        done.then_inc(took["dve"], 1)
                    elif what == "state":
                        dve.wait_ge(state_read, i + 1)
                        st = K.stateT
                        link(nc.vector.tensor_tensor(st, st, heads(K.ps[:, 7, :]), ALU.add))
                        nc.vector.tensor_tensor(st, st, K.tot[:, i, :].unsqueeze(2).broadcast_to([P, H, HD]),
                                                ALU.mult).then_inc(s_taken, 1)
    A.high = top
    if not lat:
        A.low = K.dup_low


def rwkv_context(nc, K):
    rwkv_prepare_stage(nc, K, CTX)
    rwkv_chunks_stage(nc, K, CTX)


def rwkv_latent(nc, K):
    rwkv_prepare_stage(nc, K, LAT)
    K.A.high = K.A.t.shape[1]
    rwkv_chunks_stage(nc, K, LAT)


def rwkv_output(nc, K):
    A = K.A
    y = K.y
    g, bonus = K.da, K.db
    sq, root = A.keep(H, T), A.keep(H, T)
    per_head = lambda i: K.dup_vecs[:, i, :].unsqueeze(2).broadcast_to([P, H, T])
    part = lambda ap, n: ap[:, 2 * n:2 * n + 2, :]
    bank = lambda n: K.ps[:, n, :].rearrange("p (h t) -> p h t", t=T)
    with nc.cleanup_on_exit():
        mean_made, centred, squared, var_made, rooted, z_ready, folded, dve_step = (K.sem("o_" + n) for n in (
            "mean_made", "centred", "squared", "var_made", "rooted", "z_ready", "folded", "dve_step"))
        g_made, g_taken = K.sem("o_g_made"), K.sem("o_g_taken")
        prod_ready, bonus_made = K.sem("o_prod_ready"), K.sem("o_bonus_made")
        with nc.Block() as block:
            @block.tensor
            def _(pe):
                for n in range(4):
                    nc.tensor.matmul(bank(n), K.head_ones, part(y, n), start=True, stop=True).then_inc(mean_made, 1)
                for n in range(4):
                    pe.wait_ge(squared, n + 1)
                    nc.tensor.matmul(bank(4 + n), K.head_ones, part(sq, n), start=True, stop=True).then_inc(var_made, 1)
                for n in range(4):
                    pe.wait_ge(centred, n + 1)
                    for j in range(2):
                        for d in range(2):
                            h = 2 * n + j
                            last = nc.tensor.matmul(K.ps[HD * d:HD * d + HD, n, T * j:T * j + T],
                                                    K.g2[:, d, HD * h:HD * h + HD], K.glT[:, d, :],
                                                    start=True, stop=True)
                    last.then_inc(g_made, 1)
                pe.wait_ge(rooted, 4)
                for n in range(4):
                    pe.wait_ge(prod_ready, n + 1)
                    nc.tensor.matmul(bank(4 + n), K.head_ones, part(bonus, n), start=True, stop=True).then_inc(bonus_made, 1)
                pe.wait_ge(g_taken, 4)
                for n in range(4):
                    pe.wait_ge(z_ready, n + 1)
                    for i in range(2):
                        last = nc.tensor.matmul(K.ps[HD * i:HD * i + HD, n, 0:T], K.fold, y[:, 2 * n + i, :],
                                                start=True, stop=True)
                    last.then_inc(folded, 1)

            @block.scalar
            def _(act):
                for n in range(4):
                    act.wait_ge(centred, n + 1)
                    nc.scalar.activation(part(sq, n), part(y, n), ACT.Square).then_inc(squared, 1)
                for n in range(4):
                    act.wait_ge(var_made, n + 1)
                    nc.scalar.activation(part(root, n), bank(4 + n), ACT.Sqrt, bias=K.gn_eps[:, 0:1],
                                         scale=1.0 / HD).then_inc(rooted, 1)
                for n in range(4):
                    act.wait_ge(g_made, n + 1)
                    nc.scalar.activation(part(g, n), bank(n), ACT.Copy).then_inc(g_taken, 1)
                for n in range(4):
                    act.wait_ge(folded, n + 1)
                    nc.scalar.activation(K.mixT[:, 4 + n, :], K.ps[:, n, 0:T], ACT.Copy)

            @block.vector
            def _(dve):
                link = chain(dve, dve_step)
                for n in range(4):
                    dve.wait_ge(mean_made, n + 1)
                    nc.vector.scalar_tensor_tensor(part(y, n), bank(n), -1.0 / HD, part(y, n), ALU.mult,
                                                   ALU.add).then_inc(centred, 1)
                for n in range(4):
                    link(nc.vector.tensor_tensor(part(bonus, n), part(K.dr, n), part(per_head(0), n), ALU.mult))
                    nc.vector.tensor_tensor(part(bonus, n), part(bonus, n), part(K.dk, n), ALU.mult).then_inc(prod_ready, 1)
                dve.wait_ge(squared, 4)
                link(nc.vector.tensor_tensor(y, y, per_head(1), ALU.mult))
                for n in range(4):
                    dve.wait_ge(bonus_made, n + 1)
                    link(nc.vector.tensor_tensor(part(bonus, n), bank(4 + n), part(K.dv, n), ALU.mult))
                link(nc.vector.tensor_tensor(bonus, bonus, per_head(2), ALU.add))
                for n in range(4):
                    dve.wait_ge(rooted, n + 1)
                    link(nc.vector.reciprocal(part(root, n), part(root, n)))
                    link(nc.vector.tensor_tensor(part(y, n), part(y, n), part(root, n), ALU.mult))
                    link(nc.vector.tensor_tensor(part(y, n), part(y, n), part(bonus, n), ALU.add))
                    dve.wait_ge(g_taken, n + 1)
                    nc.vector.tensor_tensor(part(y, n), part(y, n), part(g, n), ALU.mult).then_inc(z_ready, 1)
    A.low = K.rwkv_low
    A.high = A.t.shape[1]


def mixers_out(nc, K):
    A, W = K.A, K.W
    K.x = A.keep(TT, D)
    K.gt2 = A.keep(D)
    K.base = A.low
    K.h2 = A.keep(TT, D)
    top = A.high
    cT = A.temp(KT * 2)
    cond = A.temp(KT, 32)
    part = A.temp(2, 512)
    brow = A.temp(4 * D)
    gains = A.temp(3, D)
    gt1, g2, sh2 = A.temp(D), A.temp(D), A.temp(D)
    mix, junk = A.temp(TT, D), A.temp(D)
    sums, ms, root = A.temp(6), A.temp(4), A.temp(4)
    with nc.cleanup_on_exit():
        small, silued, cond_ready = K.sem("small_landed"), K.sem("silued"), K.sem("cond_ready")
        mod_made, mix_made, part_made, part_kept = (K.sem(n) for n in ("mod_made", "mix_made", "part_made", "part_kept"))
        took, mix_kept, dve_step = K.sem("took"), K.sem("mix_kept"), K.sem("dve_step")
        ms_ready, rooted, x_ready, squared = K.sem("ms_ready"), K.sem("rooted"), K.sem("x_ready"), K.sem("squared")
        mod_bank = [0, 1, 6, 7, 0, 1, 2, 3]
        with nc.Block() as block:
            @block.sync
            def _(sp):
                sp.dma_start(cT, K.dram["cT"]).then_inc(small, 16)
                sp.dma_start(brow[0:1, :], K.dram["b_mod"][:, 2 * D:6 * D]).then_inc(small, 16)
                for n in range(3):
                    sp.dma_start(gains[:, n, :], K.dram["norm_gains"][n + 1, :].partition_broadcast(P)).then_inc(small, 16)
                sp.dma_start(K.x, K.dram["x"].rearrange("(t p) d -> p t d", p=P)).then_inc(small, 16)
                W.load_ahead(sp, 10)

            @block.tensor
            def _(pe):
                pe.wait_ge(small, 96)
                pe.wait_ge(cond_ready, 1)

                def partial(m, used):
                    if m >= 4:
                        pe.wait_ge(took, min(m - 3, 2))
                        if m >= 6:
                            pe.wait_ge(mix_kept, m - 5)
                    partial_modulation(nc, K, K.ps[:, mod_bank[m], :], cond, W.take(pe), brow[0:1, 512 * m:512 * m + 512],
                                       used).then_inc(part_made, 1)

                def combine(m):
                    pe.wait_ge(part_kept, m + 1)
                    nc.tensor.matmul(K.ps[:, mod_bank[m], :], K.sel[:, 1:2].broadcast_to([P, P]), part[:, m % 2, :],
                                     start=True, stop=True).then_inc(mod_made, 1)

                partial(0, None)
                for m in range(1, 8):
                    partial(m, W.used)
                    combine(m - 1)
                    if m > 1:
                        continue
                    for n in range(2):
                        w = W.take(pe)
                        for t in range(TT):
                            for k in range(KT):
                                last = nc.tensor.matmul(K.ps[:, 2 + 2 * n + t, :], K.mixT[:, k, P * t:P * t + P],
                                                        w[:, k, :], start=(k == 0), stop=(k == KT - 1))
                                if t == 0 and k == 0:
                                    last.then_inc(W.used, 1)
                            last.then_inc(mix_made, 1)
                combine(7)
                pe.wait_ge(mod_made, 8)
                nc.tensor.nop().then_inc(W.used, 1)

            @block.scalar
            def _(act):
                act.wait_ge(small, 96)
                nc.scalar.activation(cT, cT, ACT.Silu).then_inc(silued, 1)

                def keep_part(m):
                    act.wait_ge(part_made, m + 1)
                    if m >= 2:
                        act.wait_ge(mod_made, m - 1)
                    nc.scalar.activation(part[:, m % 2, :], K.ps[:, mod_bank[m], :], ACT.Copy).then_inc(part_kept, 1)

                keep_part(0)
                keep_part(1)
                for m in range(4):
                    n, t = m // 2, m % 2
                    act.wait_ge(mix_made, m + 1)
                    if m:
                        act.wait_ge(mix_kept, m)
                    nc.scalar.activation(junk[:, 0:512], K.ps[:, 2 + m, :], ACT.Square,
                                         accum_out=sums[:, 2 * t + n:2 * t + n + 1])
                    nc.scalar.activation(mix[:, t, 512 * n:512 * n + 512], K.ps[:, 2 + m, :], ACT.Copy).then_inc(mix_kept, 1)
                for m in range(2, 8):
                    keep_part(m)
                act.wait_ge(ms_ready, 1)
                nc.scalar.activation(root[:, 0:2], ms[:, 0:2], ACT.Sqrt).then_inc(rooted, 1)
                for t in range(TT):
                    act.wait_ge(x_ready, t + 1)
                    nc.scalar.activation(mix[:, t, :], K.x[:, t, :], ACT.Square,
                                         accum_out=sums[:, 4 + t:5 + t]).then_inc(squared, 1)
                act.wait_ge(ms_ready, 2)
                nc.scalar.activation(root[:, 2:4], ms[:, 2:4], ACT.Sqrt).then_inc(rooted, 1)

            @block.vector
            def _(dve):
                link = chain(dve, dve_step)
                dve.wait_ge(silued, 1)
                nc.vector.tensor_copy(cond, cT[:, KT:2 * KT].unsqueeze(2).broadcast_to([P, KT, 32])).then_inc(cond_ready, 1)
                count = 0
                for n in range(8):
                    half = slice(512 * (n % 2), 512 * (n % 2) + 512)
                    dve.wait_ge(mod_made, n + 1)
                    bank = K.ps[:, mod_bank[n], :]
                    if n < 2:
                        ins = nc.vector.tensor_tensor(gt1[:, half], bank, gains[:, 0, half], ALU.mult)
                    elif n < 4:
                        ins = nc.vector.tensor_copy(sh2[:, half], bank)
                    elif n < 6:
                        ins = nc.vector.scalar_tensor_tensor(g2[:, half], bank, 1.0, gains[:, 1, half], ALU.add, ALU.mult)
                    else:
                        ins = nc.vector.tensor_tensor(K.gt2[:, half], bank, gains[:, 2, half], ALU.mult)
                    count += 1
                    ins.then_inc(took, 1)
                dve.wait_ge(took, count)
                dve.wait_ge(mix_kept, 4)
                link(nc.vector.tensor_tensor(ms[:, 0:2], sums[:, 0:4:2], sums[:, 1:4:2], ALU.add))
                nc.vector.tensor_scalar(ms[:, 0:2], ms[:, 0:2], 1.0 / D, EPS, ALU.mult, ALU.add).then_inc(ms_ready, 1)
                dve.wait_ge(rooted, 1)
                link(nc.vector.reciprocal(root[:, 0:2], root[:, 0:2]))
                for t in range(TT):
                    link(nc.vector.scalar_tensor_tensor(mix[:, t, :], mix[:, t, :], root[:, t:t + 1], gt1,
                                                        ALU.mult, ALU.mult))
                    nc.vector.tensor_tensor(K.x[:, t, :], K.x[:, t, :], mix[:, t, :], ALU.add).then_inc(x_ready, 1)
                dve.wait_ge(squared, 2)
                nc.vector.tensor_scalar(ms[:, 2:4], sums[:, 4:6], 1.0 / D, EPS, ALU.mult, ALU.add).then_inc(ms_ready, 1)
                dve.wait_ge(rooted, 2)
                link(nc.vector.reciprocal(root[:, 2:4], root[:, 2:4]))
                for t in range(TT):
                    link(nc.vector.scalar_tensor_tensor(K.h2[:, t, :], K.x[:, t, :], root[:, 2 + t:3 + t], g2,
                                                        ALU.mult, ALU.mult))
                    link(nc.vector.tensor_tensor(K.h2[:, t, :], K.h2[:, t, :], sh2, ALU.add))
    A.high = top


def route(nc, K):
    A = K.A
    K.xsT = A.keep(KT, NE * CAP)
    K.scatter = A.keep(NE, T)
    top = A.high
    wr = A.temp(KT, NE)
    earlier = A.temp(TT, T)
    places = A.temp(CAP)
    h2T = A.temp(KT, T)
    aff, rank, tie = A.temp(TT, NE), A.temp(TT, NE), A.temp(TT, NE)
    affT = A.temp(T)
    all_aff = A.temp(NE * T)
    sel, weighted = A.temp(TT, NE * CAP), A.temp(TT, NE * CAP)
    spread = A.temp(2, 4, P)
    by_expert = all_aff.rearrange("p (e t) -> p e t", t=T)
    top8, total = A.temp(TT), A.temp(TT)
    junk, junk2 = A.temp(T), A.temp(T)
    rows = nc.dram_tensor("affinity_rows", (NE, T), F32).ap()
    with nc.cleanup_on_exit():
        rows_stored = K.sem("rows_stored")
        landed, t_made, t_kept = K.sem("landed"), K.sem("h2T_made"), K.sem("h2T_kept")
        logits, maxed, expd, aff_ready = K.sem("logits"), K.sem("maxed"), K.sem("expd"), K.sem("aff_ready")
        affT_made, affT_kept, spread_landed = K.sem("affT_made"), K.sem("affT_kept"), K.sem("affinities_landed")
        sel_ready, gathered, gather_kept = K.sem("sel_ready"), K.sem("gathered"), K.sem("gather_kept")
        wide_ready, wide_made, wide_kept, dve_step = (K.sem("wide_ready"), K.sem("wide_made"), K.sem("wide_kept"),
                                                      K.sem("dve_step"))
        with nc.Block() as block:
            @block.sync
            def _(sp):
                for dst, name in ((wr, "w_router"), (earlier, "earlier"), (places, "places")):
                    sp.dma_start(dst, K.dram[name]).then_inc(landed, 16)
                sp.wait_ge(affT_kept, 1)
                sp.dma_start(rows, affT[0:NE, :]).then_inc(rows_stored, 16)
                sp.wait_ge(rows_stored, 16)
                sp.dma_start(all_aff, rows.rearrange("e t -> (e t)").partition_broadcast(P)).then_inc(spread_landed, 16)

            @block.tensor
            def _(pe):
                for n in range(4):
                    t, q = n // 2, n % 2
                    for k in range(4):
                        c = P * (4 * q + k)
                        last = nc.tensor.transpose(K.ps[:, n, P * k:P * k + P], K.h2[:, t, c:c + P], K.ident)
                    last.then_inc(t_made, 1)
                pe.wait_ge(landed, 48)
                pe.wait_ge(t_kept, 4)
                for t in range(TT):
                    for k in range(KT):
                        last = nc.tensor.matmul(K.ps[:, 4, NE * t:NE * t + NE], h2T[:, k, P * t:P * t + P], wr[:, k, :],
                                                start=(k == 0), stop=(k == KT - 1))
                last.then_inc(logits, 1)
                pe.wait_ge(aff_ready, 1)
                for t in range(TT):
                    last = nc.tensor.transpose(K.ps[0:NE, 5, P * t:P * t + P], aff[:, t, :], K.ident)
                last.then_inc(affT_made, 1)
                pe.wait_ge(sel_ready, 2)
                for d in range(KT):
                    if d >= 4:
                        pe.wait_ge(gather_kept, d - 3)
                    for t in range(TT):
                        last = nc.tensor.matmul(K.ps[:, d % 4, :], K.h2[:, t, P * d:P * d + P], sel[:, t, :],
                                                start=(t == 0), stop=(t == 1))
                    last.then_inc(gathered, 1)
                for n in range(8):
                    if n >= 4:
                        pe.wait_ge(wide_kept, n - 3)
                    pe.wait_ge(wide_ready, n + 1)
                    for k in range(4):
                        last = nc.tensor.transpose(K.ps[:, 4 + n % 4, P * k:P * k + P], spread[:, n % 2, k, :], K.ident)
                    last.then_inc(wide_made, 1)

            @block.scalar
            def _(act):
                for n in range(4):
                    t, q = n // 2, n % 2
                    act.wait_ge(t_made, n + 1)
                    nc.scalar.activation(h2T[:, 4 * q:4 * q + 4, P * t:P * t + P],
                                         K.ps[:, n, :].rearrange("p (k t) -> p k t", t=P), ACT.Copy).then_inc(t_kept, 1)
                act.wait_ge(maxed, 1)
                for t in range(TT):
                    nc.scalar.activation(aff[:, t, :], K.ps[:, 4, NE * t:NE * t + NE], ACT.Exp, bias=top8[:, t:t + 1],
                                         accum_out=total[:, t:t + 1]).then_inc(expd, 1)
                act.wait_ge(affT_made, 1)
                nc.scalar.activation(affT[0:NE, :], K.ps[0:NE, 5, 0:T], ACT.Copy).then_inc(affT_kept, 1)
                for d in range(KT):
                    act.wait_ge(gathered, d + 1)
                    nc.scalar.activation(K.xsT[:, d, :], K.ps[:, d % 4, :], ACT.Copy).then_inc(gather_kept, 1)
                for n in range(8):
                    t, q = n // 4, n % 4
                    act.wait_ge(wide_made, n + 1)
                    nc.scalar.activation(K.scatter[:, 4 * q:4 * q + 4, P * t:P * t + P],
                                         K.ps[:, 4 + n % 4, :].rearrange("p (k t) -> p k t", t=P),
                                         ACT.Copy).then_inc(wide_kept, 1)

            @block.vector
            def _(dve):
                link = chain(dve, dve_step)
                dve.wait_ge(logits, 1)
                nc.vector.tensor_reduce(top8, K.ps[:, 4, 0:TT * NE].rearrange("p (t e) -> p t e", e=NE), AX, ALU.max,
                                        negate=True).then_inc(maxed, 1)
                dve.wait_ge(expd, 2)
                link(nc.vector.reciprocal(total, total))
                nc.vector.tensor_tensor(aff, aff, total.unsqueeze(2).broadcast_to([P, TT, NE]),
                                        ALU.mult).then_inc(aff_ready, 1)
                dve.wait_ge(aff_ready, 1)
                dve.wait_ge(spread_landed, 16)
                for t in range(TT):
                    for e in range(NE):
                        mine = aff[:, t, e:e + 1]
                        nc.vector.tensor_scalar(junk, by_expert[:, e, :], mine, 0.0, ALU.is_gt, ALU.add,
                                                accum_out=rank[:, t, e:e + 1])
                        link(nc.vector.scalar_tensor_tensor(junk2, by_expert[:, e, :], mine, earlier[:, t, :],
                                                            ALU.is_equal, ALU.mult, accum_out=tie[:, t, e:e + 1]))
                    link(nc.vector.tensor_tensor(rank[:, t, :], rank[:, t, :], tie[:, t, :], ALU.add))
                    nc.vector.tensor_tensor(sel[:, t, :].rearrange("p (e c) -> p e c", c=CAP),
                                            rank[:, t, :].unsqueeze(2).broadcast_to([P, NE, CAP]),
                                            places.unsqueeze(1).broadcast_to([P, NE, CAP]),
                                            ALU.is_equal).then_inc(sel_ready, 1)
                dve.wait_ge(sel_ready, 2)
                for t in range(TT):
                    link(nc.vector.tensor_tensor(weighted[:, t, :].rearrange("p (e c) -> p e c", c=CAP),
                                                 sel[:, t, :].rearrange("p (e c) -> p e c", c=CAP),
                                                 aff[:, t, :].unsqueeze(2).broadcast_to([P, NE, CAP]), ALU.mult))
                for n in range(8):
                    t, q = n // 4, n % 4
                    if n >= 2:
                        dve.wait_ge(wide_made, n - 1)
                    w = weighted[:, t, P * q:P * q + P].rearrange("p (e c) -> p e c", c=CAP)
                    nc.vector.tensor_copy(spread[:, n % 2].rearrange("p e (r c) -> p e r c", c=CAP),
                                          w.unsqueeze(2).broadcast_to([P, 4, 4, CAP])).then_inc(wide_ready, 1)
    A.high = top


def experts(nc, K):
    A, W = K.A, K.W
    top = A.high
    W.extra = A.temp(NX, SLOT)
    gu = A.temp(512)
    gate = A.temp(2, 4, CAP)
    hidT = A.temp(2, 4, CAP)
    parts = A.temp(2, 512)
    y, junk = K.h2, A.temp(512)
    sums, ms, root = A.temp(4), A.temp(2), A.temp(2)
    with nc.cleanup_on_exit():
        gu_made, gu_kept, gu_turned, gated, hid_ready = (K.sem(n) for n in (
            "gu_made", "gu_kept", "gu_turned", "gated", "hid_ready"))
        down_made, parts_kept, y_made, y_kept = K.sem("down_made"), K.sem("parts_kept"), K.sem("y_made"), K.sem("y_kept")
        ms_ready, rooted, dve_step = K.sem("ms_ready"), K.sem("rooted"), K.sem("dve_step")
        strip = lambda j: slice(CAP * j, CAP * j + CAP)
        with nc.Block() as block:
            @block.sync
            def _(sp):
                W.load_ahead(sp, 6 * NE)

            @block.tensor
            def _(pe):
                def scatter(e):
                    pe.wait_ge(parts_kept, e + 1)
                    for t in range(TT):
                        for n in range(2):
                            last = nc.tensor.matmul(K.ps[:, 2 * t + n, :], K.scatter[:, e, P * t:P * t + P],
                                                    parts[:, n, :], start=(e == 0), stop=(e == NE - 1))
                    last.then_inc(y_made, 1)

                for e in range(NE):
                    ws = [W.take(pe) for _ in range(4)]
                    if e:
                        pe.wait_ge(gu_kept, e)
                    for k in range(KT):
                        for j in range(4):
                            last = nc.tensor.matmul(K.ps[strip(j), 4, :], K.xsT[:, k, CAP * e:CAP * e + CAP],
                                                    ws[j][:, k, :], start=(k == 0), stop=(k == KT - 1),
                                                    skip_group_check=True)
                    last.then_inc(gu_made, 1)
                    if e:
                        scatter(e - 1)
                    pe.wait_ge(gu_kept, e + 1)
                    if e:
                        pe.wait_ge(hid_ready, e)
                    for c in range(4):
                        last = nc.tensor.transpose(K.ps[:, 5, P * c:P * c + P], gu[:, P * c:P * c + P], K.ident)
                        if c == 0:
                            last.then_inc(W.used, 4)
                    last.then_inc(gu_turned, 1)
                    wd = [W.take(pe) for _ in range(2)]
                    pe.wait_ge(hid_ready, e + 1)
                    if e:
                        pe.wait_ge(parts_kept, e)
                    for n in range(2):
                        for i in range(2):
                            for j in range(4):
                                k = 2 * j + i
                                last = nc.tensor.matmul(K.ps[strip(j), 6 + n, :], hidT[:, k // 4, k % 4, :],
                                                        wd[n][:, k, :], start=(i == 0), stop=(i == 1),
                                                        skip_group_check=True)
                    last.then_inc(down_made, 1)
                    pe.wait_ge(down_made, e + 1)
                    nc.tensor.nop().then_inc(W.used, 2)
                scatter(NE - 1)

            @block.scalar
            def _(act):
                for e in range(NE):
                    act.wait_ge(gu_turned, e + 1)
                    turned = K.ps[:, 5, :].rearrange("p (c j t) -> p j c t", j=4, t=CAP)
                    nc.scalar.activation(gate, turned[:, 0:2], ACT.Silu).then_inc(gated, 1)
                    act.wait_ge(down_made, e + 1)
                    if e:
                        act.wait_ge(y_made, e)
                    for n in range(2):
                        last = nc.scalar.activation(parts[:, n, :], K.ps[:, 6 + n, :], ACT.Copy)
                    last.then_inc(parts_kept, 1)
                act.wait_ge(y_made, NE)
                for m in range(4):
                    t, n = m // 2, m % 2
                    if m:
                        act.wait_ge(y_kept, m)
                    nc.scalar.activation(junk[:, 0:512], K.ps[:, m, :], ACT.Square, accum_out=sums[:, m:m + 1])
                    nc.scalar.activation(y[:, t, 512 * n:512 * n + 512], K.ps[:, m, :], ACT.Copy).then_inc(y_kept, 1)
                act.wait_ge(ms_ready, 1)
                nc.scalar.activation(root, ms, ACT.Sqrt).then_inc(rooted, 1)

            @block.vector
            def _(dve):
                link = chain(dve, dve_step)
                for e in range(NE):
                    dve.wait_ge(gu_made, e + 1)
                    if e:
                        dve.wait_ge(gu_turned, e)
                    nc.vector.tensor_copy(gu, K.ps[:, 4, :]).then_inc(gu_kept, 1)
                    dve.wait_ge(gated, e + 1)
                    if e:
                        dve.wait_ge(down_made, e)
                    turned = K.ps[:, 5, :].rearrange("p (c j t) -> p j c t", j=4, t=CAP)
                    nc.vector.tensor_tensor(hidT, gate, turned[:, 2:4], ALU.mult).then_inc(hid_ready, 1)
                dve.wait_ge(y_kept, 4)
                link(nc.vector.tensor_tensor(ms, sums[:, 0:4:2], sums[:, 1:4:2], ALU.add))
                nc.vector.tensor_scalar(ms, ms, 1.0 / D, EPS, ALU.mult, ALU.add).then_inc(ms_ready, 1)
                dve.wait_ge(rooted, 1)
                link(nc.vector.reciprocal(root, root))
                for t in range(TT):
                    link(nc.vector.scalar_tensor_tensor(y[:, t, :], y[:, t, :], root[:, t:t + 1], K.gt2,
                                                        ALU.mult, ALU.mult))
                    link(nc.vector.tensor_tensor(K.x[:, t, :], K.x[:, t, :], y[:, t, :], ALU.add))
    A.high = top
    A.low = K.base


def attention_inputs(nc, K, layer):
    A, W = K.A, K.W
    A.low = K.base
    K.zT = A.keep(16, T)
    K.ztok = A.keep(TT, 1280)
    K.zhigh = A.high
    top = A.high
    gain, h, hT = A.temp(D), A.temp(TT, D), A.temp(KT, T)
    sums, ms, root = A.temp(2), A.temp(2), A.temp(2)
    jobs = [(n // 4, "T", n % 4, T, K.zT[:, n, :]) for n in range(16)]
    for i, width in enumerate((512, 512, 256)):
        jobs += [(4 + i, "tok", t, width, K.ztok[:, t, 512 * i:512 * i + width]) for t in range(TT)]
    with nc.cleanup_on_exit():
        landed, squared, ms_ready, rooted, h_ready = (K.sem(n) for n in (
            "gain_landed", "squared", "ms_ready", "rooted", "h_ready"))
        t_made, t_kept, made, act_took, dve_took, dve_step = (K.sem(n) for n in (
            "t_made", "t_kept", "made", "act_took", "dve_took", "dve_step"))
        with nc.Block() as block:
            @block.sync
            def _(sp):
                sp.dma_start(gain, K.dram["norm_mix_2"][layer].partition_broadcast(P)).then_inc(landed, 16)
                W.load_ahead(sp, 7)

            @block.tensor
            def _(pe):
                for n in range(4):
                    t, q = n // 2, n % 2
                    pe.wait_ge(h_ready, t + 1)
                    for k in range(4):
                        c = P * (4 * q + k)
                        last = nc.tensor.transpose(K.ps[:, n, P * k:P * k + P], h[:, t, c:c + P], K.ident)
                    last.then_inc(t_made, 1)
                pe.wait_ge(t_kept, 4)
                for n, (s, kind, b, width, dst) in enumerate(jobs):
                    if n == 0 or jobs[n - 1][0] != s:
                        w = W.take(pe)
                    if n >= 8:
                        pe.wait_ge(dve_took if n % 2 else act_took, (n - 8) // 2 + 1)
                    for k in range(KT):
                        if kind == "T":
                            last = nc.tensor.matmul(K.ps[:, n % 8, 0:T], w[:, k, P * b:P * b + P], hT[:, k, :],
                                                    start=(k == 0), stop=(k == KT - 1))
                        else:
                            last = nc.tensor.matmul(K.ps[:, n % 8, 0:width], hT[:, k, P * b:P * b + P],
                                                    w[:, k, 0:width], start=(k == 0), stop=(k == KT - 1))
                        if k == 0 and n and jobs[n - 1][0] != s:
                            last.then_inc(W.used, 1)
                    last.then_inc(made, 1)
                pe.wait_ge(made, len(jobs))
                nc.tensor.nop().then_inc(W.used, 1)

            @block.scalar
            def _(act):
                for t in range(TT):
                    nc.scalar.activation(h[:, t, :], K.x[:, t, :], ACT.Square, accum_out=sums[:, t:t + 1]).then_inc(squared, 1)
                act.wait_ge(ms_ready, 1)
                nc.scalar.activation(root, ms, ACT.Sqrt).then_inc(rooted, 1)
                for n in range(4):
                    t, q = n // 2, n % 2
                    act.wait_ge(t_made, n + 1)
                    nc.scalar.activation(hT[:, 4 * q:4 * q + 4, P * t:P * t + P],
                                         K.ps[:, n, :].rearrange("p (k t) -> p k t", t=P), ACT.Copy).then_inc(t_kept, 1)
                for n, (s, kind, b, width, dst) in enumerate(jobs):
                    if n % 2 == 0:
                        act.wait_ge(made, n + 1)
                        nc.scalar.activation(dst, K.ps[:, n % 8, 0:width], ACT.Copy).then_inc(act_took, 1)

            @block.vector
            def _(dve):
                link = chain(dve, dve_step)
                dve.wait_ge(squared, 2)
                nc.vector.tensor_scalar(ms, sums, 1.0 / D, EPS, ALU.mult, ALU.add).then_inc(ms_ready, 1)
                dve.wait_ge(rooted, 1)
                link(nc.vector.reciprocal(root, root))
                dve.wait_ge(landed, 16)
                for t in range(TT):
                    nc.vector.scalar_tensor_tensor(h[:, t, :], K.x[:, t, :], root[:, t:t + 1], gain,
                                                   ALU.mult, ALU.mult).then_inc(h_ready, 1)
                for n, (s, kind, b, width, dst) in enumerate(jobs):
                    if n % 2:
                        dve.wait_ge(made, n + 1)
                        nc.vector.tensor_copy(dst, K.ps[:, n % 8, 0:width]).then_inc(dve_took, 1)
    A.high = top


def mixer_preparation(nc, K, layer):
    A = K.A
    zT, ztok = K.zT, K.ztok
    K.qrot = A.keep(2, T)
    K.mq = A.keep(2, 2, T)
    K.kcT = A.keep(16)
    K.vc = A.keep(HD)
    K.gates = A.keep(TT, 12)
    K.fsum = A.keep(TT, 4)
    K.igate = A.keep(TT, 4)
    K.nlam = A.keep(1)
    K.sub_g = A.keep(HD)
    K.head_g = A.keep(256)
    top = A.high
    cos64, sin64, cos32, sin32 = (A.temp(T) for _ in range(4))
    swap64, swap32, tri = A.temp(P), A.temp(P), A.temp(P)
    turned = A.temp(2, 512)
    cmp_w, pos = A.temp(2, 32, HD), A.temp(2, 32)
    blocks = A.temp(2, 32, 15)
    conv, wqk = A.temp(2, 5), A.temp(2, 2, HD)
    uc = A.temp(2, T)
    gate_b, lam = A.temp(8), A.temp(P)
    f, fa, lam2 = A.temp(TT, 4), A.temp(TT, 4), A.temp(HD)
    lsum = A.temp(2)
    lam_init = 0.8 - 0.6 * float(np.exp(-0.3 * layer))
    turns = [(zT[:, 0:2, :], K.qrot, swap64, cos64, sin64), (zT[:, 4:6, :], zT[:, 4:6, :], swap64, cos64, sin64),
             (zT[:, 12:14, :], zT[:, 12:14, :], swap64, cos64, sin64), (zT[:, 14:16, :], zT[:, 14:16, :], swap64, cos64, sin64),
             (zT[:, 6:8, :], zT[:, 6:8, :], swap32, cos32, sin32), (zT[:, 8:10, :], zT[:, 8:10, :], swap32, cos32, sin32)]
    dram = K.dram
    tables = [(cos64, dram["cos64"]), (sin64, dram["sin64"]), (cos32, dram["cos32"]), (sin32, dram["sin32"]),
              (swap64, dram["swap64"]), (swap32, dram["swap32"]), (tri, dram["tri"])]
    params = [(cmp_w, dram["nsa_cmp_w_2"][layer]), (pos, dram["nsa_cmp_pos_2"][layer]), (conv, dram["mlstm_conv_2"][layer]),
              (wqk, dram["mlstm_wqk_2"][layer]), (gate_b, dram["mlstm_gate_b_2"][layer].partition_broadcast(P)),
              (lam, dram["diff_lambda_2"][layer].partition_broadcast(P)),
              (K.sub_g, dram["diff_norm_2"][layer].partition_broadcast(P)),
              (K.head_g, dram["mlstm_norm_2"][layer].partition_broadcast(P))]
    with nc.cleanup_on_exit():
        tables_in, params_in, swapped, rotated = (K.sem(n) for n in ("tables_in", "params_in", "swapped", "rotated"))
        blocks_ready, compressed, cmp_kept = K.sem("blocks_ready"), K.sem("compressed"), K.sem("cmp_kept")
        uc_conv, uc_ready, mqk_made = K.sem("uc_conv"), K.sem("uc_ready"), K.sem("mqk_made")
        f_abs, f_exp, f_ln, lf_ready, f_made, act_step, dve_step = (K.sem(n) for n in (
            "f_abs", "f_exp", "f_ln", "lf_ready", "f_made", "act_step", "dve_step"))
        lam_ready, lam_exp = K.sem("lam_ready"), K.sem("lam_exp")
        with nc.Block() as block:
            @block.sync
            def _(sp):
                for dst, src in tables:
                    sp.dma_start(dst, src).then_inc(tables_in, 16)
                for dst, src in params:
                    sp.dma_start(dst, src).then_inc(params_in, 16)

            @block.tensor
            def _(pe):
                pe.wait_ge(tables_in, 16 * len(tables))
                for n in range(4):
                    nc.tensor.matmul(K.ps[:, n, :], turns[n][2], turns[n][0], start=True, stop=True).then_inc(swapped, 1)
                pe.wait_ge(params_in, 16 * len(params))
                pe.wait_ge(blocks_ready, 1)
                for i in range(2):
                    rows = slice(HD * i, HD * i + HD)
                    for l in range(32):
                        nc.tensor.matmul(K.ps[rows, 4, 0:15], cmp_w[rows, 0, l, :], blocks[rows, 0, l, :],
                                         start=(l == 0), stop=(l == 31))
                for l in range(32):
                    last = nc.tensor.matmul(K.ps[0:15, 5, 0:HD], blocks[0:HD, 1, l, :], cmp_w[0:HD, 1, l, :],
                                            start=(l == 0), stop=(l == 31))
                last.then_inc(compressed, 1)
                for n in range(4, 6):
                    pe.wait_ge(rotated, n - 3)
                    nc.tensor.matmul(K.ps[:, n % 4, :], turns[n][2], turns[n][0], start=True, stop=True).then_inc(swapped, 1)
                pe.wait_ge(uc_ready, 1)
                for i in range(2):
                    for b in range(2):
                        for j in range(2):
                            rows = slice(HD * j, HD * j + HD)
                            last = nc.tensor.matmul(K.ps[rows, 6 + i, T * b:T * b + T], wqk[rows, i, b, :], uc[rows, b, :],
                                                    start=True, stop=True)
                last.then_inc(mqk_made, 1)
                pe.wait_ge(lf_ready, 1)
                pe.wait_ge(cmp_kept, 1)
                nc.tensor.matmul(K.ps[:, 4, 0:4], tri, f[:, 0, :], start=True, stop=True)
                nc.tensor.matmul(K.ps[:, 4, 4:8], K.ones, f[:, 0, :], start=True, stop=False)
                nc.tensor.matmul(K.ps[:, 4, 4:8], tri, f[:, 1, :], start=False, stop=True).then_inc(f_made, 1)

            @block.scalar
            def _(act):
                act.wait_ge(uc_conv, 1)
                nc.scalar.activation(uc, uc, ACT.Silu).then_inc(uc_ready, 1)
                nc.scalar.activation(K.gates, ztok[:, :, 128:140], ACT.Sigmoid)
                nc.scalar.activation(ztok[:, :, 768:1024], ztok[:, :, 768:1024], ACT.Sigmoid)
                act.wait_ge(compressed, 1)
                nc.scalar.activation(K.kcT[:, 0:15], K.ps[:, 4, 0:15], ACT.Copy)
                nc.scalar.activation(K.vc[0:15, :], K.ps[0:15, 5, 0:HD], ACT.Copy).then_inc(cmp_kept, 1)
                act.wait_ge(mqk_made, 1)
                nc.scalar.activation(K.mq[:, 0], K.ps[:, 6, :].rearrange("p (b t) -> p b t", t=T), ACT.Copy)
                nc.scalar.activation(K.mq[:, 1], K.ps[:, 7, :].rearrange("p (b t) -> p b t", t=T), ACT.Copy,
                                     scale=HD ** -0.5)
                act.wait_ge(f_abs, 1)
                nc.scalar.activation(fa, fa, ACT.Exp, scale=-1.0).then_inc(f_exp, 1)
                act.wait_ge(lam_ready, 1)
                nc.scalar.activation(lsum, lsum, ACT.Exp).then_inc(lam_exp, 1)
                act.wait_ge(f_exp, 1)
                nc.scalar.activation(fa, fa, ACT.Ln, bias=K.ones[:, 0:1]).then_inc(f_ln, 1)

            @block.vector
            def _(dve):
                link = chain(dve, dve_step)

                def rotate(n):
                    src, dst, _, cos, sin = turns[n]
                    wide = [P, 2, T]
                    dve.wait_ge(swapped, n + 1)
                    t = turned[:, n % 2, :].rearrange("p (b t) -> p b t", b=2)
                    link(nc.vector.tensor_tensor(t, K.ps[:, n % 4, :].rearrange("p (b t) -> p b t", b=2),
                                                 sin.unsqueeze(1).broadcast_to(wide), ALU.mult))
                    link(nc.vector.tensor_tensor(dst, src, cos.unsqueeze(1).broadcast_to(wide), ALU.mult))
                    nc.vector.tensor_tensor(dst, dst, t, ALU.add).then_inc(rotated, 1)

                dve.wait_ge(params_in, 16 * len(params))
                for i in range(2):
                    for half in range(2):
                        view = zT[:, 2 + i, 16 * half:16 * half + 240].rearrange("p (n l) -> p l n", l=16)
                        last = nc.vector.tensor_tensor(blocks[:, i, 16 * half:16 * half + 16, :], view,
                                                       pos[:, i, 16 * half:16 * half + 16].unsqueeze(2)
                                                       .broadcast_to([P, 16, 15]), ALU.add)
                last.then_inc(blocks_ready, 1)
                for b in range(2):
                    u, o = zT[:, 10 + b, :], uc[:, b, :]
                    link(nc.vector.tensor_scalar(o, u, conv[:, b, 3:4], conv[:, b, 4:5], ALU.mult, ALU.add))
                    for tap in range(3):
                        by = 3 - tap
                        ins = nc.vector.scalar_tensor_tensor(o[:, by:T], u[:, 0:T - by], conv[:, b, tap:tap + 1],
                                                             o[:, by:T], ALU.mult, ALU.add)
                        if b == 1 and tap == 2:
                            ins.then_inc(uc_conv, 1)
                        else:
                            link(ins)
                for n in range(4):
                    rotate(n)
                per_tile = lambda at: gate_b[:, at:at + 4].unsqueeze(1).broadcast_to([P, TT, 4])
                link(nc.vector.tensor_tensor(f, ztok[:, :, 144:148], per_tile(4), ALU.add))
                link(nc.vector.tensor_tensor(K.igate, ztok[:, :, 140:144], per_tile(0), ALU.add))
                link(nc.vector.tensor_scalar(fa, f, -1.0, None, ALU.mult))
                nc.vector.tensor_tensor(fa, fa, f, ALU.max).then_inc(f_abs, 1)
                for i in range(2):
                    link(nc.vector.tensor_tensor(lam2[:, 32 * i:32 * i + 32], lam[:, 64 * i:64 * i + 32],
                                                 lam[:, 64 * i + 32:64 * i + 64], ALU.mult))
                nc.vector.tensor_reduce(lsum, lam2.rearrange("p (i d) -> p i d", i=2), AX, ALU.add).then_inc(lam_ready, 1)
                link(nc.vector.tensor_scalar(f, f, 0.0, None, ALU.min))
                dve.wait_ge(f_ln, 1)
                nc.vector.tensor_tensor(f, f, fa, ALU.subtract).then_inc(lf_ready, 1)
                dve.wait_ge(lam_exp, 1)
                link(nc.vector.tensor_tensor(K.nlam, lsum[:, 1:2], lsum[:, 0:1], ALU.subtract))
                link(nc.vector.tensor_scalar(K.nlam, K.nlam, -lam_init, None, ALU.add))
                for n in range(4, 6):
                    rotate(n)
                dve.wait_ge(f_made, 1)
                link(nc.vector.tensor_copy(K.fsum, K.ps[:, 4, 0:8].rearrange("p (t h) -> p t h", h=4)))
                link(nc.vector.tensor_tensor(K.igate, K.igate, K.fsum, ALU.subtract))
    A.high = top


def attention(nc, K, layer):
    A = K.A
    zT, ztok = K.zT, K.ztok
    K.o = A.keep(TT, D)
    K.den = A.keep(TT, 4)
    K.em = A.keep(TT, 4)
    top = A.high
    bias = A.temp(2, TT, T)
    cmp_bias, cmp_on = A.temp(TT, 16), A.temp(TT, 16)
    scores = A.temp(2, 8, T)
    probsT = A.temp(2, 8, P)
    nmax, z, coef = A.temp(2, 8), A.temp(2, 8), A.temp(2, 4)
    tmp, negm = A.temp(256), A.temp(2, 4)
    units = [(kind, t) for kind in ("cmp", "slc", "win", "dil", "diff", "mlstm") for t in range(TT)]
    NU = len(units)
    heads_of = {"cmp": 4, "slc": 4, "win": 4, "dil": 4, "diff": 8, "mlstm": 4}
    wide = lambda u: units[u][0] in ("diff", "mlstm")
    base = lambda u: 0 if wide(u) else 2 * (u % 2)
    keys = lambda u: 16 if units[u][0] == "cmp" else P * (units[u][1] + 1)
    scale = {"cmp": HD ** -0.5, "slc": HD ** -0.5, "win": HD ** -0.5, "dil": HD ** -0.5, "diff": 32 ** -0.5}
    order = [0, 2, 1, 3]
    col = {"cmp": 0, "slc": 0, "win": 0, "diff": 256, "mlstm": 512, "dil": 768}

    with nc.cleanup_on_exit():
        masks_in, scored, scores_read, maxed, expd, p_ready = (K.sem(n) for n in (
            "masks_in", "scored", "scores_read", "maxed", "expd", "p_ready"))
        turned, pt_kept, pv_made, o_taken, dve_step, negm_ready = (K.sem(n) for n in (
            "turned", "pt_kept", "pv_made", "o_taken", "dve_step", "negm_ready"))
        with nc.Block() as block:
            @block.sync
            def _(sp):
                for dst, name in ((bias, "attn_bias"), (cmp_bias, "cmp_bias"), (cmp_on, "cmp_on")):
                    sp.dma_start(dst, K.dram[name]).then_inc(masks_in, 16)

            @block.tensor
            def _(pe):
                def score(u):
                    kind, t = units[u]
                    n = keys(u)
                    if u and (wide(u) or wide(u - 1)):
                        pe.wait_ge(scores_read, u)
                    elif u >= 2:
                        pe.wait_ge(scores_read, u - 1)
                    q = slice(P * t, P * t + P)
                    if kind == "diff":
                        for b in range(2):
                            for s in range(4):
                                rows = slice(32 * s, 32 * s + 32)
                                last = nc.tensor.matmul(K.ps[:, s, T * b:T * b + n], zT[rows, 6 + b, q], zT[rows, 8 + b, 0:n],
                                                        start=True, stop=True, tile_position=(32 * s, 0))
                    else:
                        for h in range(4):
                            rows = slice(HD * (h % 2), HD * (h % 2) + HD)
                            b = h // 2
                            lhs, rhs = {"cmp": lambda: (zT[rows, b, q], K.kcT[rows, 0:15]),
                                        "slc": lambda: (K.qrot[rows, b, q], zT[rows, 4, 0:n]),
                                        "win": lambda: (K.qrot[rows, b, q], zT[rows, 5, 0:n]),
                                        "dil": lambda: (zT[rows, 12 + b, q], zT[rows, 14 + b, 0:n]),
                                        "mlstm": lambda: (K.mq[rows, 0, b, q], K.mq[rows, 1, b, 0:n])}[kind]()
                            wid = 15 if kind == "cmp" else n
                            last = nc.tensor.matmul(K.ps[:, base(u) + h % 2, T * b:T * b + wid], lhs, rhs,
                                                    start=True, stop=True)
                    if kind == "mlstm":
                        for h in range(4):
                            for k in range(t + 1):
                                at = T * (h // 2) + P * k
                                last = nc.tensor.matmul(K.ps[:, 2 + h % 2, at:at + P],
                                                        K.igate[:, k, h:h + 1].broadcast_to([P, P]), K.ident,
                                                        start=True, stop=True)
                    last.then_inc(scored, 1)

                def turn(u):
                    kind, t = units[u]
                    pe.wait_ge(p_ready, u + 1)
                    if u:
                        pe.wait_ge(pt_kept, u)
                    for j in range(4):
                        if kind == "cmp":
                            last = nc.tensor.transpose(K.ps[0:16, 4, P * j:P * j + P], scores[:, u % 2, j, 0:16], K.ident)
                        else:
                            for k in range(t + 1):
                                n = (t + 1) * j + k
                                last = nc.tensor.transpose(K.ps[:, 4 + n // 4, P * (n % 4):P * (n % 4) + P],
                                                           scores[:, u % 2, j, P * k:P * k + P], K.ident)
                    last.then_inc(turned, 1)

                def values(u):
                    kind, t = units[u]
                    pe.wait_ge(pt_kept, u + 1)
                    if u >= 2:
                        pe.wait_ge(o_taken, u - 1)
                    bank = 6 + u % 2
                    for j in range(4):
                        h = order[j]
                        out = K.ps[:, bank, HD * h:HD * h + HD]
                        if kind == "cmp":
                            last = nc.tensor.matmul(out, probsT[0:15, u % 2, j, :], K.vc[0:15, :], start=True, stop=True)
                            continue
                        for k in range(t + 1):
                            v = {"slc": lambda: ztok[:, k, 0:64], "win": lambda: ztok[:, k, 64:128],
                                 "diff": lambda: ztok[:, k, 256 + HD * h:256 + HD * h + HD],
                                 "mlstm": lambda: ztok[:, k, 512 + HD * h:512 + HD * h + HD],
                                 "dil": lambda: ztok[:, k, 1024 + HD * h:1024 + HD * h + HD]}[kind]()
                            last = nc.tensor.matmul(out, probsT[:, u % 2, (t + 1) * j + k, :], v,
                                                    start=(k == 0), stop=(k == t))
                    last.then_inc(pv_made, 1)

                score(0)
                score(1)
                for u in range(NU):
                    turn(u)
                    early = u + 2 < NU and not (wide(u + 1) or wide(u + 2))
                    if early:
                        score(u + 2)
                    values(u)
                    if u + 2 < NU and not early:
                        score(u + 2)

            @block.scalar
            def _(act):
                def exps(u):
                    kind, t = units[u]
                    n = keys(u)
                    act.wait_ge(maxed, u + 1)
                    for j in range(heads_of[kind]):
                        s = scores[:, u % 2, j, 0:n]
                        if kind in ("cmp", "mlstm"):
                            last = nc.scalar.activation(s, s, ACT.Exp, bias=nmax[:, u % 2, j:j + 1])
                        else:
                            last = nc.scalar.activation(s, s, ACT.Exp, bias=nmax[:, u % 2, j:j + 1],
                                                        accum_out=z[:, u % 2, j:j + 1])
                    if kind == "mlstm":
                        last = nc.scalar.activation(K.em[:, t, :], negm[:, t, :], ACT.Exp)
                    last.then_inc(expd, 1)

                def keep(u):
                    kind, t = units[u]
                    act.wait_ge(turned, u + 1)
                    if u >= 2:
                        act.wait_ge(pv_made, u - 1)
                    if kind == "cmp":
                        last = nc.scalar.activation(probsT[0:16, u % 2, 0:4, :], K.ps[0:16, 4, :]
                                                    .rearrange("p (n q) -> p n q", q=P), ACT.Copy)
                    else:
                        for i in range(t + 1):
                            last = nc.scalar.activation(probsT[:, u % 2, 4 * i:4 * i + 4, :], K.ps[:, 4 + i, :]
                                                        .rearrange("p (n q) -> p n q", q=P), ACT.Copy)
                    last.then_inc(pt_kept, 1)

                exps(0)
                for u in range(NU):
                    keep(u)
                    if u + 1 < NU:
                        exps(u + 1)

            @block.vector
            def _(dve):
                link = chain(dve, dve_step)

                def maxima(u):
                    kind, t = units[u]
                    n, nh = keys(u), heads_of[kind]
                    dve.wait_ge(scored, u + 1)
                    if u >= 2:
                        dve.wait_ge(turned, u - 1)
                    s = scores[:, u % 2, 0:nh, 0:n]
                    if kind == "mlstm":
                        src = K.ps[:, 2:4, :].rearrange("p a (b t) -> p (a b) t", t=T)
                        link(nc.vector.scalar_tensor_tensor(s, src[:, :, 0:n], 1.0, bias[:, 0, t, 0:n].unsqueeze(1)
                                                            .broadcast_to([P, 4, n]), ALU.mult, ALU.add))
                        link(nc.vector.tensor_reduce(nmax[:, u % 2, 0:4], s, AX, ALU.max, negate=True))
                        link(nc.vector.tensor_scalar(nmax[:, u % 2, 0:4], nmax[:, u % 2, 0:4], 0.0, None, ALU.min))
                        by_head = nmax[:, u % 2, 0:4].rearrange("p (a b) -> p b a", a=2)
                        nc.vector.tensor_tensor(negm[:, t, :].rearrange("p (b a) -> p b a", a=2), by_head,
                                                K.fsum[:, t, :].rearrange("p (b a) -> p b a", a=2),
                                                ALU.subtract).then_inc(maxed, 1)
                        return
                    a = base(u)
                    src = K.ps[:, a:a + nh // 2, :].rearrange("p a (b t) -> p (a b) t", t=T)
                    if kind == "cmp":
                        link(nc.vector.memset(s[:, :, 15:16], NEG))
                        s, src, m = s[:, :, 0:15], src[:, :, 0:15], cmp_bias[:, t, 0:15]
                        n = 15
                    else:
                        src, m = src[:, :, 0:n], bias[:, 1 if kind == "dil" else 0, t, 0:n]
                    nc.vector.scalar_tensor_tensor(s, src, scale[kind], m.unsqueeze(1).broadcast_to([P, nh, n]),
                                                   ALU.mult, ALU.add).then_inc(scores_read, 1)
                    dve.wait_ge(scores_read, u + 1)
                    nc.vector.tensor_reduce(nmax[:, u % 2, 0:nh], s, AX, ALU.max, negate=True).then_inc(maxed, 1)

                def weigh(u):
                    kind, t = units[u]
                    n = keys(u)
                    dve.wait_ge(expd, u + 1)
                    s = scores[:, u % 2]
                    if kind == "cmp":
                        link(nc.vector.tensor_tensor(s[:, 0:4, 0:16], s[:, 0:4, 0:16], cmp_on[:, t, :].unsqueeze(1)
                                                     .broadcast_to([P, 4, 16]), ALU.mult))
                        link(nc.vector.tensor_reduce(z[:, u % 2, 0:4], s[:, 0:4, 0:16], AX, ALU.add))
                        nc.vector.tensor_scalar(z[:, u % 2, 0:4], z[:, u % 2, 0:4], 1e-30, None,
                                                ALU.max).then_inc(p_ready, 1)
                        dve.wait_ge(p_ready, u + 1)
                        link(nc.vector.reciprocal(z[:, u % 2, 0:4], z[:, u % 2, 0:4]))
                        link(nc.vector.tensor_copy(coef[:, u % 2, :].rearrange("p (b a) -> p a b", a=2),
                                                   z[:, u % 2, 0:4].rearrange("p (a b) -> p a b", a=2)))
                    elif kind == "diff":
                        zz = z[:, u % 2]
                        link(nc.vector.reciprocal(zz, zz))
                        for i in range(2):
                            at = 2 * (2 * i + 1)
                            link(nc.vector.tensor_scalar(zz[:, at:at + 2], zz[:, at:at + 2], K.nlam[:, 0:1], None, ALU.mult))
                        for i in range(2):
                            for b in range(2):
                                p0, p1 = 4 * i + b, 4 * i + 2 + b
                                link(nc.vector.tensor_scalar(s[:, p1, 0:n], s[:, p1, 0:n], zz[:, p1:p1 + 1], None, ALU.mult))
                                ins = nc.vector.scalar_tensor_tensor(s[:, 2 * i + b, 0:n], s[:, p0, 0:n], zz[:, p0:p0 + 1],
                                                                     s[:, p1, 0:n], ALU.mult, ALU.add)
                                if i == 1 and b == 1:
                                    ins.then_inc(p_ready, 1)
                                    dve.wait_ge(p_ready, u + 1)
                                else:
                                    link(ins)
                    elif kind == "mlstm":
                        qk = K.ps[:, 0:2, :].rearrange("p a (b t) -> p (a b) t", t=T)
                        nc.vector.tensor_tensor(s[:, 0:4, 0:n], s[:, 0:4, 0:n], qk[:, :, 0:n], ALU.mult).then_inc(scores_read, 1)
                        dve.wait_ge(scores_read, u + 1)
                        by_head = K.den[:, t, :].rearrange("p (b a) -> p a b", a=2)
                        nc.vector.tensor_reduce(by_head, s[:, 0:4, 0:n].rearrange("p (a b) t -> p a b t", a=2), AX,
                                                ALU.add).then_inc(p_ready, 1)
                        dve.wait_ge(p_ready, u + 1)
                    else:
                        link(nc.vector.reciprocal(z[:, u % 2, 0:4], z[:, u % 2, 0:4]))
                        nc.vector.tensor_copy(coef[:, u % 2, :].rearrange("p (b a) -> p a b", a=2),
                                              z[:, u % 2, 0:4].rearrange("p (a b) -> p a b", a=2)).then_inc(p_ready, 1)
                        dve.wait_ge(p_ready, u + 1)

                def output(u):
                    kind, t = units[u]
                    c = coef[:, u % 2, :]
                    if kind in ("cmp", "slc", "win"):
                        g = {"cmp": 0, "slc": 4, "win": 8}[kind]
                        link(nc.vector.tensor_tensor(c, c, K.gates[:, t, g:g + 4], ALU.mult))
                    dve.wait_ge(pv_made, u + 1)
                    dst = K.o[:, t, col[kind]:col[kind] + 256].rearrange("p (h e) -> p h e", e=HD)
                    src = K.ps[:, 6 + u % 2, 0:256].rearrange("p (h e) -> p h e", e=HD)
                    if kind in ("diff", "mlstm"):
                        nc.vector.tensor_copy(dst, src).then_inc(o_taken, 1)
                        return
                    by = c.unsqueeze(2).broadcast_to([P, 4, HD])
                    if kind in ("slc", "win"):
                        part = tmp.rearrange("p (h e) -> p h e", e=HD)
                        nc.vector.tensor_tensor(part, src, by, ALU.mult).then_inc(o_taken, 1)
                        dve.wait_ge(o_taken, u + 1)
                        link(nc.vector.tensor_tensor(dst, dst, part, ALU.add))
                    else:
                        nc.vector.tensor_tensor(dst, src, by, ALU.mult).then_inc(o_taken, 1)
                        dve.wait_ge(o_taken, u + 1)

                dve.wait_ge(masks_in, 48)
                maxima(0)
                for u in range(NU):
                    weigh(u)
                    if u + 1 < NU:
                        maxima(u + 1)
                    if u:
                        output(u - 1)
                output(NU - 1)
    A.high = top


def attention_out(nc, K, layer):
    A, W = K.A, K.W
    top = A.high
    sq, den = A.temp(TT, 512), A.temp(TT, 4)
    ss, root = A.temp(TT, 8), A.temp(TT, 8)
    lam_init = 0.8 - 0.6 * float(np.exp(-0.3 * layer))
    ztok, o = K.ztok, K.o
    with nc.cleanup_on_exit():
        ms_ready, rooted, o_ready, t_made, t_kept, made, dve_step = (K.sem(n) for n in (
            "ms_ready", "rooted", "o_ready", "t_made", "t_kept", "made", "dve_step"))
        with nc.Block() as block:
            @block.sync
            def _(sp):
                W.load_ahead(sp, 2)

            @block.tensor
            def _(pe):
                pe.wait_ge(o_ready, 1)
                for n in range(4):
                    t, q = n // 2, n % 2
                    for k in range(4):
                        c = P * (4 * q + k)
                        last = nc.tensor.transpose(K.ps[:, n, P * k:P * k + P], o[:, t, c:c + P], K.ident)
                    last.then_inc(t_made, 1)
                pe.wait_ge(t_kept, 4)
                for n in range(2):
                    w = W.take(pe)
                    for t in range(TT):
                        for k in range(KT):
                            last = nc.tensor.matmul(K.ps[:, 4 + 2 * t + n, :], K.mixT[:, k, P * t:P * t + P], w[:, k, :],
                                                    start=(k == 0), stop=(k == KT - 1))
                            if n and t == 0 and k == 0:
                                last.then_inc(W.used, 1)
                        last.then_inc(made, 1)
                pe.wait_ge(made, 4)
                nc.tensor.nop().then_inc(W.used, 1)

            @block.scalar
            def _(act):
                act.wait_ge(ms_ready, 1)
                nc.scalar.activation(root, ss, ACT.Sqrt).then_inc(rooted, 1)
                for n in range(4):
                    t, q = n // 2, n % 2
                    act.wait_ge(t_made, n + 1)
                    nc.scalar.activation(K.mixT[:, 4 * q:4 * q + 4, P * t:P * t + P],
                                         K.ps[:, n, :].rearrange("p (k t) -> p k t", t=P), ACT.Copy).then_inc(t_kept, 1)

            @block.vector
            def _(dve):
                link = chain(dve, dve_step)
                heads = lambda ap: ap.rearrange("p (h e) -> p h e", e=HD)
                link(nc.vector.tensor_scalar(den, K.den, -1.0, None, ALU.mult))
                link(nc.vector.tensor_tensor(den, den, K.den, ALU.max))
                link(nc.vector.tensor_tensor(den, den, K.em, ALU.max))
                link(nc.vector.reciprocal(den, den))
                for t in range(TT):
                    h = heads(o[:, t, 512:768])
                    link(nc.vector.tensor_tensor(h, h, den[:, t, :].unsqueeze(2).broadcast_to([P, 4, HD]), ALU.mult))
                    both = o[:, t, 256:768]
                    link(nc.vector.tensor_tensor(sq[:, t, :], both, both, ALU.mult))
                    link(nc.vector.tensor_reduce(ss[:, t, :], heads(sq[:, t, :]), AX, ALU.add))
                nc.vector.tensor_scalar(ss, ss, 1.0 / HD, EPS, ALU.mult, ALU.add).then_inc(ms_ready, 1)
                dve.wait_ge(rooted, 1)
                link(nc.vector.reciprocal(root, root))
                link(nc.vector.tensor_scalar(root[:, :, 0:4], root[:, :, 0:4], 1.0 - lam_init, None, ALU.mult))
                link(nc.vector.tensor_tensor(ztok[:, :, 768:1024], ztok[:, :, 768:1024],
                                             K.head_g.unsqueeze(1).broadcast_to([P, TT, 256]), ALU.mult))
                for t in range(TT):
                    both = heads(o[:, t, 256:768])
                    link(nc.vector.tensor_tensor(both, both, root[:, t, :].unsqueeze(2).broadcast_to([P, 8, HD]), ALU.mult))
                    h = heads(o[:, t, 256:512])
                    link(nc.vector.tensor_tensor(h, h, K.sub_g.unsqueeze(1).broadcast_to([P, 4, HD]), ALU.mult))
                    ins = nc.vector.tensor_tensor(o[:, t, 512:768], o[:, t, 512:768], ztok[:, t, 768:1024], ALU.mult)
                    if t == 0:
                        link(ins)
                ins.then_inc(o_ready, 1)
                for m in range(4):
                    n, t = m // 2, m % 2
                    half = slice(512 * n, 512 * n + 512)
                    dve.wait_ge(made, m + 1)
                    nc.vector.tensor_tensor(K.x[:, t, half], K.x[:, t, half], K.ps[:, 4 + 2 * t + n, :], ALU.add)
    A.high = top


def feed_forward(nc, K, layer):
    A, W = K.A, K.W
    A.low = K.base
    top = A.high
    last_layer = layer == 1
    gain, h, hT = A.temp(D), A.temp(TT, D), A.temp(KT, T)
    gate = A.temp(4, T)
    hidT = A.temp(NFT, T)
    sums, ms, root = A.temp(4), A.temp(4), A.temp(4)
    final_gain = A.temp(D)
    with nc.cleanup_on_exit():
        landed, squared, ms_ready, rooted, h_ready = (K.sem(n) for n in (
            "gain_landed", "squared", "ms_ready", "rooted", "h_ready"))
        t_made, t_kept, made, gated, hid_ready, y_made, dve_step = (K.sem(n) for n in (
            "t_made", "t_kept", "made", "gated", "hid_ready", "y_made", "dve_step"))
        x_ready, out_ready = K.sem("x_ready"), K.sem("out_ready")
        with nc.Block() as block:
            @block.sync
            def _(sp):
                sp.dma_start(gain, K.dram["norm_ffn_2"][layer].partition_broadcast(P)).then_inc(landed, 16)
                sp.dma_start(final_gain, K.dram["norm_final_2"].partition_broadcast(P)).then_inc(landed, 16)
                W.load_ahead(sp, 3 * FCH)
                sp.wait_ge(landed, 32)
                if last_layer:
                    sp.wait_ge(out_ready, 2)
                    sp.dma_start(K.out.rearrange("(t p) d -> p t d", p=P), h).then_inc(K.out_stored, 16)
                    sp.wait_ge(K.out_stored, 16)

            @block.tensor
            def _(pe):
                for n in range(4):
                    t, q = n // 2, n % 2
                    pe.wait_ge(h_ready, t + 1)
                    for k in range(4):
                        c = P * (4 * q + k)
                        last = nc.tensor.transpose(K.ps[:, n, P * k:P * k + P], h[:, t, c:c + P], K.ident)
                    last.then_inc(t_made, 1)
                pe.wait_ge(t_kept, 4)
                for f in range(NFT):
                    if f % 4 == 0:
                        wg, wu = W.take(pe), W.take(pe)
                    if f >= 4:
                        pe.wait_ge(hid_ready, f - 3)
                    at = P * (f % 4)
                    for i, w in enumerate((wg, wu)):
                        for k in range(KT):
                            last = nc.tensor.matmul(K.ps[:, f % 4, T * i:T * i + T], w[:, k, at:at + P], hT[:, k, :],
                                                    start=(k == 0), stop=(k == KT - 1))
                            if f and f % 4 == 0 and i == 0 and k == 0:
                                last.then_inc(W.used, 2)
                    last.then_inc(made, 1)
                for f in range(NFT):
                    if f % 4 == 0:
                        wd = W.take(pe).rearrange("p k n -> p (k n)").rearrange("p (f d) -> p f d", d=D)
                    pe.wait_ge(hid_ready, f + 1)
                    for t in range(TT):
                        for n in range(2):
                            last = nc.tensor.matmul(K.ps[:, 4 + 2 * t + n, :], hidT[:, f, P * t:P * t + P],
                                                    wd[:, f % 4, 512 * n:512 * n + 512],
                                                    start=(f == 0), stop=(f == NFT - 1))
                            if f % 4 == 0 and t == 0 and n == 0:
                                last.then_inc(W.used, 1 if f else 2)
                last.then_inc(y_made, 1)
                pe.wait_ge(y_made, 1)
                nc.tensor.nop().then_inc(W.used, 1)

            @block.scalar
            def _(act):
                for t in range(TT):
                    nc.scalar.activation(h[:, t, :], K.x[:, t, :], ACT.Square, accum_out=sums[:, t:t + 1]).then_inc(squared, 1)
                act.wait_ge(ms_ready, 1)
                nc.scalar.activation(root[:, 0:2], ms[:, 0:2], ACT.Sqrt).then_inc(rooted, 1)
                for n in range(4):
                    t, q = n // 2, n % 2
                    act.wait_ge(t_made, n + 1)
                    nc.scalar.activation(hT[:, 4 * q:4 * q + 4, P * t:P * t + P],
                                         K.ps[:, n, :].rearrange("p (k t) -> p k t", t=P), ACT.Copy).then_inc(t_kept, 1)
                for f in range(NFT):
                    act.wait_ge(made, f + 1)
                    if f >= 4:
                        act.wait_ge(hid_ready, f - 3)
                    nc.scalar.activation(gate[:, f % 4, :], K.ps[:, f % 4, 0:T], ACT.Silu).then_inc(gated, 1)
                if last_layer:
                    for t in range(TT):
                        act.wait_ge(x_ready, 2 * t + 2)
                        nc.scalar.activation(h[:, t, :], K.x[:, t, :], ACT.Square, accum_out=sums[:, 2 + t:3 + t]).then_inc(squared, 1)
                    act.wait_ge(ms_ready, 2)
                    nc.scalar.activation(root[:, 2:4], ms[:, 2:4], ACT.Sqrt).then_inc(rooted, 1)

            @block.vector
            def _(dve):
                link = chain(dve, dve_step)
                dve.wait_ge(squared, 2)
                nc.vector.tensor_scalar(ms[:, 0:2], sums[:, 0:2], 1.0 / D, EPS, ALU.mult, ALU.add).then_inc(ms_ready, 1)
                dve.wait_ge(rooted, 1)
                link(nc.vector.reciprocal(root[:, 0:2], root[:, 0:2]))
                dve.wait_ge(landed, 32)
                for t in range(TT):
                    nc.vector.scalar_tensor_tensor(h[:, t, :], K.x[:, t, :], root[:, t:t + 1], gain,
                                                   ALU.mult, ALU.mult).then_inc(h_ready, 1)
                for f in range(NFT):
                    dve.wait_ge(gated, f + 1)
                    nc.vector.tensor_tensor(hidT[:, f, :], gate[:, f % 4, :], K.ps[:, f % 4, T:2 * T],
                                            ALU.mult).then_inc(hid_ready, 1)
                dve.wait_ge(y_made, 1)
                for t in range(TT):
                    for n in range(2):
                        half = slice(512 * n, 512 * n + 512)
                        nc.vector.tensor_tensor(K.x[:, t, half], K.x[:, t, half], K.ps[:, 4 + 2 * t + n, :],
                                                ALU.add).then_inc(x_ready, 1)
                if last_layer:
                    dve.wait_ge(squared, 4)
                    nc.vector.tensor_scalar(ms[:, 2:4], sums[:, 2:4], 1.0 / D, EPS, ALU.mult, ALU.add).then_inc(ms_ready, 1)
                    dve.wait_ge(rooted, 2)
                    link(nc.vector.reciprocal(root[:, 2:4], root[:, 2:4]))
                    for t in range(TT):
                        nc.vector.scalar_tensor_tensor(h[:, t, :], K.x[:, t, :], root[:, 2 + t:3 + t], final_gain,
                                                       ALU.mult, ALU.mult).then_inc(out_ready, 1)
    A.high = top


def layer_stages():
    return [(stage, layer) for layer in range(2)
            for stage in (attention_inputs, mixer_preparation, attention, attention_out, feed_forward)]


def first_and_second_block(nc, dram, out):
    K = Kept()
    K.nc, K.dram, K.out = nc, dram, out
    K.A = Arena(nc, 127 * 256)
    K.W = WeightStream(nc, dram)
    K.out_stored = nc.alloc_semaphore("out_stored")
    K.ps = nc.alloc_psum_tensor("psum", [P, 8, 512], F32)
    A = K.A
    K.ident = A.keep(P)
    K.ones = A.keep(P)
    K.head_ones = A.keep(P)
    K.sel = A.keep(2)
    K.mixT = A.keep(KT, T)
    K.glT = A.keep(2, T)
    K.after_mixT = A.low
    K.rT = A.temp(4, T)
    K.rkT = A.temp(4, 2 * T)
    K.rvT = A.temp(4, 2 * T)
    K.wlT = A.temp(2 * T)
    K.alT = A.temp(2 * T)
    K.hT = A.temp(KT, 2 * T)
    for n, stage in enumerate(STAGES):
        K.stage = n + 1
        if isinstance(stage, tuple):
            stage[0](nc, K, stage[1])
        else:
            stage(nc, K)


class Kept:

    stage = 0

    def sem(self, name):
        return self.nc.alloc_semaphore(f"stage{self.stage}_{name}")


STAGES = [modulate_and_norm, project_in, retention, rwkv_constants, rwkv_context, rwkv_latent, rwkv_output, mixers_out, route, experts] + layer_stages()


def slots(w, width=512):
    k, n = w.shape
    pad = -n % width
    if pad:
        w = np.concatenate([w, np.zeros((k, pad), w.dtype)], 1)
    m = (n + pad) // width
    return np.ascontiguousarray(w.reshape(k // P, P, m, width).transpose(2, 1, 0, 3)).reshape(m, P, -1)


def layout(i):
    a = {}
    f = {k: np.asarray(v) for k, v in i.items()}
    a["x"], a["ctx"] = f["x"][0], f["ctx"][0]
    a["cT"] = np.concatenate([f["c_ctx"].reshape(KT, P).T, f["c"][0].reshape(KT, P).T], 1)
    a["ident"] = np.eye(P, dtype=np.float32)
    a["b_mod"] = f["b_mod"]
    a["norm_gains"] = f["norm_gains"][0]
    a["w_mod"] = slots(f["w_mod"][0])
    wi = f["w_in"][0]
    at = np.cumsum([0, 512, 512, 512, 64, 64, 64, 128, 128])
    piece = lambda w, n: w[..., at[n]:at[n + 1]]
    rw = wi[:, 2560:]
    doubled = lambda w: np.concatenate([piece(w, n) for n in (0, 1, 2, 3, 4, 5, 5, 6, 7)], -1)
    a["w_in"] = slots(np.concatenate([wi[:, :2560], doubled(rw)], 1))
    a["rwkv_conv"] = doubled(f["rwkv_conv"][0]).reshape(3, 16, P).transpose(2, 1, 0)
    by_channel = lambda v: v.reshape(4, P).T
    a["rwkv_w0"] = f["rwkv_w0"][0].reshape(2, H, HD).transpose(0, 2, 1).reshape(P, H)
    a["rwkv_w2"] = f["rwkv_w2"][0].reshape(P, 512)
    a["rwkv_a2"] = f["rwkv_a2"][0]
    a["rwkv_g2"] = f["rwkv_g2"][0].transpose(1, 0, 2)
    a["rwkv_vecs"] = np.stack([by_channel(f[n][0]) for n in
                               ("rwkv_a0", "rwkv_k_k", "rwkv_k_a")], 1)
    by_head = lambda v: np.concatenate([v.reshape(H, HD).T] * 2, 0)
    a["rwkv_dup_vecs"] = np.stack([by_head(f[n][0]) for n in ("rwkv_r_k", "rwkv_lnx_w", "rwkv_lnx_b")], 1)
    a["w_out"] = slots(f["w_out"][0])
    wg, wu, wd = (f[n][0] for n in ("w_gate", "w_up", "w_down"))
    a["w_moe"] = np.concatenate([np.stack([slots(w[e]) for e in range(NE)]) for w in (wg, wu, wd)], 1).reshape(6 * NE, P, -1)
    a["w_router"] = f["w_router"][0].reshape(KT, P, NE).transpose(1, 0, 2)
    second = [second_layout(f, layer) for layer in range(2)]
    for name in second[0]:
        a[name] = np.stack([s[name] for s in second])
    for name in ("w_in_2", "w_out_2", "w_gate_2", "w_up_2", "w_down_2"):
        a[name] = a[name].reshape(-1, P, SLOT)
    a["norm_mix_2"], a["norm_ffn_2"], a["norm_final_2"] = f["norm_mix_2"], f["norm_ffn_2"], f["norm_final_2"]
    a.update(tables())
    return a


def second_layout(f, layer):
    w = f["w_in_2"][layer]
    names = ["aq", "kc", "vc", "ks", "vs", "kw", "vw", "ag", "bq", "bk", "bv", "cu", "cv", "ci", "cf", "co", "dq", "dk", "dv"]
    sizes = [256, 64, 64, 64, 64, 64, 64, 12, 256, 256, 256, 256, 256, 4, 4, 256, 256, 256, 256]
    at = np.cumsum([0] + sizes)
    col = {n: w[:, at[i]:at[i + 1]] for i, n in enumerate(names)}
    pad = np.zeros((D, 108), w.dtype)
    order = ["aq", "kc", "kc", "vc", "vc", "ks", "ks", "kw", "kw", "bq", "bk", "cu", "dq", "dk"]
    by_token = [col[n] for n in ("vs", "vw", "ag", "ci", "cf")] + [pad] + [col[n] for n in ("bv", "cv", "co", "dv")]
    twice = lambda v: np.concatenate([v, v], 0)
    cmp_w = f["nsa_cmp_w_2"][layer].reshape(2, 32, HD, HD).transpose(2, 0, 1, 3)
    conv = np.concatenate([f["mlstm_conv_w_2"][layer], f["mlstm_conv_b_2"][layer][None]], 0)
    wqk = np.stack([f["mlstm_wq_2"][layer], f["mlstm_wk_2"][layer]]).reshape(2, 2, 2, HD, HD)
    down = np.concatenate([f["w_down_2"][layer], np.zeros((2 * P, D), w.dtype)]).reshape(FCH, 4, P, D)
    return {
        "w_in_2": slots(np.concatenate([col[n] for n in order] + by_token, 1)),
        "w_out_2": slots(f["w_out_2"][layer]),
        "w_gate_2": slots(f["w_gate_2"][layer]),
        "w_up_2": slots(f["w_up_2"][layer]),
        "w_down_2": down.transpose(0, 2, 1, 3),
        "nsa_cmp_w_2": twice(cmp_w),
        "nsa_cmp_pos_2": twice(f["nsa_cmp_pos_2"][layer].transpose(2, 0, 1)),
        "mlstm_conv_2": conv.reshape(5, 2, P).transpose(2, 1, 0),
        "mlstm_wqk_2": wqk.transpose(2, 3, 0, 1, 4).reshape(P, 2, 2, HD),
        "mlstm_gate_b_2": f["mlstm_gate_b_2"][layer].reshape(8),
        "diff_lambda_2": f["diff_lambda_2"][layer].reshape(P),
        "diff_norm_2": f["diff_norm_2"][layer],
        "mlstm_norm_2": f["mlstm_norm_2"][layer],
    }


def tables():
    t = {}
    n = np.arange(T, dtype=np.float32)
    freq = 10000.0 ** (-np.arange(16, dtype=np.float32) / 16)
    ang = np.concatenate([np.floor(n / 64)[:, None] * freq, (n % 64)[:, None] * freq], 1)
    lane = np.arange(P)
    sign = np.where(lane % 64 < 32, -1.0, 1.0)[:, None]
    t["rope_cos"] = np.cos(ang).T[lane % 32]
    t["rope_sin"] = np.sin(ang).T[lane % 32] * sign
    t["swap64"] = (lane[:, None] == (lane ^ 32)[None, :])
    log_gamma = np.log1p(-np.exp2(-5.0 - np.arange(H)))
    s, q = np.arange(P)[:, None, None], np.arange(T)[None, None, :]
    g = log_gamma[None, :, None]
    power = lambda e: np.where(e >= 0, np.exp(np.maximum(e, 0) * g), 0.0)
    t["ret_decay_f"] = power(q - s)
    t["ret_decay_b"] = power(P + s - q)
    head = 2 * np.arange(4)[None, :, None] + (lane >= 64)[:, None, None]
    lg = log_gamma[head]
    t["ret_q_decay"] = np.stack([np.exp((q + 1) * lg), np.exp((T - q) * lg)], 1)
    j = np.arange(TT)[None, :, None] * P + lane[:, None, None]
    lg = log_gamma[None, None, :]
    t["ret_k_decay"] = np.stack([np.exp((T - 1 - j) * lg), np.exp(j * lg)], 1)
    i, j = np.arange(C)[:, None], np.arange(C)[None, :]
    joins = lambda m, r, c: (r // (2 * m) == c // (2 * m)) & (r // m % 2 == 1) & (c // m % 2 == 0)
    fwd = [joins(2 ** n, i, j) for n in range(1, 6)] + [joins(1, j, i), j > i, j >= i]
    bwd = [joins(2 ** n, j, i) for n in range(1, 6)] + [joins(1, i, j), j < i, j <= i]
    t["rwkv_masks"] = np.concatenate([np.stack(fwd, 1), np.stack(bwd, 1)], 0)
    for dim in (64, 32):
        inv = 1.0 / (10000.0 ** (np.arange(0, dim, 2, dtype=np.float32) / dim))
        ang = (n[:, None] * inv[None, :]).T[lane % (dim // 2)]
        t[f"cos{dim}"] = np.cos(ang)
        t[f"sin{dim}"] = np.sin(ang) * np.where(lane % dim < dim // 2, -1.0, 1.0)[:, None]
    t["swap32"] = (lane[:, None] == (lane ^ 16)[None, :])
    t["tri"] = lane[:, None] <= lane[None, :]
    back = (np.arange(TT)[None, :, None] * P + lane[:, None, None]) - np.arange(T)[None, None, :]
    times = sum(((back >= 0) & (back <= window) & (back % step == 0)).astype(int)
                for window, step in ((128, 1), (512, 4), (2048, 16)))
    t["attn_bias"] = np.stack([np.where(back >= 0, 0.0, NEG), np.where(times > 0, np.log(np.maximum(times, 1)), NEG)], 1)
    seen = (np.arange(16) * 16 + 31)[None, None, :] <= np.arange(TT)[None, :, None] * P + lane[:, None, None]
    seen[:, :, 15] = False
    t["cmp_bias"], t["cmp_on"] = np.where(seen, 0.0, NEG), seen
    t["earlier"] = np.arange(T)[None, None, :] < (np.arange(TT)[None, :, None] * P + lane[:, None, None])
    t["places"] = np.tile(np.arange(CAP), (P, 1))
    return {k: np.ascontiguousarray(v, dtype=np.float32) for k, v in t.items()}


def kernel(**inputs):
    import concourse.bacc as bacc
    from concourse.bass_utils import run_bass_kernel_spmd

    nc = bacc.Bacc("TRN2", target_bir_lowering=False, num_devices=1)
    arrays, dram = {}, {}
    for name, a in layout(inputs).items():
        a = np.ascontiguousarray(a)
        arrays[f"in_{name}"] = a
        dram[name] = nc.dram_tensor(f"in_{name}", a.shape, mybir.dt.from_np(a.dtype), kind="ExternalInput").ap()
    out = nc.dram_tensor("out_0", (T, D), F32, kind="ExternalOutput").ap()
    first_and_second_block(nc, dram, out)
    r = run_bass_kernel_spmd(nc, [arrays], core_ids=[0])
    return r.results[0]["out_0"].reshape(1, T, D)
```
